# Optimizing a Trainium2 kernel written in Bass

```python
import math
import functools
import jax
import jax.numpy as jnp
from jax import lax
import numpy as np

D_MODEL = 1024
BATCH = 1
SEQ = 256
DEPTH = 2

GRID_W = 64
CTX_LEN = 256
EPS = 1e-6
HEAD_DIM = 64
GROUP_WIDTH = D_MODEL // 2
MIX_WIDTH = 2 * GROUP_WIDTH

HY_CH = GROUP_WIDTH
HY_BANDS = 16
HY_EMB = 2 * HY_BANDS + 1
HY_FILT_HID = 64
HY_FAST_DECAY = 0.3
HY_SLOW_DECAY = 1.5
HY_DECAY_TARGET = 1e-2
SHORT_CONV = 3

SSM_INNER = GROUP_WIDTH
SSM_HEADDIM = 64
SSM_HEADS = SSM_INNER // SSM_HEADDIM
SSM_GROUPS = 2
SSM_STATE = 128
SSM_CHUNK = 128
SSM_CONV_CH = SSM_INNER + 2 * SSM_GROUPS * SSM_STATE
EVEN_IN = 3 * HY_CH + SSM_INNER + SSM_CONV_CH + 2 * SSM_HEADS

MLA_HEADS = GROUP_WIDTH // HEAD_DIM
MLA_NOPE = 64
MLA_ROPE = 32
MLA_V = 64
MLA_Q_LORA = D_MODEL // 4
MLA_KV_LORA = D_MODEL // 8

GQA_HEADS = GROUP_WIDTH // HEAD_DIM
GQA_KV = GQA_HEADS // 4
WINDOW = 128
ODD_IN = MLA_Q_LORA + MLA_KV_LORA + MLA_ROPE + (GQA_HEADS + 2 * GQA_KV) * HEAD_DIM

ROPE_BASE = 10000.0
ATTN_BLOCK = 128

D_FF = ((8 * D_MODEL // 3 + 127) // 128) * 128
N_EXPERTS = 8
TOP_K = 2
D_FF_EXPERT = 7 * D_MODEL // 2

N_EVEN = (DEPTH + 1) // 2
N_ODD = DEPTH // 2

kernel_name = 'hybrid_flow_prefix_block'

def rmsnorm(x, g):
    xf = x.astype(jnp.float32)
    y = xf * lax.rsqrt(jnp.mean(xf * xf, axis=-1, keepdims=True) + EPS)
    return (y * g.astype(jnp.float32)).astype(x.dtype)

def ada_params(cond, w, b):
    m = jax.nn.silu(cond) @ w + b
    return [t[:, None, :] for t in jnp.split(m, 6, axis=-1)]

def modulate(h, shift, scale):
    return h * (1 + scale) + shift

def split_last(x, sizes):
    out, start = [], 0
    for s in sizes:
        out.append(x[..., start:start + s])
        start += s
    return out

def flip_seq(t):
    return jnp.flip(t, axis=1)

def dwconv_centred(x, w, b):
    k_w, ch = w.shape
    pad = k_w // 2
    y = lax.conv_general_dilated(x, w[:, None, :].astype(x.dtype), window_strides=(1,), padding=[(pad, pad)],
                                 dimension_numbers=('NWC', 'WIO', 'NWC'), feature_group_count=ch)
    return y + b

def hyena_filters(n, w1, b1, w2, b2, w3, freq):
    pos = jnp.arange(n, dtype=jnp.float32)
    t = pos / (n - 1)
    omega = 2.0 * math.pi * pos / n
    bands = jnp.linspace(1e-4, HY_BANDS - 1, HY_BANDS, dtype=jnp.float32)
    z = jnp.concatenate([t[:, None], jnp.cos(omega[:, None] * bands), -jnp.sin(omega[:, None] * bands)], axis=-1)
    f = freq.astype(jnp.float32)
    h = jnp.sin(f * (z @ w1.astype(jnp.float32) + b1.astype(jnp.float32)))
    h = jnp.sin(f * (h @ w2.astype(jnp.float32) + b2.astype(jnp.float32)))
    h = (h @ w3.astype(jnp.float32)).reshape(n, 2, HY_CH)
    deltas = jnp.abs(jnp.linspace(math.log(HY_DECAY_TARGET) / HY_SLOW_DECAY, math.log(HY_DECAY_TARGET) / HY_FAST_DECAY,
                                  HY_CH, dtype=jnp.float32))
    decay = jnp.exp(-t[:, None] * deltas[None, :])
    return h[:, 0] * decay, h[:, 1] * decay

def long_conv_bidir(u, h_fwd, h_bwd, bias):
    n, ch = h_fwd.shape
    filt = jnp.concatenate([h_fwd, jnp.zeros((1, ch), jnp.float32), h_bwd[1:][::-1]], axis=0)
    uf = jnp.fft.rfft(u, n=2 * n, axis=1)
    ff = jnp.fft.rfft(filt, n=2 * n, axis=0)
    y = jnp.fft.irfft(uf * ff[None], n=2 * n, axis=1)[:, :n]
    return y + u * bias

def hyena_mixer(proj, conv_w, conv_b, w1, b1, w2, b2, w3, freq, bias):
    n = proj.shape[1]
    x0, x1, v = jnp.split(dwconv_centred(proj, conv_w, conv_b).astype(jnp.float32), 3, axis=-1)
    h_fwd, h_bwd = hyena_filters(n, w1, b1, w2, b2, w3, freq)
    y = x0 * long_conv_bidir(x1 * v, h_fwd, h_bwd, bias.astype(jnp.float32))
    return y.astype(proj.dtype)

def segsum(a):
    t_len = a.shape[-1]
    cs = jnp.cumsum(a, axis=-1)
    seg = cs[..., :, None] - cs[..., None, :]
    mask = jnp.tril(jnp.ones((t_len, t_len), dtype=bool))
    return jnp.where(mask, seg, -jnp.inf)

def ssd_scan(x, dt, a_head, b_in, c_in, init_state):
    bsz, n, nh, hp = x.shape
    ns = b_in.shape[-1]
    nc = n // SSM_CHUNK
    xd = (x * dt[..., None]).reshape(bsz, nc, SSM_CHUNK, nh, hp)
    a = (dt * a_head).reshape(bsz, nc, SSM_CHUNK, nh).transpose(0, 3, 1, 2)
    bc = b_in.reshape(bsz, nc, SSM_CHUNK, nh, ns)
    cc = c_in.reshape(bsz, nc, SSM_CHUNK, nh, ns)
    a_cs = jnp.cumsum(a, axis=-1)
    lmat = jnp.exp(segsum(a))
    scores = jnp.einsum('bcqhn,bcshn->bhcqs', cc, bc) * lmat
    y_diag = jnp.einsum('bhcqs,bcshp->bcqhp', scores, xd)
    decay_states = jnp.exp(a_cs[..., -1:] - a_cs).transpose(0, 2, 3, 1)
    states = jnp.einsum('bcqhn,bcqhp->bchpn', bc * decay_states[..., None], xd)
    states = jnp.concatenate([init_state[:, None], states], axis=1)
    chunk_a = jnp.pad(a_cs[..., -1], ((0, 0), (0, 0), (1, 0)))
    decay_chunk = jnp.exp(segsum(chunk_a))
    new_states = jnp.einsum('bhzc,bchpn->bzhpn', decay_chunk, states)
    states_in, final_state = new_states[:, :-1], new_states[:, -1]
    out_decay = jnp.exp(a_cs).transpose(0, 2, 3, 1)
    y_off = jnp.einsum('bcqhn,bchpn->bcqhp', cc * out_decay[..., None], states_in)
    return (y_diag + y_off).reshape(bsz, n, nh, hp), final_state

def ssd_mixer(proj, init_f, init_b, conv_w, conv_b, dt_bias, a_log, d_skip, norm_g):
    bsz, n, _ = proj.shape
    f32 = jnp.float32
    z, xbc, dt_raw = split_last(proj, [SSM_INNER, SSM_CONV_CH, 2 * SSM_HEADS])
    xbc = jax.nn.silu(dwconv_centred(xbc, conv_w, conv_b)).astype(f32)
    xs, b_in, c_in = split_last(xbc, [SSM_INNER, SSM_GROUPS * SSM_STATE, SSM_GROUPS * SSM_STATE])
    xs = xs.reshape(bsz, n, SSM_HEADS, SSM_HEADDIM)
    rep = SSM_HEADS // SSM_GROUPS
    b_in = jnp.repeat(b_in.reshape(bsz, n, SSM_GROUPS, SSM_STATE), rep, axis=2)
    c_in = jnp.repeat(c_in.reshape(bsz, n, SSM_GROUPS, SSM_STATE), rep, axis=2)
    dt = jax.nn.softplus(dt_raw.astype(f32).reshape(bsz, n, 2, SSM_HEADS) + dt_bias.astype(f32))
    a = -jnp.exp(a_log.astype(f32))
    y_f, s_f = ssd_scan(xs, dt[:, :, 0], a[0], b_in, c_in, init_f)
    y_b, s_b = ssd_scan(flip_seq(xs), flip_seq(dt[:, :, 1]), a[1], flip_seq(b_in), flip_seq(c_in), init_b)
    y = y_f + flip_seq(y_b) + xs * d_skip.astype(f32)[:, None]
    y = y.reshape(bsz, n, SSM_INNER) * jax.nn.silu(z.astype(f32))
    yg = y.reshape(bsz, n, SSM_GROUPS, SSM_INNER // SSM_GROUPS)
    yg = yg * lax.rsqrt(jnp.mean(yg * yg, axis=-1, keepdims=True) + EPS)
    y = yg.reshape(bsz, n, SSM_INNER) * norm_g.astype(f32)
    return y.astype(proj.dtype), s_f, s_b

def even_mix(h, init_f, init_b, w_in, hy_conv_w, hy_conv_b, f_w1, f_b1, f_w2, f_b2, f_w3, hy_freq, hy_bias,
             ssm_conv_w, ssm_conv_b, dt_bias, a_log, d_skip, ssm_norm_g, w_out):
    proj = h @ w_in
    y_hy = hyena_mixer(proj[..., :3 * HY_CH], hy_conv_w, hy_conv_b, f_w1, f_b1, f_w2, f_b2, f_w3, hy_freq, hy_bias)
    y_ssm, s_f, s_b = ssd_mixer(proj[..., 3 * HY_CH:], init_f, init_b, ssm_conv_w, ssm_conv_b, dt_bias, a_log,
                                d_skip, ssm_norm_g)
    out = jnp.concatenate([y_hy, y_ssm], axis=-1) @ w_out
    return out, s_f, s_b

def axial_rope_tables(n_tokens, rot_dim):
    n_rows = n_tokens // GRID_W
    rows, cols = jnp.meshgrid(jnp.arange(n_rows), jnp.arange(GRID_W), indexing='ij')
    rows = rows.reshape(-1).astype(jnp.float32)
    cols = cols.reshape(-1).astype(jnp.float32)
    nf = rot_dim // 4
    inv = ROPE_BASE ** (-jnp.arange(nf, dtype=jnp.float32) / nf)
    ang = jnp.concatenate([rows[:, None] * inv, cols[:, None] * inv], axis=-1)
    return jnp.cos(ang), jnp.sin(ang)

def apply_rope(x, rope):
    cos, sin = rope
    half = x.shape[-1] // 2
    x1, x2 = x[..., :half], x[..., half:]
    c, s = cos[None, :, None, :], sin[None, :, None, :]
    return jnp.concatenate([x1 * c - x2 * s, x2 * c + x1 * s], axis=-1).astype(x.dtype)

def dense_attention_blocked(q, k, v, scale):
    bsz, n, nh, d = q.shape
    nb = n // ATTN_BLOCK
    qb = q.reshape(bsz, nb, ATTN_BLOCK, nh, d).transpose(1, 0, 2, 3, 4)

    def one_block(qi):
        s = jnp.einsum('bqhd,bkhd->bhqk', qi, k).astype(jnp.float32) * scale
        p = jax.nn.softmax(s, axis=-1).astype(v.dtype)
        return jnp.einsum('bhqk,bkhd->bqhd', p, v)

    o = lax.map(one_block, qb)
    return o.transpose(1, 0, 2, 3, 4).reshape(bsz, n, nh, v.shape[-1])

def window_gqa_sink(q, k, v, k_ctx, v_ctx, sink):
    bsz, n, gh, d = q.shape
    n_kv = k.shape[2]
    g = gh // n_kv
    w = WINDOW
    nb = n // w
    c_len = k_ctx.shape[1]
    scale = d ** -0.5
    qb = q.reshape(bsz, nb, w, n_kv, g, d)

    def band(t):
        tp = jnp.pad(t, ((0, 0), (w, w), (0, 0), (0, 0))).reshape(bsz, nb + 2, w, n_kv, d)
        return jnp.concatenate([tp[:, :-2], tp[:, 1:-1], tp[:, 2:]], axis=2)

    kb, vb = band(k), band(v)
    qpos = jnp.arange(nb)[:, None] * w + jnp.arange(w)[None, :]
    kpos = (jnp.arange(nb)[:, None] - 1) * w + jnp.arange(3 * w)[None, :]
    rel = kpos[:, None, :] - qpos[:, :, None]
    valid = (jnp.abs(rel) <= w) & (kpos[:, None, :] >= 0) & (kpos[:, None, :] < n)
    s_loc = jnp.einsum('bnqkgd,bnrkd->bnkgqr', qb, kb).astype(jnp.float32) * scale
    s_loc = jnp.where(valid[None, :, None, None], s_loc, -jnp.inf)
    s_ctx = jnp.einsum('bnqkgd,bckd->bnkgqc', qb, k_ctx).astype(jnp.float32) * scale
    s_sink = jnp.broadcast_to(sink.astype(jnp.float32).reshape(1, 1, n_kv, g, 1, 1), s_loc.shape[:-1] + (1,))
    p = jax.nn.softmax(jnp.concatenate([s_loc, s_ctx, s_sink], axis=-1), axis=-1).astype(v.dtype)
    o = (jnp.einsum('bnkgqr,bnrkd->bnqkgd', p[..., :3 * w], vb)
         + jnp.einsum('bnkgqc,bckd->bnqkgd', p[..., 3 * w:3 * w + c_len], v_ctx))
    return o.reshape(bsz, n, gh, d)

def ctx_gqa_sink(q, k, v, sink):
    bsz, c_len, gh, d = q.shape
    n_kv = k.shape[2]
    g = gh // n_kv
    qg = q.reshape(bsz, c_len, n_kv, g, d)
    s = jnp.einsum('bqkgd,bckd->bkgqc', qg, k).astype(jnp.float32) * d ** -0.5
    s_sink = jnp.broadcast_to(sink.astype(jnp.float32).reshape(1, n_kv, g, 1, 1), s.shape[:-1] + (1,))
    p = jax.nn.softmax(jnp.concatenate([s, s_sink], axis=-1), axis=-1)[..., :-1].astype(v.dtype)
    return jnp.einsum('bkgqc,bckd->bqkgd', p, v).reshape(bsz, c_len, gh, d)

def odd_project(h, w_in, q_norm_g, w_q_up, kv_norm_g, w_kv_up):
    bsz, n, _ = h.shape
    q_lat, kv_lat, k_rope, q_g, k_g, v_g = split_last(
        h @ w_in, [MLA_Q_LORA, MLA_KV_LORA, MLA_ROPE, GQA_HEADS * HEAD_DIM, GQA_KV * HEAD_DIM, GQA_KV * HEAD_DIM])
    q = (rmsnorm(q_lat, q_norm_g) @ w_q_up).reshape(bsz, n, MLA_HEADS, MLA_NOPE + MLA_ROPE)
    kv = (rmsnorm(kv_lat, kv_norm_g) @ w_kv_up).reshape(bsz, n, MLA_HEADS, MLA_NOPE + MLA_V)
    return (q[..., :MLA_NOPE], q[..., MLA_NOPE:], kv[..., :MLA_NOPE], k_rope[:, :, None, :], kv[..., MLA_NOPE:],
            q_g.reshape(bsz, n, GQA_HEADS, HEAD_DIM), k_g.reshape(bsz, n, GQA_KV, HEAD_DIM),
            v_g.reshape(bsz, n, GQA_KV, HEAD_DIM))

def mla_keys(k_nope, k_rope):
    return jnp.concatenate([k_nope, jnp.broadcast_to(k_rope, k_nope.shape[:-1] + (MLA_ROPE,))], axis=-1)

def odd_mix(a_lat, a_ctx, need_ctx, rope_mla, rope_gqa, w_in, q_norm_g, w_q_up, kv_norm_g, w_kv_up, sink, w_out):
    bsz, n, _ = a_lat.shape
    qn_l, qr_l, kn_l, kr_l, v_l, qg_l, kg_l, vg_l = odd_project(a_lat, w_in, q_norm_g, w_q_up, kv_norm_g, w_kv_up)
    qn_c, qr_c, kn_c, kr_c, v_c, qg_c, kg_c, vg_c = odd_project(a_ctx, w_in, q_norm_g, w_q_up, kv_norm_g, w_kv_up)
    mla_scale = (MLA_NOPE + MLA_ROPE) ** -0.5
    k_c = mla_keys(kn_c, kr_c)
    q_l = jnp.concatenate([qn_l, apply_rope(qr_l, rope_mla)], axis=-1)
    k_l = mla_keys(kn_l, apply_rope(kr_l, rope_mla))
    o_mla = dense_attention_blocked(q_l, jnp.concatenate([k_c, k_l], axis=1), jnp.concatenate([v_c, v_l], axis=1),
                                    mla_scale)
    o_win = window_gqa_sink(apply_rope(qg_l, rope_gqa), apply_rope(kg_l, rope_gqa), vg_l, kg_c, vg_c, sink)
    m_lat = jnp.concatenate([o_mla.reshape(bsz, n, -1), o_win.reshape(bsz, n, -1)], axis=-1) @ w_out
    if not need_ctx:
        return m_lat, None
    c_len = a_ctx.shape[1]
    o_mla_c = dense_attention_blocked(jnp.concatenate([qn_c, qr_c], axis=-1), k_c, v_c, mla_scale)
    o_win_c = ctx_gqa_sink(qg_c, kg_c, vg_c, sink)
    m_ctx = jnp.concatenate([o_mla_c.reshape(bsz, c_len, -1), o_win_c.reshape(bsz, c_len, -1)], axis=-1) @ w_out
    return m_lat, m_ctx

def swiglu(h, w_gate, w_up, w_down):
    return (jax.nn.silu(h @ w_gate) * (h @ w_up)) @ w_down

def moe_swiglu(h, router, w_gate, w_up, w_down):
    bsz, n, d = h.shape
    t = h.reshape(-1, d)
    logits = (t @ router).astype(jnp.float32)
    vals, idx = lax.top_k(logits, TOP_K)
    wts = jax.nn.softmax(vals, axis=-1)
    gates = jnp.sum(jax.nn.one_hot(idx, N_EXPERTS, dtype=jnp.float32) * wts[..., None], axis=1).astype(t.dtype)
    out = jnp.zeros_like(t)
    for e in range(N_EXPERTS):
        out = out + gates[:, e:e + 1] * swiglu(t, w_gate[e], w_up[e], w_down[e])
    return out.reshape(bsz, n, d)

def setup_inputs(seed: int = 0) -> dict:
    key = jax.random.key(seed)
    keys = iter(jax.random.split(key, 64))
    f32 = jnp.float32
    d = D_MODEL

    def nrm(shape, scale):
        return scale * jax.random.normal(next(keys), shape, f32)

    def gain(shape):
        return 1.0 + 0.05 * jax.random.normal(next(keys), shape, f32)

    dt0 = jnp.exp(jax.random.uniform(next(keys), (N_EVEN, 2, SSM_HEADS), f32, math.log(1e-3), math.log(1e-1)))
    a0 = jax.random.uniform(next(keys), (N_EVEN, 2, SSM_HEADS), f32, 1.0, 16.0)
    return {
        'x': nrm((BATCH, SEQ, d), 1.0),
        'c': nrm((BATCH, d), 1.0),
        'ctx': nrm((BATCH, CTX_LEN, d), 1.0),
        'c_ctx': nrm((d,), 1.0),
        'ada_w': nrm((DEPTH, d, 6 * d), d ** -0.5),
        'ada_b': nrm((DEPTH, 6 * d), 0.02),
        'mix_pre_g': gain((DEPTH, d)),
        'mix_post_g': gain((DEPTH, d)),
        'ffn_pre_g': gain((DEPTH, d)),
        'ffn_post_g': gain((DEPTH, d)),
        'ev_w_in': nrm((N_EVEN, d, EVEN_IN), d ** -0.5),
        'ev_hy_conv_w': nrm((N_EVEN, SHORT_CONV, 3 * HY_CH), SHORT_CONV ** -0.5),
        'ev_hy_conv_b': nrm((N_EVEN, 3 * HY_CH), 0.02),
        'ev_hy_filt_w1': nrm((N_EVEN, HY_EMB, HY_FILT_HID), HY_EMB ** -0.5),
        'ev_hy_filt_b1': nrm((N_EVEN, HY_FILT_HID), 0.1),
        'ev_hy_filt_w2': nrm((N_EVEN, HY_FILT_HID, HY_FILT_HID), HY_FILT_HID ** -0.5),
        'ev_hy_filt_b2': nrm((N_EVEN, HY_FILT_HID), 0.1),
        'ev_hy_filt_w3': nrm((N_EVEN, HY_FILT_HID, 2 * HY_CH), 0.1 * HY_FILT_HID ** -0.5),
        'ev_hy_freq': gain((N_EVEN, HY_FILT_HID)),
        'ev_hy_bias': nrm((N_EVEN, HY_CH), 0.5),
        'ev_ssm_conv_w': nrm((N_EVEN, SHORT_CONV, SSM_CONV_CH), SHORT_CONV ** -0.5),
        'ev_ssm_conv_b': nrm((N_EVEN, SSM_CONV_CH), 0.02),
        'ev_ssm_dt_bias': dt0 + jnp.log(-jnp.expm1(-dt0)),
        'ev_ssm_a_log': jnp.log(a0),
        'ev_ssm_d': gain((N_EVEN, SSM_HEADS)),
        'ev_ssm_norm_g': gain((N_EVEN, SSM_INNER)),
        'ev_w_out': nrm((N_EVEN, MIX_WIDTH, d), MIX_WIDTH ** -0.5),
        'ev_ffn_w_gate': nrm((N_EVEN, d, D_FF), d ** -0.5),
        'ev_ffn_w_up': nrm((N_EVEN, d, D_FF), d ** -0.5),
        'ev_ffn_w_down': nrm((N_EVEN, D_FF, d), D_FF ** -0.5),
        'od_w_in': nrm((N_ODD, d, ODD_IN), d ** -0.5),
        'od_mla_q_norm_g': gain((N_ODD, MLA_Q_LORA)),
        'od_mla_w_q_up': nrm((N_ODD, MLA_Q_LORA, MLA_HEADS * (MLA_NOPE + MLA_ROPE)), MLA_Q_LORA ** -0.5),
        'od_mla_kv_norm_g': gain((N_ODD, MLA_KV_LORA)),
        'od_mla_w_kv_up': nrm((N_ODD, MLA_KV_LORA, MLA_HEADS * (MLA_NOPE + MLA_V)), MLA_KV_LORA ** -0.5),
        'od_gqa_sink': nrm((N_ODD, GQA_HEADS), 0.5),
        'od_w_out': nrm((N_ODD, MIX_WIDTH, d), MIX_WIDTH ** -0.5),
        'od_router': nrm((N_ODD, d, N_EXPERTS), d ** -0.5),
        'od_moe_w_gate': nrm((N_ODD, N_EXPERTS, d, D_FF_EXPERT), d ** -0.5),
        'od_moe_w_up': nrm((N_ODD, N_EXPERTS, d, D_FF_EXPERT), d ** -0.5),
        'od_moe_w_down': nrm((N_ODD, N_EXPERTS, D_FF_EXPERT, d), D_FF_EXPERT ** -0.5),
    }

def reference(x, c, ctx, c_ctx, ada_w, ada_b, mix_pre_g, mix_post_g, ffn_pre_g, ffn_post_g,
              ev_w_in, ev_hy_conv_w, ev_hy_conv_b, ev_hy_filt_w1, ev_hy_filt_b1, ev_hy_filt_w2, ev_hy_filt_b2,
              ev_hy_filt_w3, ev_hy_freq, ev_hy_bias, ev_ssm_conv_w, ev_ssm_conv_b, ev_ssm_dt_bias, ev_ssm_a_log,
              ev_ssm_d, ev_ssm_norm_g, ev_w_out, ev_ffn_w_gate, ev_ffn_w_up, ev_ffn_w_down,
              od_w_in, od_mla_q_norm_g, od_mla_w_q_up, od_mla_kv_norm_g, od_mla_w_kv_up, od_gqa_sink, od_w_out,
              od_router, od_moe_w_gate, od_moe_w_up, od_moe_w_down):
    bsz, n, _ = x.shape
    rope_mla = axial_rope_tables(n, MLA_ROPE)
    rope_gqa = axial_rope_tables(n, HEAD_DIM)
    h_lat, h_ctx = x, ctx
    for i in range(DEPTH):
        j = i // 2
        last = i == DEPTH - 1
        sh1, sc1, g1, sh2, sc2, g2 = ada_params(c, ada_w[i], ada_b[i])
        csh1, csc1, cg1, csh2, csc2, cg2 = ada_params(c_ctx[None, :], ada_w[i], ada_b[i])
        a_lat = modulate(rmsnorm(h_lat, mix_pre_g[i]), sh1, sc1)
        a_ctx = modulate(rmsnorm(h_ctx, mix_pre_g[i]), csh1, csc1)
        if i % 2 == 0:
            ev = (ev_w_in[j], ev_hy_conv_w[j], ev_hy_conv_b[j], ev_hy_filt_w1[j], ev_hy_filt_b1[j], ev_hy_filt_w2[j],
                  ev_hy_filt_b2[j], ev_hy_filt_w3[j], ev_hy_freq[j], ev_hy_bias[j], ev_ssm_conv_w[j], ev_ssm_conv_b[j],
                  ev_ssm_dt_bias[j], ev_ssm_a_log[j], ev_ssm_d[j], ev_ssm_norm_g[j], ev_w_out[j])
            zero_state = jnp.zeros((bsz, SSM_HEADS, SSM_HEADDIM, SSM_STATE), jnp.float32)
            m_ctx, s_f, s_b = even_mix(a_ctx, zero_state, zero_state, *ev)
            m_lat, _, _ = even_mix(a_lat, s_f, s_b, *ev)
            ffn = functools.partial(swiglu, w_gate=ev_ffn_w_gate[j], w_up=ev_ffn_w_up[j], w_down=ev_ffn_w_down[j])
        else:
            m_lat, m_ctx = odd_mix(a_lat, a_ctx, not last, rope_mla, rope_gqa, od_w_in[j], od_mla_q_norm_g[j],
                                   od_mla_w_q_up[j], od_mla_kv_norm_g[j], od_mla_w_kv_up[j], od_gqa_sink[j],
                                   od_w_out[j])
            ffn = functools.partial(moe_swiglu, router=od_router[j], w_gate=od_moe_w_gate[j],
                                    w_up=od_moe_w_up[j], w_down=od_moe_w_down[j])
        h_lat = h_lat + g1 * rmsnorm(m_lat, mix_post_g[i])
        f_lat = ffn(modulate(rmsnorm(h_lat, ffn_pre_g[i]), sh2, sc2))
        h_lat = h_lat + g2 * rmsnorm(f_lat, ffn_post_g[i])
        if not last:
            h_ctx = h_ctx + cg1 * rmsnorm(m_ctx, mix_post_g[i])
            f_ctx = ffn(modulate(rmsnorm(h_ctx, ffn_pre_g[i]), csh2, csc2))
            h_ctx = h_ctx + cg2 * rmsnorm(f_ctx, ffn_post_g[i])
    return h_lat


_drawn_inputs = setup_inputs


def setup_inputs(seed=0):
    import zlib

    import numpy as np

    out = dict(_drawn_inputs(seed))
    spreads = {}
    factors = {'ev_ssm_conv_b': 3.547,
     'ev_ssm_d': 14.719,
     'od_mla_q_norm_g': 3.012,
     'od_gqa_sink': 64.0,
     'ev_hy_freq': 2.745}
    for name, (base, spread) in spreads.items():
        noise = np.random.default_rng([zlib.crc32(name.encode()), seed]).standard_normal(out[name].shape)
        drawn = base * np.exp(spread * noise) if base else spread * noise
        out[name] = jnp.asarray(drawn.astype(out[name].dtype))
    for name, factor in factors.items():
        out[name] = (out[name] * factor).astype(out[name].dtype)
    return out
```

```python
from contextlib import ExitStack

import numpy as np

import concourse.bass as bass
from concourse import mybir

ALU = mybir.AluOpType
ACT = mybir.ActivationFunctionType
F32 = mybir.dt.float32
I32 = mybir.dt.int32
AX_X = mybir.AxisListType.X

P = 128
D = 1024
KD = D // P
CTX = 256
LAT = 256
T = CTX + LAT
NCH = T // P
GW = D // 2
FF = 2816
NFF = FF // P
NEXP = 8
FFE = 3584
NFE = FFE // P
HEADS = 8
EPS = 1e-6
GRID_W = 64
UNIT = 1024
SLOTS = 6

N_ADA_A = 8
N_EVIN = 12
N_EVOUT = 4
N_GU = NFF
N_ADA_C = 2
N_DOWN = NFF // 2
N_ODIN = 4
N_ODOUT = 4
S_EVIN = N_ADA_A
S_EVOUT = S_EVIN + 2 * N_EVIN
S_GU = S_EVOUT + 2 * N_EVOUT
S_ADAC = S_GU + 2 * N_GU
S_DOWN = S_ADAC + N_ADA_C
S_ODIN = S_DOWN + N_DOWN
S_ODOUT = S_ODIN + N_ODIN
N_PRE = S_ODOUT + N_ODOUT
E_SLOTS = 3 * NFE // 2
N_MOE = NEXP * E_SLOTS
TIERS = (128, 168, 208, 256)

VEC = {}
_n = 0
for _name, _w in [("ada_b0", 48), ("ada_b1", 48), ("mix_pre0", 8), ("mix_pre1", 8), ("mix_post0", 8), ("mix_post1", 8),
                  ("ffn_pre0", 8), ("ffn_pre1", 8), ("ffn_post0", 8), ("ffn_post1", 8), ("hy_w", 36), ("hy_b", 12),
                  ("hy_bias", 4), ("ssm_w", 24), ("ssm_b", 8), ("ssm_d", 4), ("norm_g", 4), ("q_norm", 2),
                  ("kv_norm", 1), ("dt_bias", 16), ("a_log", 16), ("sink", 8), ("f_b1", 1), ("f_b2", 1),
                  ("f_freq", 1), ("firstrow", 2)]:
    VEC[_name] = (_n, _w)
    _n += _w
NVEC = _n

NORMS = [(8, D, T), (2, 256, T), (2, 256, T), (8, D, T), (8, D, T), (8, D, T),
         (8, D, T), (2, 256, LAT), (1, 128, T), (8, D, LAT), (8, D, LAT), (8, D, LAT)]
(PRE0, SSMG0, SSMG1, POST0, FPRE0, FPOST0, PRE1, QLAT, KVLAT, POST1, FPRE1, FPOST1) = range(12)


RSTD_USED = [("scaled", 8), ("ymix_ready", 6), ("ymix_ready", 8), ("h_ready", 8), ("scaled", 16), ("h_ready", 16),
             ("scaled", 24), ("lat_ready", 2), ("lat_ready", 3), ("h_ready", 24), ("scaled", 32)]
STATE_ORDER = [(0, 0), (1, 1), (1, 0), (0, 1), (2, 0), (3, 1)]
XD_ORDER = STATE_ORDER + [(3, 0), (2, 1)]
NEXT = {(0, 0): 1, (1, 0): 2, (2, 0): 3, (1, 1): 0, (0, 1): 3, (3, 1): 2}
ZERO_STATE = [(0, 0), (1, 1)]
MAGIC = 12582912.0
TWO_PI_HI, TWO_PI_LO = 6.28125, 0.0019353071795864769
PI_DOWN = 3.1415925


def bc_last(ap, n):
    if len(ap.shape) == 3:
        ap = ap.rearrange("p a b -> p (a b)")
    return ap.unsqueeze(2).to_broadcast([ap.shape[0], ap.shape[1], n])


def bc_mid(ap, n):
    return ap.unsqueeze(1).to_broadcast([ap.shape[0], n, ap.shape[1]])


def gu_slot(t):
    return t if t < 2 else 3 * (t // 2) - 1 + t % 2


def squares_before(n):
    return sum(t for t, _, _ in NORMS[:n])


def build(nc, io):
    ctx = ExitStack()
    with ctx:
        def sb(name, shape, dt=F32):
            return ctx.enter_context(nc.sbuf_tensor(name, shape, dt))

        sems = {}

        def sem(name):
            if name not in sems:
                sems[name] = ctx.enter_context(nc.semaphore(name))
            return sems[name]

        bank = [ctx.enter_context(nc.psum_tensor(f"bank{i}", [P, 512], F32)) for i in range(8)]

        ring = sb("ring", [P, SLOTS, 2 * UNIT])
        hT = sb("hT", [P, KD, T])
        aT = sb("aT", [P, KD, T])
        mT = sb("mT", [P, KD, T])
        yT = sb("yT", [P, KD, T])
        vec = sb("vec", [P, NVEC])
        ident = sb("ident", [P, P])
        ones = sb("ones", [P, P])
        tri = sb("tri", [P, 2, P])
        cond = sb("cond", [P, KD, 2])
        cond_e = sb("cond_e", [P, KD, 2])
        mod = sb("mod", [P, 2, 48, 2])
        coef = sb("coef", [P, 2, 4, KD, 2])
        rstd = sb("rstd", [P, T])
        lnv = sb("lnv", [P, T])
        tmp = sb("tmp", [P, 2, T])
        eps = sb("eps", [P, 1])
        mark_ = sb("mark_", [P, 4])
        zeros = sb("zeros", [P, 512])
        ARENA = 20100
        arena = sb("arena", [P, ARENA])

        carved = [0]

        def carve(*shape):
            n = int(np.prod(shape))
            v = arena[:, carved[0]:carved[0] + n]
            carved[0] += n
            assert carved[0] <= ARENA, carved[0]
            if len(shape) == 1:
                return v
            names = "abcd"[:len(shape)]
            spec = " ".join(names)
            return v.rearrange(f"p ({spec}) -> p {spec}", **{k: s for k, s in zip(names, shape)})

        x0 = carve(4, T)
        u = carve(4, T)
        conv = carve(8, T)
        z = carve(4, T)
        xs, bT, cT = conv[:, 0:4, :], conv[:, 4:6, :], conv[:, 6:8, :]
        mark = carved[0]
        dft = carve(2, 512)
        dftB = carve(2, P)
        dftD = carve(2, P)
        idft = carve(4, 256)
        spec = carve(5, 512)
        u_tok = yT[:, 4:8, :]
        pm = carve(2, 2, 512)
        prod = carve(4, 512)
        filt_small = mT[:, 6:8, :].rearrange("p a b -> p (a b)")
        Y = mT[:, :, :].rearrange("p (f s) c -> p f s c", f=4)
        decay = mT[:, 0:2, :]
        w3 = mT[:, 2:4, :].rearrange("p a b -> p (a b)")[0:64, :]
        zT = filt_small[0:33, 0:256]
        w1 = filt_small[0:33, 256:320]
        w2 = filt_small[0:64, 320:384]
        hid = [filt_small[0:64, 384 + 256 * i:640 + 256 * i] for i in range(2)]
        hk = mT[0:64, 4, 0:256]
        harg = mT[0:64, 5, 0:256]
        vtmp = yT[:, 0:4, :]
        carved[0] = mark
        xs_tok = carve(4, 512)
        b_tok = carve(4, 256)
        cb = carve(4, 2, 2, P)
        CS = carve(NCH, 32)
        ncs = carve(4, 16)
        dec = carve(4, 16)
        etot = carve(4, 16)
        dt_x, dt_r, sp, dtt, att = (tmp[:, 1, 64 * i:64 * (i + 1)].rearrange("p (c n) -> p c n", c=NCH)
                                    for i in range(5))
        xd = aT[:, :, :].rearrange("p (c e) f -> p c e f", c=4)
        xdd = x0[:, 0:2, :]
        st = mT[:, :, :].rearrange("p (c e) f -> p c e f", c=4)
        dif = u[:, 0:2, :]
        lm = u[:, 2:4, :]
        er = carve(2, 512)
        sc = carve(3, 512)
        ce = carve(3, 512)
        w_dt = tmp[:, 0, 0:P].rearrange("p (k n) -> p k n", k=KD)
        nega = tmp[:, 0, P:P + 16]
        ssd_end = carved[0]
        carved[0] = 0
        hff = carve(NFF, T)
        sg = carve(2, T)
        carved[0] = 0
        qlat = carve(2, LAT)
        kvlat = carve(T)
        qh = carve(HEADS, LAT)
        kcat = carve(HEADS, T)
        v_tok = carve(NCH, 512)
        qg = carve(4, LAT)
        kg = carve(T)
        vg_tok = carve(NCH, P)
        w_krv = carve(KD, 160)
        q_up = carve(2, 768)
        kv_up = carve(1024)
        rope_g = carve(2, LAT)
        rope_m = carve(2, LAT)
        perm_g = carve(P)
        perm_m = carve(P)
        wmask = carve(2, LAT)
        pr = mT[:, 0:4, :]
        scr = mT[:, 4:6, :]
        scw = carve(2, T + 1)
        pT = carve(2, NCH, P)
        stat = carve(8, 4)
        sinks = carve(8)
        carved[0] = 0
        router = carve(KD, NEXP)
        lower8 = carve(NEXP, NEXP)
        rt = carve(2, 2, 64)
        lg = carve(2, 8)
        rank = carve(2, 8)
        sel = carve(2, 2, 8)
        mval = carve(2, 8)
        gates = carve(2, 8)
        gv = carve(2, 8)
        seltok = carve(2, 8)
        key = carve(2, NEXP + 1)
        tier = carve(NEXP).bitcast(I32)
        tier_f = carve(3, NEXP)
        iota = carve(LAT)
        iota_p = carve(2)
        krow = carve(NEXP, LAT)
        gbc = carve(NEXP, LAT)
        a_tokm = carve(2, D)
        xg = carve(KD, LAT)
        perm = carve(2, LAT)
        spread = carve(2, LAT)
        y_e = carve(KD, LAT)
        y_row = carve(2, D)
        acc = mT[:, :, 0:LAT]
        hmoe = carve(4, LAT)
        sgm = carve(4, LAT)

        def V(name, i=0, n=1, p=P):
            at, w = VEC[name]
            return vec[0:p, at + i:at + i + n]

        SEQ = [slice(0, CTX), slice(CTX, T)]

        def norm_cols(n):
            return slice(0, T) if NORMS[n][2] == T else slice(0, LAT)

        def slot_tile(s, unit, k):
            return ring[:, s % SLOTS, unit * UNIT + k * P:unit * UNIT + (k + 1) * P]

        SMALL = [(vec[:, :], "vec"), (cond[:, :, :], "cond"), (zT, "zT"), (w1, "w1"), (w2, "w2"), (w3, "w3"),
                 (hT[:, :, :], "xT"), (ident[:, :], "ident"), (tri[:, :, :], "tri"), (decay, "decay"), (dft, "dft"),
                 (dftB, "dftB"), (dftD, "dftD"), (idft, "idft"), (w_dt, "w_dt")]
        OD_SMALL = [(w_krv, "w_krv"), (q_up, "q_up"), (kv_up, "kv_up"), (rope_g, "rope_g"), (rope_m, "rope_m"),
                    (perm_g, "perm_g"), (perm_m, "perm_m"), (wmask, "wmask")]
        block = ctx.enter_context(nc.Block())

        @block.sync
        def _(sp_):
            for s in range(SLOTS):
                sp_.dma_start(ring[:, s, :], io["pre"][s]).then_inc(sem(f"slot{s}_in"), 16)
            rounds = (N_PRE - SLOTS) // SLOTS
            with sp_.Fori(0, rounds) as i:
                for s in range(SLOTS):
                    sp_.wait_ge(sem("slot_used"), i * SLOTS + (s + 1))
                    sp_.dma_start(ring[:, s, :], io["pre"][i * SLOTS + (SLOTS + s)]).then_inc(sem(f"slot{s}_in"), 16)
            for n in range(SLOTS * (rounds + 1), N_PRE):
                sp_.wait_ge(sem("slot_used"), n - SLOTS + 1)
                sp_.dma_start(ring[:, n % SLOTS, :], io["pre"][n]).then_inc(sem(f"slot{n % SLOTS}_in"), 16)
            with sp_.Fori(0, N_MOE // SLOTS) as i:
                for s in range(SLOTS):
                    sp_.wait_ge(sem("slot_used"), i * SLOTS + (N_PRE + s - SLOTS + 1))
                    sp_.dma_start(ring[:, (N_PRE + s) % SLOTS, :], io["moe"][i * SLOTS + s]).then_inc(
                        sem(f"slot{(N_PRE + s) % SLOTS}_in"), 16)

            for k in range(2):
                sp_.wait_ge(sem("h_ready"), 28 + 4 * k)
                sp_.dma_start(io["out"][:, 4 * k:4 * k + 4, :], hT[:, 4 * k:4 * k + 4, CTX:T]).then_inc(sem("stored"), 16)
            sp_.wait_ge(sem("stored"), 32)

        @block.tensor
        def _(pe):
            def slot_wait(s, base=0):
                pe.wait_ge(sem(f"slot{s % SLOTS}_in"), base * 16 + 16 * (s // SLOTS + 1))

            def ada_slot(s, dst, j, rounds=0):
                slot_wait(s, rounds)
                for h in range(2):
                    for k in range(KD):
                        m = pe.matmul(dst[:, 2 * (j + h):2 * (j + h) + 2], slot_tile(s, h, k), cond[:, k, :],
                                      start=(k == 0), stop=(k == KD - 1))
                m.then_inc(sem("slot_used"), 1)

            def norm_sum(n, src):
                tiles, _, tok = NORMS[n]
                if n >= 1:
                    pe.wait_ge(sem("ln_done"), n)
                for k in range(tiles):
                    pe.wait_ge(sem("square_ready"), squares_before(n) + k + 1)
                    m = pe.matmul(bank[7][:, 0:tok], ones[:, :], src(k), start=(k == 0), stop=(k == tiles - 1))
                m.then_inc(sem("norm_sum"), 1)

            pe.wait_ge(sem("small_in"), 16 * len(SMALL))
            pe.matmul(bank[0][0:64, 0:256], w1, zT, start=True, stop=True).then_inc(sem("filt_mm"), 1)
            pe.wait_ge(sem("filt_sin"), 1)
            pe.matmul(bank[1][0:64, 0:256], w2, hid[0], start=True, stop=True).then_inc(sem("filt_mm"), 1)
            pe.wait_ge(sem("filt_sin"), 2)
            for t in range(2):
                for d in range(2):
                    m = pe.matmul(bank[2 + 2 * t + d][:, :], hid[1][:, t * P:(t + 1) * P], w3[:, d * 512:(d + 1) * 512],
                                  start=True, stop=True)
                m.then_inc(sem("filt_mm"), 1)

            pe.wait_ge(sem("cond_ready"), 1)
            for s in range(N_ADA_A):
                ada_slot(s, bank[6], 2 * s)
            norm_sum(PRE0, lambda k: aT[:, k, :])

            pe.wait_ge(sem("filt_pm"), 4)
            for i, (w, src) in enumerate([(dft[:, :, 0:P], 0), (dft[:, :, P:2 * P], 0), (dftB, 1),
                                          (dft[:, :, 3 * P:4 * P], 1), (dftD, 0)]):
                for t in range(2):
                    m = pe.matmul(bank[i][:, :], w[:, t, :], pm[:, src, t, :], start=(t == 0), stop=(t == 1))
                m.then_inc(sem("spec_mm"), 1)
            pe.wait_ge(sem("spec_ready"), 5)

            pe.wait_ge(sem("mod_ready"), 1)
            for s in range(N_EVIN):
                n = S_EVIN + 2 * s
                slot_wait(n)
                for h in range(2):
                    j = 2 * s + h
                    if j >= 4:
                        pe.wait_ge(sem("conv_done"), j - 3)
                    for k in range(KD):
                        if j == 0:
                            pe.wait_ge(sem("a_ready"), k + 1)
                        m = pe.matmul(bank[j % 4][:, :], slot_tile(n, h, k), aT[:, k, :],
                                      start=(k == 0), stop=(k == KD - 1))
                    if h == 0:
                        m.then_inc(sem("proj_mm"), 1)
                m.then_inc(sem("slot_used"), 1)
                ada_slot(n + 1, bank[6], 2 * s)
            for c in range(NCH):
                for k in range(KD):
                    m = pe.matmul(bank[4][:, 16 * c:16 * c + 16], aT[:, k, c * P:(c + 1) * P], w_dt[:, k, :],
                                  start=(k == 0), stop=(k == KD - 1))
            m.then_inc(sem("dt_mm"), 1)

            for c in range(NCH):
                if c == 0:
                    pe.wait_ge(sem("u_ready"), 4)
                    pe.wait_ge(sem("z_ready"), 4)
                for i in range(4):
                    m = pe.transpose(bank[c][:, i * P:(i + 1) * P], u[:, i, c * P:(c + 1) * P], ident[:, :])
                m.then_inc(sem("u_tr"), 1)
            for s in range(2):
                for t in range(2):
                    g = 2 * s + t
                    b = 2 * (g % 2)
                    pe.wait_ge(sem("u_tok"), 4)
                    if g >= 2:
                        pe.wait_ge(sem("prod_mul"), 4 * (g - 1))
                    for ri in range(2):
                        for kt in range(2):
                            m = pe.matmul(bank[b + ri][:, :], dft[:, kt, (2 * ri + t) * P:(2 * ri + t + 1) * P],
                                          u_tok[:, 2 * s + kt, :], start=(kt == 0), stop=(kt == 1))
                    m.then_inc(sem("U_mm"), 1)
            pe.wait_ge(sem("Y_ready"), 8)
            pe.wait_ge(sem("prod_mul"), 16)
            for i in range(4):
                for s in range(2):
                    for f in range(4):
                        m = pe.matmul(bank[i][:, s * 256:(s + 1) * 256], Y[:, f, s, i * P:(i + 1) * P], idft[:, f, :],
                                      start=(f == 0), stop=(f == 3))
                m.then_inc(sem("iy_mm"), 1)

            for c in range(NCH):
                if c >= 1:
                    pe.wait_ge(sem("tok_copied"), 2 * c - 1)
                if c == 0:
                    pe.wait_ge(sem("xbc_ready"), 8)
                    pe.wait_ge(sem("sp_ready"), 1)
                for i in range(4):
                    m = pe.transpose(bank[5][:, i * P:(i + 1) * P], xs[:, i, c * P:(c + 1) * P], ident[:, :])
                m.then_inc(sem("tok_tr"), 1)
                if c >= 1:
                    pe.wait_ge(sem("tok_copied"), 2 * c)
                for i in range(2):
                    m = pe.transpose(bank[4][:, i * P:(i + 1) * P], bT[:, i, c * P:(c + 1) * P], ident[:, :])
                m.then_inc(sem("tok_tr"), 1)
            pe.wait_ge(sem("a_tok"), 1)
            pe.wait_ge(sem("iy_read"), 4)
            for c in range(NCH):
                for d in range(2):
                    pe.matmul(bank[0][:, 32 * c + 8 * d:32 * c + 8 * d + 8], tri[:, d, :], att[:, c, 8 * d:8 * d + 8],
                              start=True, stop=True)
                m = pe.matmul(bank[0][:, 32 * c + 16:32 * c + 32], ones[:, :], att[:, c, :], start=True, stop=True)
            m.then_inc(sem("cs_mm"), 1)
            for c in range(NCH):
                if c >= 2:
                    pe.wait_ge(sem("cb_ready"), 4 * (c - 1))
                for g in range(2):
                    m = pe.matmul(bank[1 + c % 2][:, g * P:(g + 1) * P], bT[:, g, c * P:(c + 1) * P],
                                  cT[:, g, c * P:(c + 1) * P], start=True, stop=True)
                m.then_inc(sem("cb_mm"), 1)
            for n, (c, d) in enumerate(STATE_ORDER):
                pe.wait_ge(sem("xdd_ready"), n + 1)
                if n >= 1:
                    pe.wait_ge(sem("state_ready"), n)
                else:
                    pe.wait_ge(sem("tok_copied"), 8)
                for g in range(2):
                    m = pe.matmul(bank[3][:, g * 256:(g + 1) * 256], b_tok[:, c, g * P:(g + 1) * P],
                                  xdd[:, n % 2, g * 256:(g + 1) * 256], start=True, stop=True)
                m.then_inc(sem("state_mm"), 1)

            def rows(r):
                c, g, d = r // 4, r // 2 % 2, r % 2
                if r >= 2:
                    pe.wait_ge(sem("row_dif"), 4 * (r - 1))
                    pe.wait_ge(sem("row_exp"), r - 1)
                elif r == 0:
                    pe.wait_ge(sem("cs_ready"), 1)
                else:
                    pe.wait_ge(sem("cb_ready"), 16)
                for i in range(4):
                    h = 8 * d + 4 * g + i
                    m = pe.matmul(bank[r % 2][:, i * P:(i + 1) * P],
                                  att[:, c, h:h + 1].to_broadcast([P, P]), tri[:, d, :], start=True, stop=True)
                m.then_inc(sem("row_mm"), 1)

            rows(0)
            rows(1)
            pe.wait_ge(sem("state_ready"), 6)
            for r in range(0, 16, 2):
                c, g = r // 4, r // 2 % 2
                if r + 2 < 16:
                    rows(r + 2)
                    rows(r + 3)
                pe.wait_ge(sem("sc_ready"), r + 2)
                pe.wait_ge(sem("ce_ready"), r + 2)
                yb = bank[4 + c % 2]
                if g == 0 and c >= 2:
                    pe.wait_ge(sem("y_read"), 4 * (c - 1))
                for i in range(4):
                    h = 4 * g + i
                    p0 = 64 * (h % 2)
                    out = yb[p0:p0 + 64, (h // 2) * P:(h // 2 + 1) * P]
                    terms = []
                    for d in range(2):
                        terms.append((xd[:, c, d, h * 64:(h + 1) * 64], sc[:, (r + d) % 3, i * P:(i + 1) * P]))
                        if (c, d) not in ZERO_STATE:
                            terms.append((st[:, c, d, h * 64:(h + 1) * 64], ce[:, (r + d) % 3, i * P:(i + 1) * P]))
                    for n, (w, x) in enumerate(terms):
                        m = pe.matmul(out, w, x, start=(n == 0), stop=(n == len(terms) - 1))
                m.then_inc(sem("y_mm"), 1)
            norm_sum(SSMG0, lambda k: aT[:, k, :])
            norm_sum(SSMG1, lambda k: aT[:, 2 + k, :])

            pe.wait_ge(sem("ymix_ready"), 8)
            for s in range(N_EVOUT):
                n = S_EVOUT + 2 * s
                slot_wait(n)
                for h in range(2):
                    j = 2 * s + h
                    if j >= 4:
                        pe.wait_ge(sem("m_sb"), j - 3)
                    for k in range(KD):
                        m = pe.matmul(bank[j % 4][:, :], slot_tile(n, h, k), yT[:, k, :],
                                      start=(k == 0), stop=(k == KD - 1))
                    if h == 0:
                        m.then_inc(sem("m_mm"), 1)
                m.then_inc(sem("slot_used"), 1)
                ada_slot(n + 1, bank[6], 2 * (N_EVIN + s))
            norm_sum(POST0, lambda k: aT[:, k, :])
            norm_sum(FPRE0, lambda k: aT[:, k, :])

            pe.wait_ge(sem("a_ready"), 16)
            pe.wait_ge(sem("mod_ready"), 2)
            def gate_up(s, half):
                for h in range(2):
                    for k in range(KD):
                        m = pe.matmul(bank[2 * half + h][:, :], slot_tile(s, h, k), aT[:, k, :],
                                      start=(k == 0), stop=(k == KD - 1))
                m.then_inc(sem("slot_used"), 1)

            GR = NFF // 6
            with pe.Fori(0, GR) as i:
                for q in range(6):
                    s = S_GU + 2 * q
                    pe.wait_ge(sem(f"slot{s % SLOTS}_in"), i * 32 + 16 * (s // SLOTS + 1))
                    pe.wait_ge(sem("hff_done"), i * 6 + (q + 1))
                    gate_up(s, q % 2)
                    pe.wait_ge(sem(f"slot{(s + 1) % SLOTS}_in"), i * 32 + 16 * ((s + 1) // SLOTS + 1))
                    for h in range(2):
                        for k in range(KD):
                            m = pe.matmul(bank[6][:, bass.ds(i * 24 + (4 * q + 2 * h), 2)], slot_tile(s + 1, h, k),
                                          cond[:, k, :], start=(k == 0), stop=(k == KD - 1))
                    m.then_inc(sem("slot_used"), 1)
            for j in range(6 * GR, NFF):
                s = S_GU + 2 * j
                slot_wait(s)
                pe.wait_ge(sem("hff_done"), j + 1)
                gate_up(s, j % 2)
                ada_slot(s + 1, bank[6], 2 * j)
            for s in range(N_ADA_C):
                ada_slot(S_ADAC + s, bank[6], 2 * (NFF + s))

            pe.wait_ge(sem("hff_done"), 2 + NFF)
            pe.wait_ge(sem("mod_ready"), 3)
            pe.wait_ge(sem("ln_done"), 5)
            for s in range(N_DOWN):
                slot_wait(S_DOWN + s)
                for h in range(2):
                    f = 2 * s + h
                    for j in range(KD):
                        m = pe.matmul(bank[j][:, :], slot_tile(S_DOWN + s, h, j), hff[:, f, :],
                                      start=(f == 0), stop=(f == NFF - 1))
                        if f == NFF - 1 and j < KD - 1:
                            m.then_inc(sem("m_mm"), 1)
                m.then_inc(sem("slot_used"), 1)
            pe.wait_ge(sem("m_sb"), 16)
            norm_sum(FPOST0, lambda k: aT[:, k, :])

            norm_sum(PRE1, lambda k: aT[:, k, :])
            pe.wait_ge(sem("a_ready"), 24)
            for s in range(N_ODIN):
                slot_wait(S_ODIN + s)
                for h in range(2):
                    j = 2 * s + h
                    if j >= 4:
                        pe.wait_ge(sem("od_copied"), j - 3)
                    cols = slice(0, T) if j in (2, 7) else slice(CTX, T)
                    n = cols.stop - cols.start
                    for k in range(KD):
                        m = pe.matmul(bank[j % 4][:, 0:n], slot_tile(S_ODIN + s, h, k), aT[:, k, cols],
                                      start=(k == 0), stop=(k == KD - 1))
                    if h == 0:
                        m.then_inc(sem("od_mm"), 1)
                m.then_inc(sem("slot_used"), 1)
            pe.wait_ge(sem("od_in"), 16 * len(OD_SMALL))
            for k in range(KD):
                m = pe.matmul(bank[4][64:96, :], w_krv[:, k, 0:32], aT[:, k, :], start=(k == 0), stop=(k == KD - 1))
            m.then_inc(sem("kr_mm"), 1)
            for c in range(NCH):
                for k in range(KD):
                    m = pe.matmul(bank[5][:, c * P:(c + 1) * P], aT[:, k, c * P:(c + 1) * P], w_krv[:, k, 32:160],
                                  start=(k == 0), stop=(k == KD - 1))
            m.then_inc(sem("vg_mm"), 1)
            norm_sum(QLAT, lambda k: yT[:, k, 0:LAT])
            norm_sum(KVLAT, lambda k: yT[:, 2, :])
            pe.wait_ge(sem("od_copied"), 8)
            for j in range(4):
                m = pe.matmul(bank[j // 2][:, (j % 2) * LAT:(j % 2 + 1) * LAT], perm_g, qg[:, j, :], start=True, stop=True)
            m.then_inc(sem("rope_mm"), 1)
            m = pe.matmul(bank[2][:, 0:LAT], perm_g, kg[:, CTX:T], start=True, stop=True)
            m.then_inc(sem("rope_mm"), 1)
            pe.wait_ge(sem("kr_copied"), 1)
            m = pe.matmul(bank[3][64:96, 0:LAT], perm_m[64:96, 64:96], kcat[64:96, 0, CTX:T], start=True, stop=True)
            m.then_inc(sem("rope_mm"), 1)
            pe.wait_ge(sem("lat_ready"), 2)
            pe.wait_ge(sem("rope_done"), 6)
            for h in range(HEADS):
                if h >= 2:
                    pe.wait_ge(sem("qh_copied"), h - 1)
                for k in range(2):
                    m = pe.matmul(bank[h % 2][0:96, 0:LAT], q_up[:, k, h * 96:(h + 1) * 96], qlat[:, k, :],
                                  start=(k == 0), stop=(k == 1))
                m.then_inc(sem("qh_mm"), 1)
            for h in range(HEADS):
                pe.wait_ge(sem("qh_copied"), h + 1 if h >= 6 else 6)
                if h >= 2:
                    pe.wait_ge(sem("qrope_done"), h - 1)
                m = pe.matmul(bank[2 + h % 2][64:96, 0:LAT], perm_m[64:96, 64:96], qh[64:96, h, :], start=True, stop=True)
                m.then_inc(sem("qperm_mm"), 1)
            pe.wait_ge(sem("lat_ready"), 3)
            pe.wait_ge(sem("kr_copied"), 1)
            for h in range(HEADS):
                if h >= 2:
                    pe.wait_ge(sem("kn_copied"), h - 1)
                else:
                    pe.wait_ge(sem("qh_copied"), 8)
                m = pe.matmul(bank[h % 2][0:64, :], kv_up[:, h * 64:(h + 1) * 64], kvlat, start=True, stop=True)
                m.then_inc(sem("kn_mm"), 1)
            for c in range(NCH):
                b = 4 + c % 2
                if c >= 2:
                    pe.wait_ge(sem("v_copied"), c - 1)
                else:
                    pe.wait_ge(sem("vg_copied"), 1)
                m = pe.matmul(bank[b][:, :], kvlat[:, c * P:(c + 1) * P], kv_up[:, 512:1024], start=True, stop=True)
                m.then_inc(sem("v_mm"), 1)
            pe.wait_ge(sem("kn_copied"), 8)
            pe.wait_ge(sem("v_copied"), 4)
            pe.wait_ge(sem("qrope_done"), 8)
            pe.wait_ge(sem("krope_all"), 1)

            def scores(n):
                h, qt = n // 2, n % 2
                if n >= 2:
                    pe.wait_ge(sem("s_read"), n - 1)
                b = bank[n % 2]
                if h < HEADS:
                    m = pe.matmul(b[:, :], qh[0:96, h, qt * P:(qt + 1) * P], kcat[0:96, h, :], start=True, stop=True)
                else:
                    g = h - HEADS
                    p0 = 64 * (g // 4)
                    m = pe.matmul(b[:, :], qg[p0:p0 + 64, g % 4, qt * P:(qt + 1) * P], kg[p0:p0 + 64, :],
                                  start=True, stop=True)
                m.then_inc(sem("s_mm"), 1)

            def values(n):
                h, qt = n // 2, n % 2
                pe.wait_ge(sem("p_ready"), n + 1)
                if n >= 2:
                    pe.wait_ge(sem("pT_ready"), n - 1)
                for c in range(NCH):
                    m = pe.transpose(bank[2 + n % 2][:, c * P:(c + 1) * P], pr[:, n % 4, c * P:(c + 1) * P], ident[:, :])
                m.then_inc(sem("pT_mm"), 1)

            def output(n):
                h, qt = n // 2, n % 2
                pe.wait_ge(sem("pT_ready"), n + 1)
                if qt == 0 and h >= 2:
                    pe.wait_ge(sem("o_copied"), h - 1)
                if h < HEADS:
                    p0 = 64 * (h % 2)
                else:
                    p0 = 64 * ((h - HEADS) // 4)
                for c in range(NCH):
                    w = v_tok[:, c, h * 64:(h + 1) * 64] if h < HEADS else vg_tok[:, c, p0:p0 + 64]
                    m = pe.matmul(bank[4 + h % 2][p0:p0 + 64, qt * P:(qt + 1) * P], w, pT[:, n % 2, c, :],
                                  start=(c == 0), stop=(c == NCH - 1))
                m.then_inc(sem("o_mm"), 1)

            for n in range(34 + 1):
                if n < 32:
                    scores(n)
                if 2 <= n < 34:
                    values(n - 2)
                if n >= 3:
                    output(n - 3)

            pe.wait_ge(sem("o_copied"), 16)
            for s in range(N_ODOUT):
                slot_wait(S_ODOUT + s)
                for h in range(2):
                    j = 2 * s + h
                    if j >= 4:
                        pe.wait_ge(sem("m_sb"), 16 + j - 3)
                    for k in range(KD):
                        m = pe.matmul(bank[j % 4][:, 0:LAT], slot_tile(S_ODOUT + s, h, k), yT[:, k, 0:LAT],
                                      start=(k == 0), stop=(k == KD - 1))
                    if h == 0:
                        m.then_inc(sem("m_mm"), 1)
                m.then_inc(sem("slot_used"), 1)
            norm_sum(POST1, lambda k: aT[:, k, 0:LAT])
            norm_sum(FPRE1, lambda k: aT[:, k, 0:LAT])

            pe.wait_ge(sem("a_ready"), 32)
            pe.wait_ge(sem("router_in"), 64)
            for c in range(2):
                for k in range(KD):
                    m = pe.matmul(bank[0][:, 8 * c:8 * c + 8], aT[:, k, c * P:(c + 1) * P], router[:, k, :],
                                  start=(k == 0), stop=(k == KD - 1))
            m.then_inc(sem("router_mm"), 1)
            pe.wait_ge(sem("sel_ready"), 1)
            for c in range(2):
                if c == 1:
                    pe.matmul(bank[1][:, 8:16], ones[:, :], seltok[:, 0, :], start=True, stop=False)
                pe.matmul(bank[1][:, 8 * c:8 * c + 8], tri[:, 0, :], seltok[:, c, :], start=(c == 0), stop=True)
            for c in range(2):
                m = pe.matmul(bank[1][:, 16:24], ones[:, :], seltok[:, c, :], start=(c == 0), stop=(c == 1))
            m.then_inc(sem("pos_mm"), 1)
            pe.wait_ge(sem("ln_done"), 11)
            for c in range(2):
                for k in range(KD):
                    m = pe.transpose(bank[4 + 2 * c + k // 4][:, (k % 4) * P:(k % 4 + 1) * P], aT[:, k, c * P:(c + 1) * P], ident[:, :])
            m.then_inc(sem("a_tr"), 1)
            pe.wait_ge(sem("key_ready"), 1)
            for x, what in enumerate((gates, key)):
                if x == 1:
                    pe.wait_ge(sem("gbc_ready"), 4)
                for e in range(NEXP):
                    for c in range(2):
                        m = pe.matmul(bank[e // 2][:, (e % 2) * LAT + c * P:(e % 2) * LAT + (c + 1) * P],
                                      what[:, c, e:e + 1].to_broadcast([P, P]), ident[:, :], start=True, stop=True)
                m.then_inc(sem("gbc_mm"), 1)

            def moe_slot(e, n):
                s = N_PRE + n
                pe.wait_ge(sem(f"slot{s % SLOTS}_in"), e * (16 * E_SLOTS // SLOTS) + 16 * (s // SLOTS + 1))

            def gather(e, rows):
                pe.wait_ge(sem("perm_ready"), e + 1)
                pe.wait_ge(sem("hmoe_done"), e * NFE + 4)
                for k in range(KD):
                    for c in range(2):
                        m = pe.matmul(bank[k // 2][:, (k % 2) * LAT:(k % 2) * LAT + rows], a_tokm[:, c, k * P:(k + 1) * P],
                                      perm[:, c, 0:rows], start=(c == 0), stop=(c == 1))
                    if k % 2:
                        m.then_inc(sem("x_mm"), 1)

            def gate_up_tile(e, i, t, rows):
                n = gu_slot(t)
                pe.wait_ge(sem(f"slot{(N_PRE + n) % SLOTS}_in"),
                           e * (16 * E_SLOTS // SLOTS) + i * 16 + 16 * ((N_PRE + n) // SLOTS + 1))
                pe.wait_ge(sem("hmoe_done"), e * NFE + i * 4 + (t + 1))
                for h in range(2):
                    for k in range(KD):
                        m = pe.matmul(bank[t % 4][:, h * LAT:h * LAT + rows], slot_tile(N_PRE + n, h, k), xg[:, k, 0:rows],
                                      start=(k == 0), stop=(k == KD - 1))
                m.then_inc(sem("slot_used"), 1)

            def down_pair(e, i, p, rows, n, first=False, last=False):
                pe.wait_ge(sem(f"slot{(N_PRE + n) % SLOTS}_in"),
                           e * (16 * E_SLOTS // SLOTS) + i * 16 + 16 * ((N_PRE + n) // SLOTS + 1))
                for h in range(2):
                    pe.wait_ge(sem("hmoe_done"), e * NFE + i * 4 + (4 + 2 * p + h + 1))
                    for j in range(KD):
                        m = pe.matmul(bank[4 + j // 2][:, (j % 2) * LAT:(j % 2) * LAT + rows], slot_tile(N_PRE + n, h, j),
                                      hmoe[:, (2 * p + h) % 4, 0:rows], start=(first and h == 0 and j % 2 == 0),
                                      stop=(last and h == 1), skip_group_check=True)
                m.then_inc(sem("slot_used"), 1)

            def rows_major(e):
                pe.wait_ge(sem("ye_ready"), e * 4 + 4)
                for b in range(2):
                    for j in range(KD):
                        m = pe.transpose(bank[4 + 2 * b + j // 4][:, (j % 4) * P:(j % 4 + 1) * P],
                                         y_e[:, j, b * P:(b + 1) * P], ident[:, :])
                m.then_inc(sem("row_tr"), 1)

            def scatter(e):
                pe.wait_ge(sem("y_row_ready"), e * 4 + 4)
                pe.wait_ge(sem("spread_ready"), e + 1)
                for j in range(KD):
                    for b in range(2):
                        m = pe.matmul(bank[4 + j // 2][:, (j % 2) * LAT:(j % 2 + 1) * LAT], y_row[:, b, j * P:(j + 1) * P],
                                      spread[:, b, :], start=(b == 0), stop=(b == 1))
                m.then_inc(sem("scatter_mm"), 1)

            pe.wait_ge(sem("gbc_ready"), 8)
            pe.wait_ge(sem("moe_start"), 1)
            with pe.Fori(0, NEXP) as e:
                mine = pe.value_load(tier[0:1, bass.ds(e, 1)], min_val=0, max_val=len(TIERS) - 1)
                for n, rows in enumerate(TIERS):
                    with pe.If(mine == n):
                        gather(e, rows)
                        pe.wait_ge(sem("x_ready"), e * 4 + 4)
                        for t in range(2):
                            gate_up_tile(e, 0, t, rows)
                        rows_major(e)
                        for t in range(2, 4):
                            gate_up_tile(e, 0, t, rows)
                        scatter(e)
                        pe.wait_ge(sem("acc_done"), e * 4 + 4)
                        down_pair(e, 0, 0, rows, 4, first=True)
                        with pe.Fori(0, NFE // 4 - 1) as i:
                            for p in range(2):
                                for t in range(2):
                                    gate_up_tile(e, i, 4 + 2 * p + t, rows)
                                down_pair(e, i, 1 + p, rows, 3 * (1 + p) + 4)
                        down_pair(e, 0, NFE // 2 - 1, rows, E_SLOTS - 1, last=True)
            rows_major(NEXP)
            scatter(NEXP)
            pe.wait_ge(sem("acc_done"), 4 * NEXP + 4)
            norm_sum(FPOST1, lambda k: yT[:, k, 0:LAT])

        @block.scalar
        def _(act):
            for dst, name in SMALL:
                act.dma_start(dst, io[name]).then_inc(sem("small_in"), 16)
            act.wait_ge(sem("small_in"), 16 * len(SMALL))
            act.activation(cond_e[:, :, :], cond[:, :, :], ACT.Silu).then_inc(sem("cond_silu"), 1)
            act.wait_ge(sem("cond_silu"), 1)
            act.activation(cond[:, :, :], cond_e[:, :, :], ACT.Copy).then_inc(sem("cond_ready"), 1)
            for i in range(2):
                act.wait_ge(sem("filt_arg"), i + 1)
                act.activation(hid[i], hk, ACT.Sin).then_inc(sem("filt_sin"), 1)

            def product(j, name, count, slot):
                if j % 2 == 0:
                    act.wait_ge(sem(name), count)
                else:
                    act.wait_ge(sem("slot_used"), slot + 1)

            def squares(n, src, dst):
                for k in range(NORMS[n][0]):
                    act.activation(dst(k), src(k), ACT.Square).then_inc(sem("square_ready"), 1)

            def rstd_of(n):
                _, feat, tok = NORMS[n]
                act.wait_ge(sem("norm_sum"), n + 1)
                if n >= 1:
                    name, value = RSTD_USED[n - 1]
                    act.wait_ge(sem(name), value)
                act.activation(lnv[:, 0:tok], bank[7][:, 0:tok], ACT.Ln, bias=eps[:, 0:1], scale=1.0 / feat).then_inc(sem("ln_done"), 1)
                act.wait_ge(sem("ln_done"), n + 1)
                act.activation(rstd[:, 0:tok], lnv[:, 0:tok], ACT.Exp, scale=-0.5).then_inc(sem("rstd_ready"), 1)

            mods = [0]

            def modulate(layer, sub, tok_all=True):
                first = 8 * [0, 1, 2, 3][mods[0]]
                for k in range(KD):
                    act.wait_ge(sem("scaled"), first + k + 1)
                    for s in ((0, 1) if tok_all else (1,)):
                        cols = SEQ[s] if tok_all else slice(0, LAT)
                        m = act.activation(aT[:, k, cols], aT[:, k, cols], ACT.Identity,
                                           bias=mod[:, layer, (0 if sub == 0 else 24) + k, s:s + 1],
                                           scale=coef[:, layer, 2 * sub, k, s:s + 1])
                    m.then_inc(sem("a_ready"), 1)
                mods[0] += 1

            squares(PRE0, lambda k: hT[:, k, :], lambda k: aT[:, k, :])
            for i in range(5):
                act.wait_ge(sem("spec_mm"), i + 1)
                act.activation(spec[:, i, :], bank[i][:, :], ACT.Copy).then_inc(sem("spec_ready"), 1)
            rstd_of(PRE0)
            act.wait_ge(sem("mod_ready"), 1)
            modulate(0, 0)
            for j in range(20 + 1):
                if j < 20:
                    product(j, "proj_mm", j // 2 + 1, S_EVIN + 2 * (j // 2))
                    if j < 12:
                        w, b = V("hy_w", 12 + j), V("hy_b", j)
                        if 8 <= j:
                            dst = vtmp[:, j - 8, :]
                        else:
                            dst = x0[:, j, :] if j < 4 else u[:, j - 4, :]
                    else:
                        w, b = V("ssm_w", 8 + j - 12), V("ssm_b", j - 12)
                        dst = conv[:, j - 12, :]
                    act.activation(dst, bank[j % 4][:, :], ACT.Identity, bias=b, scale=w).then_inc(sem("conv_mid"), 1)
                if j >= 13:
                    act.wait_ge(sem("conv_done"), j)
                    act.activation(conv[:, j - 13, :], conv[:, j - 13, :], ACT.Silu).then_inc(sem("xbc_ready"), 1)
            for j in range(4):
                product(20 + j, "proj_mm", (20 + j) // 2 + 1, S_EVIN + 2 * ((20 + j) // 2))
                act.activation(z[:, j, :], bank[j][:, :], ACT.Silu).then_inc(sem("z_ready"), 1)
            for c in range(NCH):
                act.wait_ge(sem("u_tr"), c + 1)
                act.activation(u_tok[:, c, :], bank[c][:, :], ACT.Copy).then_inc(sem("u_tok"), 1)
            act.wait_ge(sem("sp_ready"), 1)
            act.activation(sp[:, :, :], sp[:, :, :], ACT.Exp).then_inc(sem("sp_exp"), 1)
            act.wait_ge(sem("sp_exp"), 1)
            act.activation(sp[:, :, :], sp[:, :, :], ACT.Ln, bias=1.0).then_inc(sem("sp_ln"), 1)
            act.activation(nega, V("a_log", 0, 16), ACT.Exp).then_inc(sem("sp_ln"), 1)
            for c in range(NCH):
                act.wait_ge(sem("tok_tr"), 2 * c + 1)
                act.activation(xs_tok[:, c, :], bank[5][:, :], ACT.Copy).then_inc(sem("tok_copied"), 1)
                act.wait_ge(sem("tok_tr"), 2 * c + 2)
                act.activation(b_tok[:, c, :], bank[4][:, 0:256], ACT.Copy).then_inc(sem("tok_copied"), 1)
            act.wait_ge(sem("dec_arg"), 1)
            act.activation(dec[:, :, :], dec[:, :, :], ACT.Exp).then_inc(sem("dec_ready"), 1)
            act.activation(etot[:, :, :], CS[:, :, 16:32], ACT.Exp).then_inc(sem("dec_ready"), 1)
            for r in range(16):
                act.wait_ge(sem("row_mm"), r + 1)
                if r >= 2:
                    act.wait_ge(sem("ce_ready"), r - 1)
                    act.wait_ge(sem("sc_ready"), r - 1)
                act.activation(er[:, r % 2, :], bank[r % 2][:, :], ACT.Exp).then_inc(sem("row_exp"), 1)
                act.wait_ge(sem("row_dif"), 4 * (r + 1))
                act.activation(lm[:, r % 2, :], dif[:, r % 2, :], ACT.Exp).then_inc(sem("l_ready"), 1)
            for g in range(2):
                for k in range(2):
                    if g == 0 and k == 0:
                        act.wait_ge(sem("y_gated"), 4)
                        act.wait_ge(sem("y_mm"), 8)
                    act.activation(aT[:, 2 * g + k, :], yT[:, 4 + 2 * g + k, :], ACT.Square).then_inc(sem("square_ready"), 1)
            rstd_of(SSMG0)
            rstd_of(SSMG1)

            def copy_and_square(n, first, width, banks, wait):
                for j in range(KD):
                    wait(j)
                    if j == 0 and n == POST0:
                        act.wait_ge(sem("norm_sum"), SSMG1 + 1)
                    act.activation(mT[:, j, 0:width], bank[banks(j)][:, 0:width], ACT.Copy).then_inc(sem("m_sb"), 1)
                    act.wait_ge(sem("m_sb"), first + j + 1)
                    act.activation(aT[:, j, 0:width], mT[:, j, 0:width], ACT.Square).then_inc(sem("square_ready"), 1)

            copy_and_square(POST0, 0, T, lambda j: j % 4,
                            lambda j: product(j, "m_mm", j // 2 + 1, S_EVOUT + 2 * (j // 2)))
            rstd_of(POST0)
            for k in range(KD):
                act.wait_ge(sem("h_ready"), k + 1)
                act.activation(aT[:, k, :], hT[:, k, :], ACT.Square).then_inc(sem("square_ready"), 1)
            rstd_of(FPRE0)
            modulate(0, 1)
            with act.Fori(0, NFF // 2) as i:
                for h in range(2):
                    act.wait_ge(sem("slot_used"), i * 4 + (S_GU + 2 * h + 1))
                    act.wait_ge(sem("hff_done"), i * 2 + (h + 1))
                    act.activation(sg[:, h, :], bank[2 * h][:, :], ACT.Silu).then_inc(sem("sg_ready"), 1)
            copy_and_square(FPOST0, 8, T, lambda j: j,
                            lambda j: act.wait_ge(sem("m_mm"), 4 + j + 1) if j < KD - 1 else
                            act.wait_ge(sem("slot_used"), S_ODIN))
            rstd_of(FPOST0)
            for k in range(KD):
                act.wait_ge(sem("h_ready"), 8 + k + 1)
                act.activation(aT[:, k, :], hT[:, k, :], ACT.Square).then_inc(sem("square_ready"), 1)
            for dst, name in OD_SMALL:
                act.dma_start(dst, io[name]).then_inc(sem("od_in"), 16)
            rstd_of(PRE1)
            modulate(1, 0)
            for j in range(8):
                product(j, "od_mm", j // 2 + 1, S_ODIN + j // 2)
                dst, n = [(qlat[:, 0, :], LAT), (qlat[:, 1, :], LAT), (kvlat, T), (qg[:, 0, :], LAT), (qg[:, 1, :], LAT),
                          (qg[:, 2, :], LAT), (qg[:, 3, :], LAT), (kg, T)][j]
                act.activation(dst, bank[j % 4][:, 0:n], ACT.Copy).then_inc(sem("od_copied"), 1)
                if j < 3:
                    act.wait_ge(sem("od_copied"), j + 1)
                    act.activation(yT[:, j, 0:n], dst, ACT.Square).then_inc(sem("square_ready"), 1)
            act.wait_ge(sem("kr_mm"), 1)
            act.activation(kcat[64:96, 0, :], bank[4][64:96, :], ACT.Copy).then_inc(sem("kr_copied"), 1)
            act.wait_ge(sem("vg_mm"), 1)
            act.activation(vg_tok[:, :, :], bank[5][:, :].rearrange("p (c n) -> p c n", c=NCH), ACT.Copy).then_inc(sem("vg_copied"), 1)
            rstd_of(QLAT)
            rstd_of(KVLAT)
            for h in range(HEADS):
                act.wait_ge(sem("qh_mm"), h + 1)
                act.activation(qh[0:96, h, :], bank[h % 2][0:96, 0:LAT], ACT.Copy).then_inc(sem("qh_copied"), 1)
            for h in range(HEADS):
                act.wait_ge(sem("kn_mm"), h + 1)
                act.activation(kcat[0:64, h, :], bank[h % 2][0:64, :], ACT.Copy).then_inc(sem("kn_copied"), 1)
            for c in range(NCH):
                act.wait_ge(sem("v_mm"), c + 1)
                act.activation(v_tok[:, c, :], bank[4 + c % 2][:, :], ACT.Copy).then_inc(sem("v_copied"), 1)

            def attention_exp(n):
                act.wait_ge(sem("max_ready"), n + 1)
                if n >= 4:
                    act.wait_ge(sem("pT_mm"), n - 3)
                act.activation(pr[:, n % 4, :], scw[:, n % 2, 0:T], ACT.Exp, bias=stat[:, n % 8, 1:2],
                               accum_out=stat[:, n % 8, 2:3]).then_inc(sem("exp_ready"), 1)
                if n >= 2 * HEADS:
                    act.activation(sinks[:, n % 8:n % 8 + 1], V("sink", n // 2 - HEADS), ACT.Exp,
                                   bias=stat[:, n % 8, 1:2]).then_inc(sem("sink_exp"), 1)

            def attention_pT(n):
                act.wait_ge(sem("pT_mm"), n + 1)
                if n >= 2:
                    act.wait_ge(sem("o_mm"), n - 1)
                act.activation(pT[:, n % 2, :, :], bank[2 + n % 2][:, :].rearrange("p (c n) -> p c n", c=NCH),
                               ACT.Copy).then_inc(sem("pT_ready"), 1)

            for n in range(34):
                if n < 32:
                    attention_exp(n)
                if n >= 2:
                    attention_pT(n - 2)
            copy_and_square(POST1, 16, LAT, lambda j: j % 4,
                            lambda j: product(j, "m_mm", 11 + j // 2 + 1, S_ODOUT + j // 2))
            rstd_of(POST1)
            for k in range(KD):
                act.wait_ge(sem("h_ready"), 16 + k + 1)
                act.activation(aT[:, k, 0:LAT], hT[:, k, CTX:T], ACT.Square).then_inc(sem("square_ready"), 1)
            for dst, name in ((router, "router"), (lower8, "lower8"), (iota, "iota"), (iota_p, "iota_p")):
                act.dma_start(dst, io[name]).then_inc(sem("router_in"), 16)
            rstd_of(FPRE1)
            modulate(1, 1, False)
            act.wait_ge(sem("gv_ready"), 1)
            act.activation(gv[:, :, 1:2], gv[:, :, 0:1], ACT.Exp).then_inc(sem("gv_exp"), 1)
            act.wait_ge(sem("a_tr"), 1)
            for b in range(4):
                act.activation(a_tokm[:, b // 2, (b % 2) * 512:(b % 2 + 1) * 512], bank[4 + b][:, :], ACT.Copy
                               ).then_inc(sem("atok_ready"), 1)

            def silu_tile(e, i, t, rows):
                act.wait_ge(sem("slot_used"), e * E_SLOTS + i * 6 + (N_PRE + gu_slot(t) + 1))
                act.wait_ge(sem("hmoe_done"), e * NFE + i * 4 + (t + 1))
                act.activation(sgm[:, t % 4, 0:rows], bank[t % 4][:, 0:rows], ACT.Silu).then_inc(sem("sgm_ready"), 1)

            def y_row_copies(e):
                act.wait_ge(sem("row_tr"), e + 1)
                for b in range(2):
                    act.activation(y_row[:, 0, b * 512:(b + 1) * 512], bank[4 + b][:, :], ACT.Copy
                                   ).then_inc(sem("y_row_ready"), 1)

            act.wait_ge(sem("moe_start"), 1)
            with act.Fori(0, NEXP) as e:
                mine = act.value_load(tier[0:1, bass.ds(e, 1)], min_val=0, max_val=len(TIERS) - 1)
                for n, rows in enumerate(TIERS):
                    with act.If(mine == n):
                        for b in range(2):
                            act.wait_ge(sem("x_mm"), e * 4 + (b + 1))
                            act.activation(xg[:, 2 * b:2 * b + 2, 0:rows],
                                           bank[b][:, :].rearrange("p (k r) -> p k r", k=2)[:, :, 0:rows], ACT.Copy
                                           ).then_inc(sem("x_ready"), 1)
                        silu_tile(e, 0, 0, rows)
                        silu_tile(e, 0, 1, rows)
                        y_row_copies(e)
                        silu_tile(e, 0, 2, rows)
                        silu_tile(e, 0, 3, rows)
                        with act.Fori(0, NFE // 4 - 1) as i:
                            for t in range(4, 8):
                                silu_tile(e, i, t, rows)
                        act.wait_ge(sem("slot_used"), e * E_SLOTS + (N_PRE + E_SLOTS))
                        for b in range(2):
                            act.activation(y_e[:, 2 * b:2 * b + 2, 0:rows],
                                           bank[4 + b][:, :].rearrange("p (k r) -> p k r", k=2)[:, :, 0:rows], ACT.Copy
                                           ).then_inc(sem("ye_ready"), 1)
            y_row_copies(NEXP)
            for j in range(KD):
                act.wait_ge(sem("acc_done"), 4 * NEXP + j // 2 + 1)
                act.activation(yT[:, j, 0:LAT], acc[:, j, :], ACT.Square).then_inc(sem("square_ready"), 1)
            rstd_of(FPOST1)

        @block.vector
        def _(dve):
            chain = [0]

            def link(ins):
                chain[0] += 1
                ins.then_inc(sem("dve_chain"), 1)
                dve.wait_ge(sem("dve_chain"), chain[0])

            dve.memset(ones[:, :], 1.0)
            dve.memset(zeros[:, :], 0.0)
            link(dve.memset(eps[:, :], EPS))
            dve.wait_ge(sem("small_in"), 16 * len(SMALL))
            for i in range(2):
                dve.wait_ge(sem("filt_mm"), i + 1)
                link(dve.tensor_scalar(hk, bank[i][0:64, 0:256], V(f"f_b{i + 1}", p=64), V("f_freq", p=64), ALU.add, ALU.mult))
                link(dve.tensor_scalar(harg, hk, 1.0 / (2 * np.pi), MAGIC, ALU.mult, ALU.add))
                link(dve.tensor_scalar(harg, harg, MAGIC, None, ALU.subtract))
                link(dve.scalar_tensor_tensor(hk, harg, -TWO_PI_HI, hk, ALU.mult, ALU.add))
                link(dve.scalar_tensor_tensor(hk, harg, -TWO_PI_LO, hk, ALU.mult, ALU.add))
                dve.tensor_scalar(hk, hk, PI_DOWN, -PI_DOWN, ALU.min, ALU.max).then_inc(sem("filt_arg"), 1)
                dve.wait_ge(sem("filt_sin"), i + 1)
            for t in range(2):
                dve.wait_ge(sem("filt_mm"), 3 + t)
                dve.tensor_tensor(prod[:, 0, :], bank[2 + 2 * t][:, :], decay[:, t, :], ALU.mult)
                link(dve.scalar_tensor_tensor(prod[:, 1, :], bank[3 + 2 * t][:, :], V("firstrow", t), decay[:, t, :],
                                              ALU.mult, ALU.mult))
                dve.tensor_tensor(pm[:, 0, t, :], prod[:, 0, :], prod[:, 1, :], ALU.add).then_inc(sem("filt_pm"), 1)
                m = dve.tensor_tensor(pm[:, 1, t, :], prod[:, 0, :], prod[:, 1, :], ALU.subtract)
                m.then_inc(sem("filt_pm"), 1)
                dve.wait_ge(sem("filt_pm"), 2 * t + 2)

            def ada_bias(layer, a, b, src):
                n = b - a
                link(dve.tensor_tensor(mod[:, layer, a:b, :], src[:, 2 * (a - src_off[0]):2 * (b - src_off[0])].rearrange("p (n s) -> p n s", s=2),
                                       bc_last(V(f"ada_b{layer}", a, n), 2),
                                       ALU.add))

            def coef_pre(layer, sub):
                s0 = 8 if sub == 0 else 32
                g = V(("mix_pre", "ffn_pre")[sub] + str(layer), 0, 8)
                return dve.scalar_tensor_tensor(coef[:, layer, 2 * sub, :, :], mod[:, layer, s0:s0 + 8, :], 1.0,
                                                bc_last(g, 2), ALU.add, ALU.mult)

            def coef_post(layer, sub):
                s0 = 16 if sub == 0 else 40
                g = V(("mix_post", "ffn_post")[sub] + str(layer), 0, 8)
                return dve.tensor_tensor(coef[:, layer, 2 * sub + 1, :, :], mod[:, layer, s0:s0 + 8, :], bc_last(g, 2), ALU.mult)

            src_off = [0]
            dve.wait_ge(sem("slot_used"), S_EVIN)
            ada_bias(0, 0, 16, bank[6])
            coef_pre(0, 0).then_inc(sem("mod_ready"), 1)

            def scale_rows(n, src, tok=T):
                dve.wait_ge(sem("rstd_ready"), n + 1)
                for k in range(KD):
                    m = dve.tensor_tensor(aT[:, k, 0:tok], src(k), rstd[:, 0:tok], ALU.mult)
                    m.then_inc(sem("scaled"), 1)
                return m

            hn = [0]

            def residual(n, layer, sub, width, last=False):
                dve.wait_ge(sem("rstd_ready"), n + 1)
                for k in range(KD):
                    link(dve.tensor_tensor(mT[:, k, 0:width], mT[:, k, 0:width], rstd[:, 0:width], ALU.mult))
                    for s in ((0, 1) if width == T else (1,)):
                        cols = SEQ[s]
                        mc = SEQ[s] if width == T else slice(0, LAT)
                        m = dve.scalar_tensor_tensor(hT[:, k, cols], mT[:, k, mc], coef[:, layer, 2 * sub + 1, k, s:s + 1],
                                                     hT[:, k, cols], ALU.mult, ALU.add)
                    m.then_inc(sem("h_ready"), 1)
                    hn[0] += 1
                dve.wait_ge(sem("h_ready"), hn[0])

            scale_rows(PRE0, lambda k: hT[:, k, :])

            for j in range(20):
                dve.wait_ge(sem("conv_mid"), j + 1)
                if j < 12:
                    w0, w2_ = V("hy_w", j), V("hy_w", 24 + j)
                    dst = x0[:, j, :] if j < 4 else (u[:, j - 4, :] if j < 8 else vtmp[:, j - 8, :])
                else:
                    w0, w2_ = V("ssm_w", j - 12), V("ssm_w", 16 + j - 12)
                    dst = conv[:, j - 12, :]
                d3 = dst.rearrange("p (s t) -> p s t", s=2)
                b3 = bank[j % 4][:, :].rearrange("p (s t) -> p s t", s=2)
                link(dve.scalar_tensor_tensor(d3[:, :, 1:256], b3[:, :, 0:255], w0, d3[:, :, 1:256], ALU.mult, ALU.add))
                dve.scalar_tensor_tensor(d3[:, :, 0:255], b3[:, :, 1:256], w2_, d3[:, :, 0:255], ALU.mult, ALU.add
                                         ).then_inc(sem("conv_done"), 1)
                if 8 <= j < 12:
                    dve.wait_ge(sem("conv_done"), j + 1)
                    dve.tensor_tensor(u[:, j - 8, :], u[:, j - 8, :], vtmp[:, j - 8, :], ALU.mult).then_inc(sem("u_ready"), 1)
            dve.wait_ge(sem("dt_mm"), 1)
            link(dve.tensor_tensor(dt_x, bank[4][:, 0:64].rearrange("p (c n) -> p c n", c=4),
                                   bc_mid(V("dt_bias", 0, 16), 4), ALU.add))
            link(dve.tensor_scalar(dt_r, dt_x, 0.0, None, ALU.max))
            dve.scalar_tensor_tensor(sp[:, :, :], dt_r, -2.0, dt_x, ALU.mult, ALU.add).then_inc(sem("sp_ready"), 1)

            for s in range(2):
                for t in range(2):
                    g = 2 * s + t
                    b = 2 * (g % 2)
                    dve.wait_ge(sem("U_mm"), g + 1)
                    if g >= 1:
                        dve.wait_ge(sem("Y_ready"), 2 * g)
                    A, B, Dd = spec[:, t, :], spec[:, 2 + t, :], spec[:, 4, :] if t == 0 else spec[:, 1, :]
                    dve.tensor_tensor(prod[:, 0, :], bank[b][:, :], A, ALU.mult).then_inc(sem("prod_mul"), 1)
                    dve.tensor_tensor(prod[:, 1, :], bank[b + 1][:, :], B, ALU.mult).then_inc(sem("prod_mul"), 1)
                    dve.tensor_tensor(prod[:, 2, :], bank[b][:, :], B, ALU.mult).then_inc(sem("prod_mul"), 1)
                    dve.tensor_tensor(prod[:, 3, :], bank[b + 1][:, :], Dd, ALU.mult).then_inc(sem("prod_mul"), 1)
            for i in range(4):
                dve.wait_ge(sem("iy_mm"), i + 1)
                dve.scalar_tensor_tensor(u[:, i, :], u[:, i, :], V("hy_bias", i), bank[i][:, :], ALU.mult, ALU.add
                                         ).then_inc(sem("iy_read"), 1)
                dve.wait_ge(sem("iy_read"), i + 1)
                dve.tensor_tensor(yT[:, i, :], u[:, i, :], x0[:, i, :], ALU.mult).then_inc(sem("ymix_ready"), 1)

            dve.wait_ge(sem("sp_ln"), 2)
            link(dve.tensor_tensor(dtt[:, :, :], sp[:, :, :], dt_r, ALU.add))
            dve.scalar_tensor_tensor(att[:, :, :], dtt[:, :, :], -1.0, bc_mid(nega, 4), ALU.mult, ALU.mult
                                     ).then_inc(sem("a_tok"), 1)
            dve.wait_ge(sem("cs_mm"), 1)
            link(dve.tensor_copy(CS[:, :, :], bank[0][:, 0:128].rearrange("p (c n) -> p c n", c=4)))
            dve.tensor_scalar(ncs[:, :, :], CS[:, :, 0:16], -1.0, None, ALU.mult).then_inc(sem("cs_ready"), 1)
            dve.tensor_tensor(dec[:, :, :], CS[:, :, 16:32], CS[:, :, 0:16], ALU.subtract).then_inc(sem("dec_arg"), 1)
            for c in range(NCH):
                dve.wait_ge(sem("cb_mm"), c + 1)
                for d in range(2):
                    for g in range(2):
                        dve.tensor_tensor(cb[:, c, d, g, :], bank[1 + c % 2][:, g * P:(g + 1) * P], tri[:, d, :], ALU.mult
                                          ).then_inc(sem("cb_ready"), 1)
            def chunk_state(n):
                c, d = STATE_ORDER[n]
                new = st[:, NEXT[c, d], d, :]
                dve.wait_ge(sem("state_mm"), n + 1)
                if (c, d) in ZERO_STATE:
                    m = dve.tensor_copy(new, bank[3][:, :])
                else:
                    link(dve.tensor_tensor(new.rearrange("p (h e) -> p h e", h=8),
                                           st[:, c, d, :].rearrange("p (h e) -> p h e", h=8),
                                           bc_last(etot[:, c, 8 * d:8 * d + 8], 64), ALU.mult))
                    m = dve.tensor_tensor(new, new, bank[3][:, :], ALU.add)
                m.then_inc(sem("state_ready"), 1)
                dve.wait_ge(sem("state_ready"), n + 1)

            dve.wait_ge(sem("tok_copied"), 8)
            dve.wait_ge(sem("dec_ready"), 2)
            for n, (c, d) in enumerate(XD_ORDER):
                x3 = xs_tok[:, c, :].rearrange("p (h e) -> p h e", h=8)
                o3 = xd[:, c, d, :].rearrange("p (h e) -> p h e", h=8)
                m = dve.tensor_tensor(o3, x3, bc_last(dtt[:, c, 8 * d:8 * d + 8], 64), ALU.mult)
                m.then_inc(sem("xd_ready"), 1)
                if n < 6:
                    dve.wait_ge(sem("xd_ready"), n + 1)
                    if n >= 2:
                        dve.wait_ge(sem("state_mm"), n - 1)
                    dve.tensor_tensor(xdd[:, n % 2, :].rearrange("p (h e) -> p h e", h=8), o3,
                                      bc_last(dec[:, c, 8 * d:8 * d + 8], 64), ALU.mult).then_inc(sem("xdd_ready"), 1)
                if 1 <= n < 7:
                    chunk_state(n - 1)
            def ssd_out(c):
                cols = slice(c * P, (c + 1) * P)
                dve.wait_ge(sem("y_mm"), 2 * c + 2)
                for i in range(4):
                    dve.scalar_tensor_tensor(yT[:, 4 + i, cols], xs[:, i, cols], V("ssm_d", i),
                                             bank[4 + c % 2][:, i * P:(i + 1) * P], ALU.mult, ALU.add
                                             ).then_inc(sem("y_read"), 1)

            for r in range(16):
                c, g, d = r // 4, r // 2 % 2, r % 2
                dve.wait_ge(sem("row_mm"), r + 1)
                dve.wait_ge(sem("row_exp"), r + 1)
                if r >= 2:
                    dve.wait_ge(sem("l_ready"), r - 1)
                for i in range(4):
                    h = 8 * d + 4 * g + i
                    dve.tensor_scalar(dif[:, r % 2, i * P:(i + 1) * P], bank[r % 2][:, i * P:(i + 1) * P],
                                      ncs[:, c, h:h + 1], 0.0, ALU.add, ALU.min).then_inc(sem("row_dif"), 1)
                dve.wait_ge(sem("l_ready"), r + 1)
                if r >= 3:
                    dve.wait_ge(sem("y_mm"), (r - 3) // 2 + 1)
                dve.tensor_tensor(sc[:, r % 3, :].rearrange("p (h q) -> p h q", h=4),
                                  lm[:, r % 2, :].rearrange("p (h q) -> p h q", h=4), bc_mid(cb[:, c, d, g, :], 4), ALU.mult
                                  ).then_inc(sem("sc_ready"), 1)
                if r % 4 == 3 and r >= 7:
                    ssd_out(c - 1)
            ssd_out(3)
            for g in range(2):
                dve.wait_ge(sem("rstd_ready"), SSMG0 + g + 1)
                for k in range(2):
                    i = 2 * g + k
                    m = dve.scalar_tensor_tensor(yT[:, 4 + i, :], yT[:, 4 + i, :], V("norm_g", i), rstd[:, :], ALU.mult, ALU.mult)
                    m.then_inc(sem("ymix_ready"), 1)
            src_off[0] = 16
            dve.wait_ge(sem("slot_used"), S_GU)
            ada_bias(0, 16, 48, bank[6])
            link(coef_post(0, 0))
            link(coef_pre(0, 1))
            coef_post(0, 1).then_inc(sem("mod_ready"), 1)
            dve.wait_ge(sem("mod_ready"), 2)
            residual(POST0, 0, 0, T)
            scale_rows(FPRE0, lambda k: hT[:, k, :])
            dve.memset(mark_[:, 3:4], 0.0).then_inc(sem("hff_done"), 2)
            with dve.Fori(0, NFF // 2) as i:
                for h in range(2):
                    dve.wait_ge(sem("sg_ready"), i * 2 + (h + 1))
                    dve.tensor_tensor(hff[:, i * 2 + h, :], sg[:, h, :], bank[2 * h + 1][:, :], ALU.mult
                                      ).then_inc(sem("hff_done"), 1)
            src_off[0] = 0
            dve.wait_ge(sem("slot_used"), S_DOWN)
            ada_bias(1, 0, 48, bank[6])
            for sub in range(2):
                coef_pre(1, sub)
                m = coef_post(1, sub)
            m.then_inc(sem("mod_ready"), 1)
            dve.wait_ge(sem("mod_ready"), 3)
            residual(FPOST0, 0, 1, T)
            scale_rows(PRE1, lambda k: hT[:, k, :])
            dve.wait_ge(sem("od_copied"), 8)
            dve.wait_ge(sem("rope_mm"), 1)
            rn = [0]

            def rope(dst, swapped, cos, sin, work, done="rope_done"):
                m1 = dve.tensor_tensor(work, swapped, sin, ALU.mult)
                link(m1)
                link(dve.tensor_tensor(dst, dst, cos, ALU.mult))
                dve.tensor_tensor(dst, dst, work, ALU.add).then_inc(sem(done), 1)
                rn[0] += 1

            for j in range(4):
                rope(qg[:, j, :], bank[j // 2][:, (j % 2) * LAT:(j % 2 + 1) * LAT], rope_g[:, 0, :], rope_g[:, 1, :], tmp[:, 0, 0:LAT])
                dve.wait_ge(sem("rope_done"), j + 1)
            dve.wait_ge(sem("rope_mm"), 2)
            rope(kg[:, CTX:T], bank[2][:, 0:LAT], rope_g[:, 0, :], rope_g[:, 1, :], tmp[:, 0, 0:LAT])
            dve.wait_ge(sem("rope_done"), 5)
            dve.wait_ge(sem("rope_mm"), 3)
            rope(kcat[64:96, 0, CTX:T], bank[3][64:96, 0:LAT], rope_m[64:96, 0, :], rope_m[64:96, 1, :], tmp[64:96, 0, 0:LAT])
            dve.wait_ge(sem("rope_done"), 6)
            for h in range(1, HEADS):
                m = dve.tensor_copy(kcat[64:96, h, :], kcat[64:96, 0, :])
            m.then_inc(sem("krope_all"), 1)
            dve.wait_ge(sem("rstd_ready"), QLAT + 1)
            for k in range(2):
                m = dve.scalar_tensor_tensor(qlat[:, k, :], qlat[:, k, :], V("q_norm", k), rstd[:, 0:LAT], ALU.mult, ALU.mult)
                m.then_inc(sem("lat_ready"), 1)
            dve.wait_ge(sem("rstd_ready"), KVLAT + 1)
            m = dve.scalar_tensor_tensor(kvlat, kvlat, V("kv_norm"), rstd[:, :], ALU.mult, ALU.mult)
            m.then_inc(sem("lat_ready"), 1)
            for h in range(HEADS):
                dve.wait_ge(sem("qperm_mm"), h + 1)
                dve.wait_ge(sem("qh_copied"), h + 1)
                rope(qh[64:96, h, :], bank[2 + h % 2][64:96, 0:LAT], rope_m[64:96, 0, :], rope_m[64:96, 1, :],
                     tmp[64:96, 0, 0:LAT], "qrope_done")
                dve.wait_ge(sem("qrope_done"), h + 1)

            def attention_max(n):
                h, qt = n // 2, n % 2
                dve.wait_ge(sem("s_mm"), n + 1)
                if n >= 2:
                    dve.wait_ge(sem("exp_ready"), n - 1)
                s = scw[:, n % 2, :]
                if h < HEADS:
                    dve.tensor_scalar(s[:, 0:T], bank[n % 2][:, :], 96.0 ** -0.5, None, ALU.mult).then_inc(sem("s_read"), 1)
                    dve.wait_ge(sem("s_read"), n + 1)
                    w = T
                else:
                    g = h - HEADS
                    dve.tensor_copy(s[:, T:T + 1], V("sink", g))
                    dve.tensor_scalar(s[:, 0:CTX], bank[n % 2][:, 0:CTX], 0.125, None, ALU.mult)
                    dve.scalar_tensor_tensor(s[:, CTX:T], bank[n % 2][:, CTX:T], 0.125, wmask[:, qt, :], ALU.mult, ALU.add
                                             ).then_inc(sem("s_read"), 1)
                    dve.wait_ge(sem("s_read"), n + 1)
                    w = T + 1
                dve.tensor_reduce(stat[:, n % 8, 1:2], s[:, 0:w], AX_X, ALU.max, negate=True).then_inc(sem("max_ready"), 1)

            def attention_norm(n):
                h = n // 2
                dve.wait_ge(sem("exp_ready"), n + 1)
                if h >= HEADS:
                    dve.wait_ge(sem("sink_exp"), n - 2 * HEADS + 1)
                    link(dve.tensor_tensor(stat[:, n % 8, 2:3], stat[:, n % 8, 2:3], sinks[:, n % 8:n % 8 + 1], ALU.add))
                link(dve.reciprocal(stat[:, n % 8, 3:4], stat[:, n % 8, 2:3]))
                dve.tensor_scalar(pr[:, n % 4, :], pr[:, n % 4, :], stat[:, n % 8, 3:4], None, ALU.mult).then_inc(sem("p_ready"), 1)

            def out_copy(h):
                dve.wait_ge(sem("o_mm"), 2 * h + 2)
                if h < HEADS:
                    p0, j = 64 * (h % 2), h // 2
                else:
                    p0, j = 64 * ((h - HEADS) // 4), 4 + (h - HEADS) % 4
                dve.tensor_copy(yT[p0:p0 + 64, j, 0:LAT], bank[4 + h % 2][p0:p0 + 64, 0:LAT]).then_inc(sem("o_copied"), 1)

            for n in range(36):
                if n < 32:
                    attention_max(n)
                if 1 <= n < 33:
                    attention_norm(n - 1)
                if n >= 4 and n % 2 == 0 and (n - 4) // 2 < 16:
                    out_copy((n - 4) // 2)
            residual(POST1, 1, 0, LAT)
            scale_rows(FPRE1, lambda k: hT[:, k, CTX:T], LAT)
            dve.wait_ge(sem("router_in"), 64)
            dve.wait_ge(sem("router_mm"), 1)
            link(dve.tensor_copy(lg[:, :, :], bank[0][:, 0:16].rearrange("p (c n) -> p c n", c=2)))
            for c in range(2):
                r3 = [rt[:, c, x, :].rearrange("p (a b) -> p a b", a=8) for x in range(2)]
                mine = bc_last(lg[:, c, :], 8)
                other = bc_mid(lg[:, c, :], 8)
                dve.tensor_tensor(r3[0], other, mine, ALU.is_gt)
                link(dve.tensor_tensor(r3[1], other, mine, ALU.is_equal))
                link(dve.tensor_tensor(r3[1], r3[1], lower8, ALU.mult))
                link(dve.tensor_tensor(r3[0], r3[0], r3[1], ALU.add))
                link(dve.tensor_reduce(rank[:, c, :], r3[0], AX_X, ALU.add))
                for x in range(2):
                    link(dve.tensor_scalar(sel[:, c, x, :], rank[:, c, :], float(x), None, ALU.is_equal))
                    link(dve.tensor_tensor(mval[:, c, :], sel[:, c, x, :], lg[:, c, :], ALU.mult))
                    link(dve.tensor_reduce(gv[:, c, 2 + x:3 + x], mval[:, c, :], AX_X, ALU.add))
            dve.tensor_tensor(gv[:, :, 0:1], gv[:, :, 3:4], gv[:, :, 2:3], ALU.subtract).then_inc(sem("gv_ready"), 1)
            dve.wait_ge(sem("gv_exp"), 1)
            link(dve.tensor_scalar(gv[:, :, 4:5], gv[:, :, 1:2], 1.0, None, ALU.add))
            link(dve.reciprocal(gv[:, :, 5:6], gv[:, :, 4:5]))
            link(dve.tensor_tensor(gv[:, :, 6:7], gv[:, :, 5:6], gv[:, :, 1:2], ALU.mult))
            for c in range(2):
                link(dve.tensor_scalar(gates[:, c, :], sel[:, c, 1, :], gv[:, c, 6:7], None, ALU.mult))
                m = dve.scalar_tensor_tensor(gates[:, c, :], sel[:, c, 0, :], gv[:, c, 5:6], gates[:, c, :], ALU.mult, ALU.add)
            m.then_inc(sem("gates_ready"), 1)
            link(dve.memset(key[:, :, NEXP:NEXP + 1], -1.0))
            dve.tensor_tensor(seltok[:, :, :], sel[:, :, 0, :], sel[:, :, 1, :], ALU.add).then_inc(sem("sel_ready"), 1)
            dve.wait_ge(sem("pos_mm"), 1)
            link(dve.tensor_tensor(key[:, :, 0:NEXP], bank[1][:, 0:16].rearrange("p (c n) -> p c n", c=2), seltok[:, :, :], ALU.mult))
            for n in range(3):
                m = dve.tensor_scalar(tier_f[:, n, :], bank[1][:, 16:24], float(TIERS[n]), None, ALU.is_gt)
            link(m)
            dve.tensor_scalar(key[:, :, 0:NEXP], key[:, :, 0:NEXP], -1.0, None, ALU.add).then_inc(sem("key_ready"), 1)
            link(dve.tensor_tensor(tier_f[:, 0, :], tier_f[:, 0, :], tier_f[:, 1, :], ALU.add))
            link(dve.tensor_tensor(tier_f[:, 0, :], tier_f[:, 0, :], tier_f[:, 2, :], ALU.add))
            link(dve.tensor_copy(tier[:, :], tier_f[:, 0, :]))
            for x, what in enumerate((gbc, krow)):
                dve.wait_ge(sem("gbc_mm"), x + 1)
                for b in range(4):
                    dve.tensor_copy(what[:, 2 * b:2 * b + 2, :], bank[b][:, :].rearrange("p (e t) -> p e t", e=2)
                                    ).then_inc(sem("gbc_ready"), 1)
            dve.wait_ge(sem("gbc_ready"), 8)

            def make_perm(e):
                for c in range(2):
                    m = dve.tensor_scalar(perm[:, c, :], iota, key[:, c, bass.ds(e, 1)], None, ALU.is_equal)
                m.then_inc(sem("perm_ready"), 1)

            dve.memset(acc, 0.0)
            dve.memset(spread[:, :, :], 0.0).then_inc(sem("spread_ready"), 1)
            link(dve.memset(y_e[:, :, :], 0.0))
            dve.memset(mark_[:, 0:1], 0.0).then_inc(sem("ye_ready"), 4)
            dve.memset(mark_[:, 1:2], 0.0).then_inc(sem("hmoe_done"), 4)
            dve.wait_ge(sem("atok_ready"), 4)
            for c in range(2):
                m = dve.tensor_scalar(perm[:, c, :], iota, key[:, c, 0:1], None, ALU.is_equal)
            m.then_inc(sem("perm_ready"), 1)
            dve.memset(mark_[:, 2:3], 0.0).then_inc(sem("moe_start"), 1)

            def hidden_tile(e, i, t, rows):
                dve.wait_ge(sem("sgm_ready"), e * NFE + i * 4 + (t + 1))
                dve.wait_ge(sem("slot_used"), e * E_SLOTS + i * 6 + (N_PRE + 3 * (t // 2) - 1))
                dve.tensor_tensor(hmoe[:, t % 4, 0:rows], sgm[:, t % 4, 0:rows], bank[t % 4][:, LAT:LAT + rows], ALU.mult
                                  ).then_inc(sem("hmoe_done"), 1)

            def y_row_copies(e):
                dve.wait_ge(sem("row_tr"), e + 1)
                for b in range(2):
                    dve.tensor_copy(y_row[:, 1, b * 512:(b + 1) * 512], bank[6 + b][:, :]).then_inc(sem("y_row_ready"), 1)

            def accumulate(e):
                dve.wait_ge(sem("scatter_mm"), e + 1)
                for b in range(4):
                    dve.tensor_tensor(acc[:, 2 * b:2 * b + 2, :], acc[:, 2 * b:2 * b + 2, :],
                                      bank[4 + b][:, :].rearrange("p (k t) -> p k t", k=2), ALU.add).then_inc(sem("acc_done"), 1)

            dve.wait_ge(sem("moe_start"), 1)
            with dve.Fori(0, NEXP) as e:
                mine = dve.value_load(tier[0:1, bass.ds(e, 1)], min_val=0, max_val=len(TIERS) - 1)
                for n, rows in enumerate(TIERS):
                    with dve.If(mine == n):
                        for b in range(2, 4):
                            dve.wait_ge(sem("x_mm"), e * 4 + (b + 1))
                            dve.tensor_copy(xg[:, 2 * b:2 * b + 2, 0:rows],
                                            bank[b][:, :].rearrange("p (k r) -> p k r", k=2)[:, :, 0:rows]
                                            ).then_inc(sem("x_ready"), 1)
                        hidden_tile(e, 0, 0, rows)
                        hidden_tile(e, 0, 1, rows)
                        y_row_copies(e)
                        hidden_tile(e, 0, 2, rows)
                        hidden_tile(e, 0, 3, rows)
                        accumulate(e)
                        with dve.Fori(0, NFE // 4 - 1) as i:
                            for t in range(4, 8):
                                hidden_tile(e, i, t, rows)
                        for b in range(2):
                            m = dve.scalar_tensor_tensor(spread[:, b, :], krow[:, e, :], iota_p[:, b:b + 1], gbc[:, e, :],
                                                         ALU.is_equal, ALU.mult)
                        m.then_inc(sem("spread_ready"), 1)
                        make_perm(e + 1)
                        dve.wait_ge(sem("slot_used"), e * E_SLOTS + (N_PRE + E_SLOTS))
                        for b in range(2, 4):
                            dve.tensor_copy(y_e[:, 2 * b:2 * b + 2, 0:rows],
                                            bank[4 + b][:, :].rearrange("p (k r) -> p k r", k=2)[:, :, 0:rows]
                                            ).then_inc(sem("ye_ready"), 1)
            y_row_copies(NEXP)
            accumulate(NEXP)
            dve.wait_ge(sem("acc_done"), 4 * NEXP + 4)
            residual(FPOST1, 1, 1, LAT)

        @block.gpsimd
        def _(pool):
            for s in range(2):
                for t in range(2):
                    g = 2 * s + t
                    pool.wait_ge(sem("prod_mul"), 4 * g + 2)
                    pool.tensor_tensor(Y[:, t, s, :], prod[:, 0, :], prod[:, 1, :], ALU.subtract).then_inc(sem("Y_ready"), 1)
                    pool.wait_ge(sem("prod_mul"), 4 * g + 4)
                    pool.tensor_tensor(Y[:, 2 + t, s, :], prod[:, 2, :], prod[:, 3, :], ALU.add).then_inc(sem("Y_ready"), 1)
            for r in range(16):
                c, g, d = r // 4, r // 2 % 2, r % 2
                pool.wait_ge(sem("row_exp"), r + 1)
                if r >= 3:
                    pool.wait_ge(sem("y_mm"), (r - 3) // 2 + 1)
                pool.tensor_tensor(ce[:, r % 3, :].rearrange("p (h q) -> p h q", h=4),
                                   er[:, r % 2, :].rearrange("p (h q) -> p h q", h=4),
                                   bc_mid(cT[:, g, c * P:(c + 1) * P], 4), ALU.mult).then_inc(sem("ce_ready"), 1)
            for c in range(NCH):
                cols = slice(c * P, (c + 1) * P)
                pool.wait_ge(sem("y_read"), 4 * (c + 1))
                pool.tensor_tensor(yT[:, 4:8, cols], yT[:, 4:8, cols], z[:, :, cols], ALU.mult).then_inc(sem("y_gated"), 1)


def units(w, tiles):
    return w.reshape(KD, P, tiles, P).transpose(2, 1, 0, 3).reshape(tiles, P, UNIT)


def feature_tiles(v):
    return np.ascontiguousarray(v.reshape(-1, P).T)


def shape_constants():
    n, c = LAT, {}
    pos = np.arange(n, dtype=np.float32)
    t = (pos / np.float32(n - 1)).astype(np.float32)
    omega = (np.float32(2.0 * np.pi) * pos / np.float32(n)).astype(np.float32)
    bands = np.linspace(1e-4, 15, 16).astype(np.float32)
    arg = (omega[:, None] * bands).astype(np.float32)
    c["zT"] = np.concatenate([t[:, None], np.cos(arg), -np.sin(arg)], axis=-1).T.astype(np.float32)
    deltas = np.abs(np.linspace(np.log(1e-2) / 1.5, np.log(1e-2) / 0.3, 512).astype(np.float32))
    c["decay"] = np.exp(-t[:, None] * deltas[None, :]).astype(np.float32).reshape(2, P, 512).transpose(1, 0, 2)
    k = np.arange(256)[:, None].astype(np.float64)
    f = np.arange(256)[None, :]
    cos, sin = np.cos(2 * np.pi * k * f / 512), -np.sin(2 * np.pi * k * f / 512)
    nyq = np.cos(np.pi * k[:, 0])
    imag = sin.copy()
    imag[:, 0] = nyq
    two = lambda a: a.reshape(2, P, -1).transpose(1, 0, 2)
    c["dft"] = two(np.concatenate([cos, imag], 1))
    c["dftB"] = two(sin[:, :P])
    d0 = cos[:, :P].copy()
    d0[:, 0] = nyq
    c["dftD"] = two(d0)
    icos, isin = 2 * cos.T / 512, 2 * sin.T / 512
    icos[0] /= 2
    isin[0] = nyq / 512
    c["idft"] = np.concatenate([icos, isin], 0).reshape(4, P, 256).transpose(1, 0, 2)
    c["ident"] = np.eye(P)
    i = np.arange(P)
    c["tri"] = np.stack([i[:, None] <= i[None, :], i[:, None] >= i[None, :]], 1)
    rows = np.repeat(np.arange(n // GRID_W), GRID_W).astype(np.float32)
    cols = np.tile(np.arange(GRID_W), n // GRID_W).astype(np.float32)

    def rope(dim):
        nf = dim // 4
        inv = (10000.0 ** (-np.arange(nf, dtype=np.float32) / nf)).astype(np.float32)
        ang = np.concatenate([rows[:, None] * inv, cols[:, None] * inv], -1).astype(np.float32).T
        ang = np.concatenate([ang, ang], 0)
        return np.stack([np.cos(ang), np.sin(ang)], 1)

    def swap(dim):
        half = dim // 2
        r = np.zeros((dim, dim))
        r[np.arange(half) + half, np.arange(half)] = -1
        r[np.arange(half), np.arange(half) + half] = 1
        return r

    g = rope(64)
    c["rope_g"] = np.concatenate([g, g], 0)
    m = np.zeros((P, 2, n))
    m[64:96] = rope(32)
    c["rope_m"] = m
    pg = np.zeros((P, P))
    pg[:64, :64] = pg[64:, 64:] = swap(64)
    c["perm_g"] = pg
    pm = np.zeros((P, P))
    pm[64:96, 64:96] = swap(32)
    c["perm_m"] = pm
    q = np.arange(n)
    band = np.where(np.abs(q[:, None] - q[None, :]) <= 128, 0.0, -1e30)
    c["wmask"] = band.reshape(2, P, n).transpose(1, 0, 2)
    e = np.arange(8)
    c["lower8"] = np.broadcast_to((e[None, :] < e[:, None])[None], (P, 8, 8))
    c["iota"] = np.broadcast_to(np.arange(n)[None], (P, n))
    c["iota_p"] = np.arange(P)[:, None] + P * np.arange(2)[None]
    return {k: np.ascontiguousarray(v, np.float32) for k, v in c.items()}


def layout(I):
    f = lambda name: np.asarray(I[name])
    a = shape_constants()
    tokens = np.concatenate([f("ctx")[0], f("x")[0]], 0)
    a["xT"] = tokens.T.reshape(KD, P, T).transpose(1, 0, 2)
    a["cond"] = np.stack([f("c_ctx"), f("c")[0]], 1).reshape(KD, P, 2).transpose(1, 0, 2)
    v = np.zeros((P, NVEC), np.float32)

    def put(name, x):
        at, w = VEC[name]
        v[:x.shape[0], at:at + w] = x

    for l in range(2):
        put(f"ada_b{l}", feature_tiles(f("ada_b")[l]))
        for n in ("mix_pre", "mix_post", "ffn_pre", "ffn_post"):
            put(f"{n}{l}", feature_tiles(f(f"{n}_g")[l]))
    put("hy_w", feature_tiles(f("ev_hy_conv_w")[0]))
    put("hy_b", feature_tiles(f("ev_hy_conv_b")[0]))
    put("hy_bias", feature_tiles(f("ev_hy_bias")[0]))
    put("ssm_w", feature_tiles(f("ev_ssm_conv_w")[0]))
    put("ssm_b", feature_tiles(f("ev_ssm_conv_b")[0]))
    put("ssm_d", feature_tiles(np.repeat(f("ev_ssm_d")[0], 64)))
    put("norm_g", feature_tiles(f("ev_ssm_norm_g")[0]))
    put("q_norm", feature_tiles(f("od_mla_q_norm_g")[0]))
    put("kv_norm", feature_tiles(f("od_mla_kv_norm_g")[0]))
    put("dt_bias", np.broadcast_to(f("ev_ssm_dt_bias").reshape(1, 16), (P, 16)))
    put("a_log", np.broadcast_to(f("ev_ssm_a_log").reshape(1, 16), (P, 16)))
    put("sink", np.broadcast_to(f("od_gqa_sink").reshape(1, 8), (P, 8)))
    put("f_b1", f("ev_hy_filt_b1")[0][:, None])
    put("f_b2", f("ev_hy_filt_b2")[0][:, None])
    put("f_freq", f("ev_hy_freq")[0][:, None])
    fr = np.ones((P, 2), np.float32)
    fr[0, 0] = 0
    put("firstrow", fr)
    a["vec"] = v
    a["w1"], a["w2"], a["w3"] = f("ev_hy_filt_w1")[0], f("ev_hy_filt_w2")[0], f("ev_hy_filt_w3")[0]
    ev = f("ev_w_in")[0]
    kt = lambda w: w.reshape(-1, P, w.shape[-1]).transpose(1, 0, 2)
    a["w_dt"] = kt(ev[:, 3072:3088])
    evin = units(np.concatenate([ev[:, 0:1536], ev[:, 2048:3072], ev[:, 1536:2048]], 1), 24)
    ada = [units(f("ada_w")[l], 48) for l in range(2)]
    evout = units(f("ev_w_out")[0], 8)
    gate, up = units(f("ev_ffn_w_gate")[0], NFF), units(f("ev_ffn_w_up")[0], NFF)
    down = f("ev_ffn_w_down")[0].reshape(NFF, P, UNIT)
    od = f("od_w_in")[0]
    q_lat, kv_lat, k_rope, q_g, k_g, v_g = np.split(od, [256, 384, 416, 928, 1056], 1)
    heads = [x for p in range(4) for x in (p, p + 4)]
    q_g = q_g.reshape(D, 8, 64)[:, heads].reshape(D, 512)
    odin = units(np.concatenate([q_lat, kv_lat, q_g, k_g], 1), 8)
    wo = f("od_w_out")[0].copy()
    wo[512:] = wo[512:].reshape(8, 64, D)[heads].reshape(512, D)
    odout = units(wo, 8)
    slots = []
    pair = lambda x, s: [x[2 * s], x[2 * s + 1]]
    for s in range(N_ADA_A):
        slots.append(pair(ada[0], s))
    for s in range(N_EVIN):
        slots += [pair(evin, s), pair(ada[0], N_ADA_A + s)]
    for s in range(N_EVOUT):
        slots += [pair(evout, s), pair(ada[0], N_ADA_A + N_EVIN + s)]
    for j in range(NFF):
        slots += [[gate[j], up[j]], pair(ada[1], j)]
    for s in range(N_ADA_C):
        slots.append(pair(ada[1], NFF + s))
    slots += [pair(down, s) for s in range(N_DOWN)]
    slots += [pair(odin, s) for s in range(N_ODIN)]
    slots += [pair(odout, s) for s in range(N_ODOUT)]
    assert len(slots) == N_PRE
    pre = np.empty((N_PRE, P, 2, UNIT), np.float32)
    for i, (x, y) in enumerate(slots):
        pre[i, :, 0], pre[i, :, 1] = x, y
    a["pre"] = pre.reshape(N_PRE, P, 2 * UNIT)
    a["w_krv"] = kt(np.concatenate([k_rope, v_g], 1))
    a["q_up"] = kt(f("od_mla_w_q_up")[0])
    kvu = f("od_mla_w_kv_up")[0].reshape(P, HEADS, 2, 64)
    a["kv_up"] = kvu.transpose(0, 2, 1, 3).reshape(P, 1024)
    a["router"] = kt(f("od_router")[0])
    moe = np.empty((NEXP, E_SLOTS, P, 2, UNIT), np.float32)
    for e in range(NEXP):
        g, u_ = units(f("od_moe_w_gate")[0, e], NFE), units(f("od_moe_w_up")[0, e], NFE)
        d = f("od_moe_w_down")[0, e].reshape(NFE, P, UNIT)
        for t in range(NFE):
            moe[e, gu_slot(t), :, 0], moe[e, gu_slot(t), :, 1] = g[t], u_[t]
            moe[e, min(3 * (t // 2) + 4, E_SLOTS - 1), :, t % 2] = d[t]
    a["moe"] = moe.reshape(N_MOE, P, 2 * UNIT)
    return {k: np.ascontiguousarray(x) for k, x in a.items()}


def kernel(**inputs):
    import concourse.bacc as bacc
    from concourse.bass_utils import run_bass_kernel_spmd

    arrays = layout(inputs)
    nc = bacc.Bacc("TRN2", target_bir_lowering=False, num_devices=1)
    io = {k: nc.dram_tensor(f"in_{k}", v.shape, F32, kind="ExternalInput").ap() for k, v in arrays.items()}
    io["out"] = nc.dram_tensor("out_T", (P, KD, LAT), F32, kind="ExternalOutput").ap()
    build(nc, io)
    r = run_bass_kernel_spmd(nc, [{f"in_{k}": v for k, v in arrays.items()}], core_ids=[0])
    out = np.asarray(r.results[0]["out_T"])
    return out.transpose(2, 1, 0).reshape(1, LAT, D)
```

```python
from contextlib import ExitStack

import numpy as np

import concourse.bass as bass
from concourse import mybir

ALU = mybir.AluOpType
ACT = mybir.ActivationFunctionType
F32 = mybir.dt.float32
I32 = mybir.dt.int32
F32R = mybir.dt.float32r
AX_X = mybir.AxisListType.X

P = 128
D = 1024
KD = D // P
CTX = 256
LAT = 256
T = CTX + LAT
NCH = T // P
GW = D // 2
FF = 2816
NFF = FF // P
NEXP = 8
FFE = 3584
NFE = FFE // P
HEADS = 8
EPS = 1e-6
GRID_W = 64
UNIT = 1024
SLOTS = 6

N_ADA_A = 8
N_EVIN = 12
N_EVOUT = 4
N_GU = NFF
N_ADA_C = 2
N_DOWN = NFF // 2
N_ODIN = 4
N_ODOUT = 4
S_EVIN = N_ADA_A
S_EVOUT = S_EVIN + 2 * N_EVIN
S_GU = S_EVOUT + 2 * N_EVOUT
S_ADAC = S_GU + 2 * N_GU
S_DOWN = S_ADAC + N_ADA_C
S_ODIN = S_DOWN + N_DOWN
S_ODOUT = S_ODIN + N_ODIN
N_PRE = S_ODOUT + N_ODOUT
GROUPS = NFE // 4
E_SLOTS = 6 * GROUPS
N_MOE = NEXP * E_SLOTS

VEC = {}
_n = 0
for _name, _w in [("ada_b0", 48), ("ada_b1", 48), ("mix_pre0", 8), ("mix_pre1", 8), ("mix_post0", 8), ("mix_post1", 8),
                  ("ffn_pre0", 8), ("ffn_pre1", 8), ("ffn_post0", 8), ("ffn_post1", 8), ("hy_w", 36), ("hy_b", 12),
                  ("hy_bias", 4), ("ssm_w", 24), ("ssm_b", 8), ("ssm_d", 4), ("norm_g", 4), ("q_norm", 2),
                  ("kv_norm", 1), ("dt_bias", 16), ("a_log", 16), ("sink", 8), ("f_b1", 1), ("f_b2", 1),
                  ("f_freq", 1), ("firstrow", 2)]:
    VEC[_name] = (_n, _w)
    _n += _w
NVEC = _n

NORMS = [(8, D, T), (2, 256, T), (2, 256, T), (8, D, T), (8, D, T), (8, D, T),
         (8, D, T), (2, 256, LAT), (1, 128, T), (8, D, LAT), (8, D, LAT), (8, D, LAT)]
(PRE0, SSMG0, SSMG1, POST0, FPRE0, FPOST0, PRE1, QLAT, KVLAT, POST1, FPRE1, FPOST1) = range(12)


RSTD_USED = [("scaled", 8), ("ymix_ready", 6), ("ymix_ready", 8), ("h_ready", 8), ("scaled", 16), ("h_ready", 16),
             ("scaled", 24), ("lat_ready", 2), ("lat_ready", 3), ("h_ready", 24), ("scaled", 32)]
STATE_ORDER = [(0, 0), (1, 1), (1, 0), (0, 1), (2, 0), (3, 1)]
XD_ORDER = STATE_ORDER + [(3, 0), (2, 1)]
NEXT = {(0, 0): 1, (1, 0): 2, (2, 0): 3, (1, 1): 0, (0, 1): 3, (3, 1): 2}
ZERO_STATE = [(0, 0), (1, 1)]
MAGIC = 12582912.0
TWO_PI_HI, TWO_PI_LO = 6.28125, 0.0019353071795864769
PI_DOWN = 3.1415925


def bc_last(ap, n):
    if len(ap.shape) == 3:
        ap = ap.rearrange("p a b -> p (a b)")
    return ap.unsqueeze(2).to_broadcast([ap.shape[0], ap.shape[1], n])


def bc_mid(ap, n):
    return ap.unsqueeze(1).to_broadcast([ap.shape[0], n, ap.shape[1]])


def gate_slot(g):
    return 0 if g == 0 else 6 * g - 2


def down_slot(g):
    return 6 * g + 8 if g < GROUPS - 1 else E_SLOTS - 2


def squares_before(n):
    return sum(t for t, _, _ in NORMS[:n])


def build(nc, io):
    ctx = ExitStack()
    with ctx:
        def sb(name, shape, dt=F32):
            return ctx.enter_context(nc.sbuf_tensor(name, shape, dt))

        sems = {}

        def sem(name):
            if name not in sems:
                sems[name] = ctx.enter_context(nc.semaphore(name))
            return sems[name]

        bank = [ctx.enter_context(nc.psum_tensor(f"bank{i}", [P, 512], F32)) for i in range(8)]

        ring = sb("ring", [P, SLOTS, 2 * UNIT])
        hT = sb("hT", [P, KD, T])
        aT = sb("aT", [P, KD, T])
        mT = sb("mT", [P, KD, T])
        yT = sb("yT", [P, KD, T])
        vec = sb("vec", [P, NVEC])
        ident = sb("ident", [P, P])
        ones = sb("ones", [P, P])
        tri = sb("tri", [P, 2, P])
        cond = sb("cond", [P, KD, 2])
        cond_e = sb("cond_e", [P, KD, 2])
        mod = sb("mod", [P, 2, 48, 2])
        coef = sb("coef", [P, 2, 4, KD, 2])
        rstd = sb("rstd", [P, T])
        lnv = sb("lnv", [P, T])
        tmp = sb("tmp", [P, 2, T])
        eps = sb("eps", [P, 1])
        mark_ = sb("mark_", [P, 4])
        zeros = sb("zeros", [P, 512])
        ARENA = 20100
        arena_at = nc.sbuf_base
        arena = sb("arena", [P, ARENA])

        carved = [0]

        def carve(*shape):
            n = int(np.prod(shape))
            v = arena[:, carved[0]:carved[0] + n]
            carved[0] += n
            assert carved[0] <= ARENA, carved[0]
            if len(shape) == 1:
                return v
            names = "abcd"[:len(shape)]
            spec = " ".join(names)
            return v.rearrange(f"p ({spec}) -> p {spec}", **{k: s for k, s in zip(names, shape)})

        x0 = carve(4, T)
        u = carve(4, T)
        conv = carve(8, T)
        z = carve(4, T)
        xs, bT, cT = conv[:, 0:4, :], conv[:, 4:6, :], conv[:, 6:8, :]
        mark = carved[0]
        dft = carve(2, 512)
        dftB = carve(2, P)
        dftD = carve(2, P)
        idft = carve(4, 256)
        spec = carve(5, 512)
        u_tok = yT[:, 4:8, :]
        pm = carve(2, 2, 512)
        prod = carve(4, 512)
        filt_small = mT[:, 6:8, :].rearrange("p a b -> p (a b)")
        Y = mT[:, :, :].rearrange("p (f s) c -> p f s c", f=4)
        decay = mT[:, 0:2, :]
        w3 = mT[:, 2:4, :].rearrange("p a b -> p (a b)")[0:64, :]
        zT = filt_small[0:33, 0:256]
        w1 = filt_small[0:33, 256:320]
        w2 = filt_small[0:64, 320:384]
        hid = [filt_small[0:64, 384 + 256 * i:640 + 256 * i] for i in range(2)]
        hk = mT[0:64, 4, 0:256]
        harg = mT[0:64, 5, 0:256]
        vtmp = yT[:, 0:4, :]
        carved[0] = mark
        xs_tok = carve(4, 512)
        b_tok = carve(4, 256)
        cb = carve(4, 2, 2, P)
        CS = carve(NCH, 32)
        ncs = carve(4, 16)
        dec = carve(4, 16)
        etot = carve(4, 16)
        dt_x, dt_r, sp, dtt, att = (tmp[:, 1, 64 * i:64 * (i + 1)].rearrange("p (c n) -> p c n", c=NCH)
                                    for i in range(5))
        xd = aT[:, :, :].rearrange("p (c e) f -> p c e f", c=4)
        xdd = x0[:, 0:2, :]
        st = mT[:, :, :].rearrange("p (c e) f -> p c e f", c=4)
        dif = u[:, 0:2, :]
        lm = u[:, 2:4, :]
        er = carve(2, 512)
        sc = carve(3, 512)
        ce = carve(3, 512)
        w_dt = tmp[:, 0, 0:P].rearrange("p (k n) -> p k n", k=KD)
        nega = tmp[:, 0, P:P + 16]
        ssd_end = carved[0]
        carved[0] = 0
        hff = carve(NFF, T)
        sg = carve(2, T)
        carved[0] = 0
        qlat = carve(2, LAT)
        kvlat = carve(T)
        qh = carve(HEADS, LAT)
        kcat = carve(HEADS, T)
        v_tok = carve(NCH, 512)
        qg = carve(4, LAT)
        kg = carve(T)
        vg_tok = carve(NCH, P)
        w_krv = carve(KD, 160)
        q_up = carve(2, 768)
        kv_up = carve(1024)
        rope_g = carve(2, LAT)
        rope_m = carve(2, LAT)
        perm_g = carve(P)
        perm_m = carve(P)
        wmask = carve(2, LAT)
        pr = mT[:, 0:4, :]
        scr = mT[:, 4:6, :]
        scw = carve(2, T + 1)
        pT = carve(2, NCH, P)
        stat = carve(8, 4)
        sinks = carve(8)
        carved[0] = 0
        router = carve(KD, NEXP)
        lower8 = carve(NEXP, NEXP)
        rt = carve(2, 2, 64)
        lg = carve(2, 8)
        rank = carve(2, 8)
        sel = carve(2, 2, 8)
        mval = carve(2, 8)
        gates = carve(2, 8)
        gv = carve(2, 8)
        seltok = carve(2, 8)
        key = carve(2, NEXP + 1)
        two = carve(NEXP).bitcast(I32)
        two_f = carve(NEXP)
        iota = carve(LAT)
        iota_p = carve(2)
        krow = mT[:, :, LAT:T]
        gbc = hT[:, :, 0:CTX]
        acc = mT[:, :, 0:LAT]
        a_tokm = yT[:, 0:4, :].rearrange("p (c k) t -> p c (k t)", c=2)
        y_row = yT[:, 4:8, :].rearrange("p (c k) t -> p c (k t)", c=2)
        sg2 = aT[:, 0:2, :]
        h2 = aT[:, 2:4, :]
        perm = aT[:, 4, :].rearrange("p (c r) -> p c r", c=2)
        spread = aT[:, 5, :].rearrange("p (c r) -> p c r", c=2)
        at = arena_at + 4 * (-(-carved[0] // 16) * 16)

        def split_at(name, shape):
            nonlocal at
            t = nc.alloc_sbuf_tensor_at(name, [P] + shape, F32R, offset=at)
            at += 4 * int(np.prod(shape))
            assert at <= arena_at + 4 * ARENA
            return t

        w_hi, w_lo = split_at("w_hi", [4, UNIT]), split_at("w_lo", [4, UNIT])
        x_hi, x_lo = split_at("x_hi", [KD, LAT]), split_at("x_lo", [KD, LAT])
        h_hi, h_lo = split_at("h_hi", [2, 4, LAT]), split_at("h_lo", [2, 4, LAT])

        def V(name, i=0, n=1, p=P):
            at, w = VEC[name]
            return vec[0:p, at + i:at + i + n]

        SEQ = [slice(0, CTX), slice(CTX, T)]

        def norm_cols(n):
            return slice(0, T) if NORMS[n][2] == T else slice(0, LAT)

        def slot_tile(s, unit, k):
            return ring[:, s % SLOTS, unit * UNIT + k * P:unit * UNIT + (k + 1) * P]

        SMALL = [(vec[:, :], "vec"), (cond[:, :, :], "cond"), (zT, "zT"), (w1, "w1"), (w2, "w2"), (w3, "w3"),
                 (hT[:, :, :], "xT"), (ident[:, :], "ident"), (tri[:, :, :], "tri"), (decay, "decay"), (dft, "dft"),
                 (dftB, "dftB"), (dftD, "dftD"), (idft, "idft"), (w_dt, "w_dt")]
        OD_SMALL = [(w_krv, "w_krv"), (q_up, "q_up"), (kv_up, "kv_up"), (rope_g, "rope_g"), (rope_m, "rope_m"),
                    (perm_g, "perm_g"), (perm_m, "perm_m"), (wmask, "wmask")]
        block = ctx.enter_context(nc.Block())

        @block.sync
        def _(sp_):
            for s in range(SLOTS):
                sp_.dma_start(ring[:, s, :], io["pre"][s]).then_inc(sem(f"slot{s}_in"), 16)
            rounds = (N_PRE - SLOTS) // SLOTS
            with sp_.Fori(0, rounds) as i:
                for s in range(SLOTS):
                    sp_.wait_ge(sem("slot_used"), i * SLOTS + (s + 1))
                    sp_.dma_start(ring[:, s, :], io["pre"][i * SLOTS + (SLOTS + s)]).then_inc(sem(f"slot{s}_in"), 16)
            for n in range(SLOTS * (rounds + 1), N_PRE):
                sp_.wait_ge(sem("slot_used"), n - SLOTS + 1)
                sp_.dma_start(ring[:, n % SLOTS, :], io["pre"][n]).then_inc(sem(f"slot{n % SLOTS}_in"), 16)
            for s in range(SLOTS):
                sp_.wait_ge(sem("slot_used"), N_PRE + s - SLOTS + 1)
                sp_.dma_start(ring[:, (N_PRE + s) % SLOTS, :], io["moe"][s]).then_inc(
                    sem(f"slot{(N_PRE + s) % SLOTS}_in"), 16)
            with sp_.Fori(0, N_MOE // SLOTS - 1) as i:
                for s in range(SLOTS):
                    sp_.wait_ge(sem("w_split"), i * (2 * SLOTS) + (2 * s + 2))
                    sp_.dma_start(ring[:, (N_PRE + s) % SLOTS, :], io["moe"][i * SLOTS + (SLOTS + s)]).then_inc(
                        sem(f"slot{(N_PRE + s) % SLOTS}_in"), 16)
            for k in range(2):
                sp_.wait_ge(sem("h_ready"), 28 + 4 * k)
                sp_.dma_start(io["out"][:, 4 * k:4 * k + 4, :], hT[:, 4 * k:4 * k + 4, CTX:T]).then_inc(sem("stored"), 16)
            sp_.wait_ge(sem("stored"), 32)

        @block.tensor
        def _(pe):
            def slot_wait(s, base=0):
                pe.wait_ge(sem(f"slot{s % SLOTS}_in"), base * 16 + 16 * (s // SLOTS + 1))

            def ada_slot(s, dst, j, rounds=0):
                slot_wait(s, rounds)
                for h in range(2):
                    for k in range(KD):
                        m = pe.matmul(dst[:, 2 * (j + h):2 * (j + h) + 2], slot_tile(s, h, k), cond[:, k, :],
                                      start=(k == 0), stop=(k == KD - 1))
                m.then_inc(sem("slot_used"), 1)

            def norm_sum(n, src):
                tiles, _, tok = NORMS[n]
                if n >= 1:
                    pe.wait_ge(sem("ln_done"), n)
                for k in range(tiles):
                    pe.wait_ge(sem("square_ready"), squares_before(n) + k + 1)
                    m = pe.matmul(bank[7][:, 0:tok], ones[:, :], src(k), start=(k == 0), stop=(k == tiles - 1))
                m.then_inc(sem("norm_sum"), 1)

            pe.wait_ge(sem("small_in"), 16 * len(SMALL))
            pe.matmul(bank[0][0:64, 0:256], w1, zT, start=True, stop=True).then_inc(sem("filt_mm"), 1)
            pe.wait_ge(sem("filt_sin"), 1)
            pe.matmul(bank[1][0:64, 0:256], w2, hid[0], start=True, stop=True).then_inc(sem("filt_mm"), 1)
            pe.wait_ge(sem("filt_sin"), 2)
            for t in range(2):
                for d in range(2):
                    m = pe.matmul(bank[2 + 2 * t + d][:, :], hid[1][:, t * P:(t + 1) * P], w3[:, d * 512:(d + 1) * 512],
                                  start=True, stop=True)
                m.then_inc(sem("filt_mm"), 1)

            pe.wait_ge(sem("cond_ready"), 1)
            for s in range(N_ADA_A):
                ada_slot(s, bank[6], 2 * s)
            norm_sum(PRE0, lambda k: aT[:, k, :])

            pe.wait_ge(sem("filt_pm"), 4)
            for i, (w, src) in enumerate([(dft[:, :, 0:P], 0), (dft[:, :, P:2 * P], 0), (dftB, 1),
                                          (dft[:, :, 3 * P:4 * P], 1), (dftD, 0)]):
                for t in range(2):
                    m = pe.matmul(bank[i][:, :], w[:, t, :], pm[:, src, t, :], start=(t == 0), stop=(t == 1))
                m.then_inc(sem("spec_mm"), 1)
            pe.wait_ge(sem("spec_ready"), 5)

            pe.wait_ge(sem("mod_ready"), 1)
            for s in range(N_EVIN):
                n = S_EVIN + 2 * s
                slot_wait(n)
                for h in range(2):
                    j = 2 * s + h
                    if j >= 4:
                        pe.wait_ge(sem("conv_done"), j - 3)
                    for k in range(KD):
                        if j == 0:
                            pe.wait_ge(sem("a_ready"), k + 1)
                        m = pe.matmul(bank[j % 4][:, :], slot_tile(n, h, k), aT[:, k, :],
                                      start=(k == 0), stop=(k == KD - 1))
                    if h == 0:
                        m.then_inc(sem("proj_mm"), 1)
                m.then_inc(sem("slot_used"), 1)
                ada_slot(n + 1, bank[6], 2 * s)
            for c in range(NCH):
                for k in range(KD):
                    m = pe.matmul(bank[4][:, 16 * c:16 * c + 16], aT[:, k, c * P:(c + 1) * P], w_dt[:, k, :],
                                  start=(k == 0), stop=(k == KD - 1))
            m.then_inc(sem("dt_mm"), 1)

            for c in range(NCH):
                if c == 0:
                    pe.wait_ge(sem("u_ready"), 4)
                    pe.wait_ge(sem("z_ready"), 4)
                for i in range(4):
                    m = pe.transpose(bank[c][:, i * P:(i + 1) * P], u[:, i, c * P:(c + 1) * P], ident[:, :])
                m.then_inc(sem("u_tr"), 1)
            for s in range(2):
                for t in range(2):
                    g = 2 * s + t
                    b = 2 * (g % 2)
                    pe.wait_ge(sem("u_tok"), 4)
                    if g >= 2:
                        pe.wait_ge(sem("prod_mul"), 4 * (g - 1))
                    for ri in range(2):
                        for kt in range(2):
                            m = pe.matmul(bank[b + ri][:, :], dft[:, kt, (2 * ri + t) * P:(2 * ri + t + 1) * P],
                                          u_tok[:, 2 * s + kt, :], start=(kt == 0), stop=(kt == 1))
                    m.then_inc(sem("U_mm"), 1)
            pe.wait_ge(sem("Y_ready"), 8)
            pe.wait_ge(sem("prod_mul"), 16)
            for i in range(4):
                for s in range(2):
                    for f in range(4):
                        m = pe.matmul(bank[i][:, s * 256:(s + 1) * 256], Y[:, f, s, i * P:(i + 1) * P], idft[:, f, :],
                                      start=(f == 0), stop=(f == 3))
                m.then_inc(sem("iy_mm"), 1)

            for c in range(NCH):
                if c >= 1:
                    pe.wait_ge(sem("tok_copied"), 2 * c - 1)
                if c == 0:
                    pe.wait_ge(sem("xbc_ready"), 8)
                    pe.wait_ge(sem("sp_ready"), 1)
                for i in range(4):
                    m = pe.transpose(bank[5][:, i * P:(i + 1) * P], xs[:, i, c * P:(c + 1) * P], ident[:, :])
                m.then_inc(sem("tok_tr"), 1)
                if c >= 1:
                    pe.wait_ge(sem("tok_copied"), 2 * c)
                for i in range(2):
                    m = pe.transpose(bank[4][:, i * P:(i + 1) * P], bT[:, i, c * P:(c + 1) * P], ident[:, :])
                m.then_inc(sem("tok_tr"), 1)
            pe.wait_ge(sem("a_tok"), 1)
            pe.wait_ge(sem("iy_read"), 4)
            for c in range(NCH):
                for d in range(2):
                    pe.matmul(bank[0][:, 32 * c + 8 * d:32 * c + 8 * d + 8], tri[:, d, :], att[:, c, 8 * d:8 * d + 8],
                              start=True, stop=True)
                m = pe.matmul(bank[0][:, 32 * c + 16:32 * c + 32], ones[:, :], att[:, c, :], start=True, stop=True)
            m.then_inc(sem("cs_mm"), 1)
            for c in range(NCH):
                if c >= 2:
                    pe.wait_ge(sem("cb_ready"), 4 * (c - 1))
                for g in range(2):
                    m = pe.matmul(bank[1 + c % 2][:, g * P:(g + 1) * P], bT[:, g, c * P:(c + 1) * P],
                                  cT[:, g, c * P:(c + 1) * P], start=True, stop=True)
                m.then_inc(sem("cb_mm"), 1)
            for n, (c, d) in enumerate(STATE_ORDER):
                pe.wait_ge(sem("xdd_ready"), n + 1)
                if n >= 1:
                    pe.wait_ge(sem("state_ready"), n)
                else:
                    pe.wait_ge(sem("tok_copied"), 8)
                for g in range(2):
                    m = pe.matmul(bank[3][:, g * 256:(g + 1) * 256], b_tok[:, c, g * P:(g + 1) * P],
                                  xdd[:, n % 2, g * 256:(g + 1) * 256], start=True, stop=True)
                m.then_inc(sem("state_mm"), 1)

            def rows(r):
                c, g, d = r // 4, r // 2 % 2, r % 2
                if r >= 2:
                    pe.wait_ge(sem("row_dif"), 4 * (r - 1))
                    pe.wait_ge(sem("row_exp"), r - 1)
                elif r == 0:
                    pe.wait_ge(sem("cs_ready"), 1)
                else:
                    pe.wait_ge(sem("cb_ready"), 16)
                for i in range(4):
                    h = 8 * d + 4 * g + i
                    m = pe.matmul(bank[r % 2][:, i * P:(i + 1) * P],
                                  att[:, c, h:h + 1].to_broadcast([P, P]), tri[:, d, :], start=True, stop=True)
                m.then_inc(sem("row_mm"), 1)

            rows(0)
            rows(1)
            pe.wait_ge(sem("state_ready"), 6)
            for r in range(0, 16, 2):
                c, g = r // 4, r // 2 % 2
                if r + 2 < 16:
                    rows(r + 2)
                    rows(r + 3)
                pe.wait_ge(sem("sc_ready"), r + 2)
                pe.wait_ge(sem("ce_ready"), r + 2)
                yb = bank[4 + c % 2]
                if g == 0 and c >= 2:
                    pe.wait_ge(sem("y_read"), 4 * (c - 1))
                for i in range(4):
                    h = 4 * g + i
                    p0 = 64 * (h % 2)
                    out = yb[p0:p0 + 64, (h // 2) * P:(h // 2 + 1) * P]
                    terms = []
                    for d in range(2):
                        terms.append((xd[:, c, d, h * 64:(h + 1) * 64], sc[:, (r + d) % 3, i * P:(i + 1) * P]))
                        if (c, d) not in ZERO_STATE:
                            terms.append((st[:, c, d, h * 64:(h + 1) * 64], ce[:, (r + d) % 3, i * P:(i + 1) * P]))
                    for n, (w, x) in enumerate(terms):
                        m = pe.matmul(out, w, x, start=(n == 0), stop=(n == len(terms) - 1))
                m.then_inc(sem("y_mm"), 1)
            norm_sum(SSMG0, lambda k: aT[:, k, :])
            norm_sum(SSMG1, lambda k: aT[:, 2 + k, :])

            pe.wait_ge(sem("ymix_ready"), 8)
            for s in range(N_EVOUT):
                n = S_EVOUT + 2 * s
                slot_wait(n)
                for h in range(2):
                    j = 2 * s + h
                    if j >= 4:
                        pe.wait_ge(sem("m_sb"), j - 3)
                    for k in range(KD):
                        m = pe.matmul(bank[j % 4][:, :], slot_tile(n, h, k), yT[:, k, :],
                                      start=(k == 0), stop=(k == KD - 1))
                    if h == 0:
                        m.then_inc(sem("m_mm"), 1)
                m.then_inc(sem("slot_used"), 1)
                ada_slot(n + 1, bank[6], 2 * (N_EVIN + s))
            norm_sum(POST0, lambda k: aT[:, k, :])
            norm_sum(FPRE0, lambda k: aT[:, k, :])

            pe.wait_ge(sem("a_ready"), 16)
            pe.wait_ge(sem("mod_ready"), 2)
            def gate_up(s, half):
                for h in range(2):
                    for k in range(KD):
                        m = pe.matmul(bank[2 * half + h][:, :], slot_tile(s, h, k), aT[:, k, :],
                                      start=(k == 0), stop=(k == KD - 1))
                m.then_inc(sem("slot_used"), 1)

            GR = NFF // 6
            with pe.Fori(0, GR) as i:
                for q in range(6):
                    s = S_GU + 2 * q
                    pe.wait_ge(sem(f"slot{s % SLOTS}_in"), i * 32 + 16 * (s // SLOTS + 1))
                    pe.wait_ge(sem("hff_done"), i * 6 + (q + 1))
                    gate_up(s, q % 2)
                    pe.wait_ge(sem(f"slot{(s + 1) % SLOTS}_in"), i * 32 + 16 * ((s + 1) // SLOTS + 1))
                    for h in range(2):
                        for k in range(KD):
                            m = pe.matmul(bank[6][:, bass.ds(i * 24 + (4 * q + 2 * h), 2)], slot_tile(s + 1, h, k),
                                          cond[:, k, :], start=(k == 0), stop=(k == KD - 1))
                    m.then_inc(sem("slot_used"), 1)
            for j in range(6 * GR, NFF):
                s = S_GU + 2 * j
                slot_wait(s)
                pe.wait_ge(sem("hff_done"), j + 1)
                gate_up(s, j % 2)
                ada_slot(s + 1, bank[6], 2 * j)
            for s in range(N_ADA_C):
                ada_slot(S_ADAC + s, bank[6], 2 * (NFF + s))

            pe.wait_ge(sem("hff_done"), 2 + NFF)
            pe.wait_ge(sem("mod_ready"), 3)
            pe.wait_ge(sem("ln_done"), 5)
            for s in range(N_DOWN):
                slot_wait(S_DOWN + s)
                for h in range(2):
                    f = 2 * s + h
                    for j in range(KD):
                        m = pe.matmul(bank[j][:, :], slot_tile(S_DOWN + s, h, j), hff[:, f, :],
                                      start=(f == 0), stop=(f == NFF - 1))
                        if f == NFF - 1 and j < KD - 1:
                            m.then_inc(sem("m_mm"), 1)
                m.then_inc(sem("slot_used"), 1)
            pe.wait_ge(sem("m_sb"), 16)
            norm_sum(FPOST0, lambda k: aT[:, k, :])

            norm_sum(PRE1, lambda k: aT[:, k, :])
            pe.wait_ge(sem("a_ready"), 24)
            for s in range(N_ODIN):
                slot_wait(S_ODIN + s)
                for h in range(2):
                    j = 2 * s + h
                    if j >= 4:
                        pe.wait_ge(sem("od_copied"), j - 3)
                    cols = slice(0, T) if j in (2, 7) else slice(CTX, T)
                    n = cols.stop - cols.start
                    for k in range(KD):
                        m = pe.matmul(bank[j % 4][:, 0:n], slot_tile(S_ODIN + s, h, k), aT[:, k, cols],
                                      start=(k == 0), stop=(k == KD - 1))
                    if h == 0:
                        m.then_inc(sem("od_mm"), 1)
                m.then_inc(sem("slot_used"), 1)
            pe.wait_ge(sem("od_in"), 16 * len(OD_SMALL))
            for k in range(KD):
                m = pe.matmul(bank[4][64:96, :], w_krv[:, k, 0:32], aT[:, k, :], start=(k == 0), stop=(k == KD - 1))
            m.then_inc(sem("kr_mm"), 1)
            for c in range(NCH):
                for k in range(KD):
                    m = pe.matmul(bank[5][:, c * P:(c + 1) * P], aT[:, k, c * P:(c + 1) * P], w_krv[:, k, 32:160],
                                  start=(k == 0), stop=(k == KD - 1))
            m.then_inc(sem("vg_mm"), 1)
            norm_sum(QLAT, lambda k: yT[:, k, 0:LAT])
            norm_sum(KVLAT, lambda k: yT[:, 2, :])
            pe.wait_ge(sem("od_copied"), 8)
            for j in range(4):
                m = pe.matmul(bank[j // 2][:, (j % 2) * LAT:(j % 2 + 1) * LAT], perm_g, qg[:, j, :], start=True, stop=True)
            m.then_inc(sem("rope_mm"), 1)
            m = pe.matmul(bank[2][:, 0:LAT], perm_g, kg[:, CTX:T], start=True, stop=True)
            m.then_inc(sem("rope_mm"), 1)
            pe.wait_ge(sem("kr_copied"), 1)
            m = pe.matmul(bank[3][64:96, 0:LAT], perm_m[64:96, 64:96], kcat[64:96, 0, CTX:T], start=True, stop=True)
            m.then_inc(sem("rope_mm"), 1)
            pe.wait_ge(sem("lat_ready"), 2)
            pe.wait_ge(sem("rope_done"), 6)
            for h in range(HEADS):
                if h >= 2:
                    pe.wait_ge(sem("qh_copied"), h - 1)
                for k in range(2):
                    m = pe.matmul(bank[h % 2][0:96, 0:LAT], q_up[:, k, h * 96:(h + 1) * 96], qlat[:, k, :],
                                  start=(k == 0), stop=(k == 1))
                m.then_inc(sem("qh_mm"), 1)
            for h in range(HEADS):
                pe.wait_ge(sem("qh_copied"), h + 1 if h >= 6 else 6)
                if h >= 2:
                    pe.wait_ge(sem("qrope_done"), h - 1)
                m = pe.matmul(bank[2 + h % 2][64:96, 0:LAT], perm_m[64:96, 64:96], qh[64:96, h, :], start=True, stop=True)
                m.then_inc(sem("qperm_mm"), 1)
            pe.wait_ge(sem("lat_ready"), 3)
            pe.wait_ge(sem("kr_copied"), 1)
            for h in range(HEADS):
                if h >= 2:
                    pe.wait_ge(sem("kn_copied"), h - 1)
                else:
                    pe.wait_ge(sem("qh_copied"), 8)
                m = pe.matmul(bank[h % 2][0:64, :], kv_up[:, h * 64:(h + 1) * 64], kvlat, start=True, stop=True)
                m.then_inc(sem("kn_mm"), 1)
            for c in range(NCH):
                b = 4 + c % 2
                if c >= 2:
                    pe.wait_ge(sem("v_copied"), c - 1)
                else:
                    pe.wait_ge(sem("vg_copied"), 1)
                m = pe.matmul(bank[b][:, :], kvlat[:, c * P:(c + 1) * P], kv_up[:, 512:1024], start=True, stop=True)
                m.then_inc(sem("v_mm"), 1)
            pe.wait_ge(sem("kn_copied"), 8)
            pe.wait_ge(sem("v_copied"), 4)
            pe.wait_ge(sem("qrope_done"), 8)
            pe.wait_ge(sem("krope_all"), 1)

            def scores(n):
                h, qt = n // 2, n % 2
                if n >= 2:
                    pe.wait_ge(sem("s_read"), n - 1)
                b = bank[n % 2]
                if h < HEADS:
                    m = pe.matmul(b[:, :], qh[0:96, h, qt * P:(qt + 1) * P], kcat[0:96, h, :], start=True, stop=True)
                else:
                    g = h - HEADS
                    p0 = 64 * (g // 4)
                    m = pe.matmul(b[:, :], qg[p0:p0 + 64, g % 4, qt * P:(qt + 1) * P], kg[p0:p0 + 64, :],
                                  start=True, stop=True)
                m.then_inc(sem("s_mm"), 1)

            def values(n):
                h, qt = n // 2, n % 2
                pe.wait_ge(sem("p_ready"), n + 1)
                if n >= 2:
                    pe.wait_ge(sem("pT_ready"), n - 1)
                for c in range(NCH):
                    m = pe.transpose(bank[2 + n % 2][:, c * P:(c + 1) * P], pr[:, n % 4, c * P:(c + 1) * P], ident[:, :])
                m.then_inc(sem("pT_mm"), 1)

            def output(n):
                h, qt = n // 2, n % 2
                pe.wait_ge(sem("pT_ready"), n + 1)
                if qt == 0 and h >= 2:
                    pe.wait_ge(sem("o_copied"), h - 1)
                if h < HEADS:
                    p0 = 64 * (h % 2)
                else:
                    p0 = 64 * ((h - HEADS) // 4)
                for c in range(NCH):
                    w = v_tok[:, c, h * 64:(h + 1) * 64] if h < HEADS else vg_tok[:, c, p0:p0 + 64]
                    m = pe.matmul(bank[4 + h % 2][p0:p0 + 64, qt * P:(qt + 1) * P], w, pT[:, n % 2, c, :],
                                  start=(c == 0), stop=(c == NCH - 1))
                m.then_inc(sem("o_mm"), 1)

            for n in range(34 + 1):
                if n < 32:
                    scores(n)
                if 2 <= n < 34:
                    values(n - 2)
                if n >= 3:
                    output(n - 3)

            pe.wait_ge(sem("o_copied"), 16)
            for s in range(N_ODOUT):
                slot_wait(S_ODOUT + s)
                for h in range(2):
                    j = 2 * s + h
                    if j >= 4:
                        pe.wait_ge(sem("m_sb"), 16 + j - 3)
                    for k in range(KD):
                        m = pe.matmul(bank[j % 4][:, 0:LAT], slot_tile(S_ODOUT + s, h, k), yT[:, k, 0:LAT],
                                      start=(k == 0), stop=(k == KD - 1))
                    if h == 0:
                        m.then_inc(sem("m_mm"), 1)
                m.then_inc(sem("slot_used"), 1)
            norm_sum(POST1, lambda k: aT[:, k, 0:LAT])
            norm_sum(FPRE1, lambda k: aT[:, k, 0:LAT])

            pe.wait_ge(sem("a_ready"), 32)
            pe.wait_ge(sem("router_in"), 64)
            for c in range(2):
                for k in range(KD):
                    m = pe.matmul(bank[0][:, 8 * c:8 * c + 8], aT[:, k, c * P:(c + 1) * P], router[:, k, :],
                                  start=(k == 0), stop=(k == KD - 1))
            m.then_inc(sem("router_mm"), 1)
            pe.wait_ge(sem("sel_ready"), 1)
            for c in range(2):
                if c == 1:
                    pe.matmul(bank[1][:, 8:16], ones[:, :], seltok[:, 0, :], start=True, stop=False)
                pe.matmul(bank[1][:, 8 * c:8 * c + 8], tri[:, 0, :], seltok[:, c, :], start=(c == 0), stop=True)
            for c in range(2):
                m = pe.matmul(bank[1][:, 16:24], ones[:, :], seltok[:, c, :], start=(c == 0), stop=(c == 1))
            m.then_inc(sem("pos_mm"), 1)
            pe.wait_ge(sem("ln_done"), 11)
            for c in range(2):
                for k in range(KD):
                    m = pe.transpose(bank[4 + 2 * c + k // 4][:, (k % 4) * P:(k % 4 + 1) * P], aT[:, k, c * P:(c + 1) * P], ident[:, :])
            m.then_inc(sem("a_tr"), 1)
            pe.wait_ge(sem("key_ready"), 1)
            for x, what in enumerate((gates, key)):
                if x == 1:
                    pe.wait_ge(sem("gbc_ready"), 4)
                for e in range(NEXP):
                    for c in range(2):
                        m = pe.matmul(bank[e // 2][:, (e % 2) * LAT + c * P:(e % 2) * LAT + (c + 1) * P],
                                      what[:, c, e:e + 1].to_broadcast([P, P]), ident[:, :], start=True, stop=True)
                m.then_inc(sem("gbc_mm"), 1)

            def gather(e, nb):
                pe.wait_ge(sem("perm_ready"), e + 1)
                pe.wait_ge(sem("h_split"), e * GROUPS + 1)
                for k in range(KD):
                    for c in range(2):
                        m = pe.matmul(bank[k // 2][:, (k % 2) * LAT:(k % 2) * LAT + nb * P], a_tokm[:, c, k * P:(k + 1) * P],
                                      perm[:, c, 0:nb * P], start=(c == 0), stop=(c == 1))
                    if k % 2:
                        m.then_inc(sem("x_mm"), 1)

            def split_products(out, x, w, first, last):
                for n, (a, b) in enumerate(((0, 0), (0, 1), (1, 0))):
                    m = pe.matmul(out, x[a], w[b], start=(first and n == 0), stop=(last and n == 2))
                return m

            def gate_up(e, i, g, q, nb):
                for s in range(4):
                    for c in range(2):
                        n = 2 * (gate_slot(g) + s) + c
                        pe.wait_ge(sem("w_split"), e * (2 * E_SLOTS) + i * 24 + (n + 1))
                        for b in range(nb):
                            dst = bank[(2 * q if nb == 1 else 2 * b) + s // 2]
                            for k in range(2):
                                kk = 4 * (s % 2) + 2 * c + k
                                cols = slice(b * P, (b + 1) * P)
                                m = split_products(dst[:, :], (x_hi[:, kk, cols], x_lo[:, kk, cols]),
                                                   [w[:, n % 4, k * 512:(k + 1) * 512] for w in (w_hi, w_lo)],
                                                   kk == 0, kk == KD - 1)
                        m.then_inc(sem("w_used"), 1)

            def turn(e, i, g, q, nb):
                pe.wait_ge(sem("h_rows"), e * GROUPS + i * 2 + (g + 1))
                for b in range(nb):
                    for f in range(4):
                        m = pe.transpose(bank[2 * q if nb == 1 else 2 * b][:, f * P:(f + 1) * P],
                                         h2[:, b, f * P:(f + 1) * P], ident[:, :])
                m.then_inc(sem("turned"), 1)

            def down(e, i, g, q, nb):
                pe.wait_ge(sem("h_split"), e * GROUPS + i * 2 + (g + 2))
                for f in range(4):
                    n = 2 * down_slot(g) + f
                    pe.wait_ge(sem("w_split"), e * (2 * E_SLOTS) + i * 24 + (n + 1))
                    for b in range(nb):
                        x = [h[:, q, f, b * P:(b + 1) * P] for h in (h_hi, h_lo)]
                        for half in range(2):
                            m = split_products(bank[4 + 2 * b + half][:, :], x,
                                               [w[:, n % 4, half * 512:(half + 1) * 512] for w in (w_hi, w_lo)],
                                               g == 0 and f == 0, g == GROUPS - 1 and f == 3)
                    m.then_inc(sem("w_used"), 1)

            def scatter(e):
                pe.wait_ge(sem("y_row_ready"), e * 4 + 4)
                pe.wait_ge(sem("spread_ready"), e + 1)
                for j in range(KD):
                    for b in range(2):
                        m = pe.matmul(bank[4 + j // 2][:, (j % 2) * LAT:(j % 2 + 1) * LAT], y_row[:, b, j * P:(j + 1) * P],
                                      spread[:, b, :], start=(b == 0), stop=(b == 1))
                m.then_inc(sem("scatter_mm"), 1)

            pe.wait_ge(sem("gbc_ready"), 8)
            pe.wait_ge(sem("moe_start"), 1)
            with pe.Fori(0, NEXP) as e:
                mine = pe.value_load(two[0:1, bass.ds(e, 1)], min_val=0, max_val=1)
                for nb in (1, 2):
                    with pe.If(mine == nb - 1):
                        gather(e, nb)
                        pe.wait_ge(sem("x_split"), e * 4 + 4)
                        gate_up(e, 0, 0, 0, nb)
                        scatter(e)
                        turn(e, 0, 0, 0, nb)
                        if nb == 2:
                            pe.wait_ge(sem("h_split"), e * GROUPS + 2)
                        gate_up(e, 0, 1, 1, nb)
                        pe.wait_ge(sem("acc_done"), e * 4 + 4)
                        down(e, 0, 0, 0, nb)
                        turn(e, 0, 1, 1, nb)
                        with pe.Fori(0, 2) as i:
                            for g in (2, 3):
                                pe.wait_ge(sem("h_split"), e * GROUPS + i * 2 + (g - 1 + nb))
                                gate_up(e, i, g, g % 2, nb)
                                down(e, i, g - 1, (g - 1) % 2, nb)
                                turn(e, i, g, g % 2, nb)
                        g = GROUPS - 1
                        pe.wait_ge(sem("h_split"), e * GROUPS + (g - 1 + nb))
                        gate_up(e, 0, g, g % 2, nb)
                        down(e, 0, g - 1, (g - 1) % 2, nb)
                        turn(e, 0, g, g % 2, nb)
                        down(e, 0, g, g % 2, nb)
            scatter(NEXP)
            pe.wait_ge(sem("acc_done"), 4 * NEXP + 4)
            norm_sum(FPOST1, lambda k: yT[:, k, 0:LAT])

        @block.scalar
        def _(act):
            for dst, name in SMALL:
                act.dma_start(dst, io[name]).then_inc(sem("small_in"), 16)
            act.wait_ge(sem("small_in"), 16 * len(SMALL))
            act.activation(cond_e[:, :, :], cond[:, :, :], ACT.Silu).then_inc(sem("cond_silu"), 1)
            act.wait_ge(sem("cond_silu"), 1)
            act.activation(cond[:, :, :], cond_e[:, :, :], ACT.Copy).then_inc(sem("cond_ready"), 1)
            for i in range(2):
                act.wait_ge(sem("filt_arg"), i + 1)
                act.activation(hid[i], hk, ACT.Sin).then_inc(sem("filt_sin"), 1)

            def product(j, name, count, slot):
                if j % 2 == 0:
                    act.wait_ge(sem(name), count)
                else:
                    act.wait_ge(sem("slot_used"), slot + 1)

            def squares(n, src, dst):
                for k in range(NORMS[n][0]):
                    act.activation(dst(k), src(k), ACT.Square).then_inc(sem("square_ready"), 1)

            def rstd_of(n):
                _, feat, tok = NORMS[n]
                act.wait_ge(sem("norm_sum"), n + 1)
                if n >= 1:
                    name, value = RSTD_USED[n - 1]
                    act.wait_ge(sem(name), value)
                act.activation(lnv[:, 0:tok], bank[7][:, 0:tok], ACT.Ln, bias=eps[:, 0:1], scale=1.0 / feat).then_inc(sem("ln_done"), 1)
                act.wait_ge(sem("ln_done"), n + 1)
                act.activation(rstd[:, 0:tok], lnv[:, 0:tok], ACT.Exp, scale=-0.5).then_inc(sem("rstd_ready"), 1)

            mods = [0]

            def modulate(layer, sub, tok_all=True):
                first = 8 * [0, 1, 2, 3][mods[0]]
                for k in range(KD):
                    act.wait_ge(sem("scaled"), first + k + 1)
                    for s in ((0, 1) if tok_all else (1,)):
                        cols = SEQ[s] if tok_all else slice(0, LAT)
                        m = act.activation(aT[:, k, cols], aT[:, k, cols], ACT.Identity,
                                           bias=mod[:, layer, (0 if sub == 0 else 24) + k, s:s + 1],
                                           scale=coef[:, layer, 2 * sub, k, s:s + 1])
                    m.then_inc(sem("a_ready"), 1)
                mods[0] += 1

            squares(PRE0, lambda k: hT[:, k, :], lambda k: aT[:, k, :])
            for i in range(5):
                act.wait_ge(sem("spec_mm"), i + 1)
                act.activation(spec[:, i, :], bank[i][:, :], ACT.Copy).then_inc(sem("spec_ready"), 1)
            rstd_of(PRE0)
            act.wait_ge(sem("mod_ready"), 1)
            modulate(0, 0)
            for j in range(20 + 1):
                if j < 20:
                    product(j, "proj_mm", j // 2 + 1, S_EVIN + 2 * (j // 2))
                    if j < 12:
                        w, b = V("hy_w", 12 + j), V("hy_b", j)
                        if 8 <= j:
                            dst = vtmp[:, j - 8, :]
                        else:
                            dst = x0[:, j, :] if j < 4 else u[:, j - 4, :]
                    else:
                        w, b = V("ssm_w", 8 + j - 12), V("ssm_b", j - 12)
                        dst = conv[:, j - 12, :]
                    act.activation(dst, bank[j % 4][:, :], ACT.Identity, bias=b, scale=w).then_inc(sem("conv_mid"), 1)
                if j >= 13:
                    act.wait_ge(sem("conv_done"), j)
                    act.activation(conv[:, j - 13, :], conv[:, j - 13, :], ACT.Silu).then_inc(sem("xbc_ready"), 1)
            for j in range(4):
                product(20 + j, "proj_mm", (20 + j) // 2 + 1, S_EVIN + 2 * ((20 + j) // 2))
                act.activation(z[:, j, :], bank[j][:, :], ACT.Silu).then_inc(sem("z_ready"), 1)
            for c in range(NCH):
                act.wait_ge(sem("u_tr"), c + 1)
                act.activation(u_tok[:, c, :], bank[c][:, :], ACT.Copy).then_inc(sem("u_tok"), 1)
            act.wait_ge(sem("sp_ready"), 1)
            act.activation(sp[:, :, :], sp[:, :, :], ACT.Exp).then_inc(sem("sp_exp"), 1)
            act.wait_ge(sem("sp_exp"), 1)
            act.activation(sp[:, :, :], sp[:, :, :], ACT.Ln, bias=1.0).then_inc(sem("sp_ln"), 1)
            act.activation(nega, V("a_log", 0, 16), ACT.Exp).then_inc(sem("sp_ln"), 1)
            for c in range(NCH):
                act.wait_ge(sem("tok_tr"), 2 * c + 1)
                act.activation(xs_tok[:, c, :], bank[5][:, :], ACT.Copy).then_inc(sem("tok_copied"), 1)
                act.wait_ge(sem("tok_tr"), 2 * c + 2)
                act.activation(b_tok[:, c, :], bank[4][:, 0:256], ACT.Copy).then_inc(sem("tok_copied"), 1)
            act.wait_ge(sem("dec_arg"), 1)
            act.activation(dec[:, :, :], dec[:, :, :], ACT.Exp).then_inc(sem("dec_ready"), 1)
            act.activation(etot[:, :, :], CS[:, :, 16:32], ACT.Exp).then_inc(sem("dec_ready"), 1)
            for r in range(16):
                act.wait_ge(sem("row_mm"), r + 1)
                if r >= 2:
                    act.wait_ge(sem("ce_ready"), r - 1)
                    act.wait_ge(sem("sc_ready"), r - 1)
                act.activation(er[:, r % 2, :], bank[r % 2][:, :], ACT.Exp).then_inc(sem("row_exp"), 1)
                act.wait_ge(sem("row_dif"), 4 * (r + 1))
                act.activation(lm[:, r % 2, :], dif[:, r % 2, :], ACT.Exp).then_inc(sem("l_ready"), 1)
            for g in range(2):
                for k in range(2):
                    if g == 0 and k == 0:
                        act.wait_ge(sem("y_gated"), 4)
                        act.wait_ge(sem("y_mm"), 8)
                    act.activation(aT[:, 2 * g + k, :], yT[:, 4 + 2 * g + k, :], ACT.Square).then_inc(sem("square_ready"), 1)
            rstd_of(SSMG0)
            rstd_of(SSMG1)

            def copy_and_square(n, first, width, banks, wait):
                for j in range(KD):
                    wait(j)
                    if j == 0 and n == POST0:
                        act.wait_ge(sem("norm_sum"), SSMG1 + 1)
                    act.activation(mT[:, j, 0:width], bank[banks(j)][:, 0:width], ACT.Copy).then_inc(sem("m_sb"), 1)
                    act.wait_ge(sem("m_sb"), first + j + 1)
                    act.activation(aT[:, j, 0:width], mT[:, j, 0:width], ACT.Square).then_inc(sem("square_ready"), 1)

            copy_and_square(POST0, 0, T, lambda j: j % 4,
                            lambda j: product(j, "m_mm", j // 2 + 1, S_EVOUT + 2 * (j // 2)))
            rstd_of(POST0)
            for k in range(KD):
                act.wait_ge(sem("h_ready"), k + 1)
                act.activation(aT[:, k, :], hT[:, k, :], ACT.Square).then_inc(sem("square_ready"), 1)
            rstd_of(FPRE0)
            modulate(0, 1)
            with act.Fori(0, NFF // 2) as i:
                for h in range(2):
                    act.wait_ge(sem("slot_used"), i * 4 + (S_GU + 2 * h + 1))
                    act.wait_ge(sem("hff_done"), i * 2 + (h + 1))
                    act.activation(sg[:, h, :], bank[2 * h][:, :], ACT.Silu).then_inc(sem("sg_ready"), 1)
            copy_and_square(FPOST0, 8, T, lambda j: j,
                            lambda j: act.wait_ge(sem("m_mm"), 4 + j + 1) if j < KD - 1 else
                            act.wait_ge(sem("slot_used"), S_ODIN))
            rstd_of(FPOST0)
            for k in range(KD):
                act.wait_ge(sem("h_ready"), 8 + k + 1)
                act.activation(aT[:, k, :], hT[:, k, :], ACT.Square).then_inc(sem("square_ready"), 1)
            for dst, name in OD_SMALL:
                act.dma_start(dst, io[name]).then_inc(sem("od_in"), 16)
            rstd_of(PRE1)
            modulate(1, 0)
            for j in range(8):
                product(j, "od_mm", j // 2 + 1, S_ODIN + j // 2)
                dst, n = [(qlat[:, 0, :], LAT), (qlat[:, 1, :], LAT), (kvlat, T), (qg[:, 0, :], LAT), (qg[:, 1, :], LAT),
                          (qg[:, 2, :], LAT), (qg[:, 3, :], LAT), (kg, T)][j]
                act.activation(dst, bank[j % 4][:, 0:n], ACT.Copy).then_inc(sem("od_copied"), 1)
                if j < 3:
                    act.wait_ge(sem("od_copied"), j + 1)
                    act.activation(yT[:, j, 0:n], dst, ACT.Square).then_inc(sem("square_ready"), 1)
            act.wait_ge(sem("kr_mm"), 1)
            act.activation(kcat[64:96, 0, :], bank[4][64:96, :], ACT.Copy).then_inc(sem("kr_copied"), 1)
            act.wait_ge(sem("vg_mm"), 1)
            act.activation(vg_tok[:, :, :], bank[5][:, :].rearrange("p (c n) -> p c n", c=NCH), ACT.Copy).then_inc(sem("vg_copied"), 1)
            rstd_of(QLAT)
            rstd_of(KVLAT)
            for h in range(HEADS):
                act.wait_ge(sem("qh_mm"), h + 1)
                act.activation(qh[0:96, h, :], bank[h % 2][0:96, 0:LAT], ACT.Copy).then_inc(sem("qh_copied"), 1)
            for h in range(HEADS):
                act.wait_ge(sem("kn_mm"), h + 1)
                act.activation(kcat[0:64, h, :], bank[h % 2][0:64, :], ACT.Copy).then_inc(sem("kn_copied"), 1)
            for c in range(NCH):
                act.wait_ge(sem("v_mm"), c + 1)
                act.activation(v_tok[:, c, :], bank[4 + c % 2][:, :], ACT.Copy).then_inc(sem("v_copied"), 1)

            def attention_exp(n):
                act.wait_ge(sem("max_ready"), n + 1)
                if n >= 4:
                    act.wait_ge(sem("pT_mm"), n - 3)
                act.activation(pr[:, n % 4, :], scw[:, n % 2, 0:T], ACT.Exp, bias=stat[:, n % 8, 1:2],
                               accum_out=stat[:, n % 8, 2:3]).then_inc(sem("exp_ready"), 1)
                if n >= 2 * HEADS:
                    act.activation(sinks[:, n % 8:n % 8 + 1], V("sink", n // 2 - HEADS), ACT.Exp,
                                   bias=stat[:, n % 8, 1:2]).then_inc(sem("sink_exp"), 1)

            def attention_pT(n):
                act.wait_ge(sem("pT_mm"), n + 1)
                if n >= 2:
                    act.wait_ge(sem("o_mm"), n - 1)
                act.activation(pT[:, n % 2, :, :], bank[2 + n % 2][:, :].rearrange("p (c n) -> p c n", c=NCH),
                               ACT.Copy).then_inc(sem("pT_ready"), 1)

            for n in range(34):
                if n < 32:
                    attention_exp(n)
                if n >= 2:
                    attention_pT(n - 2)
            copy_and_square(POST1, 16, LAT, lambda j: j % 4,
                            lambda j: product(j, "m_mm", 11 + j // 2 + 1, S_ODOUT + j // 2))
            rstd_of(POST1)
            for k in range(KD):
                act.wait_ge(sem("h_ready"), 16 + k + 1)
                act.activation(aT[:, k, 0:LAT], hT[:, k, CTX:T], ACT.Square).then_inc(sem("square_ready"), 1)
            for dst, name in ((router, "router"), (lower8, "lower8"), (iota, "iota"), (iota_p, "iota_p")):
                act.dma_start(dst, io[name]).then_inc(sem("router_in"), 16)
            rstd_of(FPRE1)
            modulate(1, 1, False)
            act.wait_ge(sem("gv_ready"), 1)
            act.activation(gv[:, :, 1:2], gv[:, :, 0:1], ACT.Exp).then_inc(sem("gv_exp"), 1)
            act.wait_ge(sem("a_tr"), 1)
            for b in range(4):
                act.activation(a_tokm[:, b // 2, (b % 2) * 512:(b % 2 + 1) * 512], bank[4 + b][:, :], ACT.Copy
                               ).then_inc(sem("atok_ready"), 1)

            def high_part(e, i, n):
                s = N_PRE + n
                act.wait_ge(sem(f"slot{s % SLOTS}_in"), e * (16 * E_SLOTS // SLOTS) + i * 32 + 16 * (s // SLOTS + 1))
                for h in (2 * n, 2 * n + 1):
                    act.wait_ge(sem("w_used"), e * (2 * E_SLOTS) + i * 24 + (h + 1))
                    act.activation(w_hi[:, h % 4, :], ring[:, s % SLOTS, (h % 2) * UNIT:(h % 2 + 1) * UNIT], ACT.Copy
                                   ).then_inc(sem("w_high"), 1)

            def silu_rows(e, i, g, q, nb):
                act.wait_ge(sem("w_used"), e * (2 * E_SLOTS) + i * 24 + (4 + 2 * (gate_slot(g) + 4)))
                for b in range(nb):
                    m = act.activation(sg2[:, b, :], bank[2 * q if nb == 1 else 2 * b][:, :], ACT.Silu)
                m.then_inc(sem("silu_done"), 1)

            def high_rows(e, i, g, q, nb):
                act.wait_ge(sem("turned"), e * GROUPS + i * 2 + (g + 1))
                for b in range(nb):
                    m = act.activation(h_hi[:, q, :, b * P:(b + 1) * P],
                                       bank[2 * q if nb == 1 else 2 * b][:, :].rearrange("p (f r) -> p f r", f=4), ACT.Copy)
                m.then_inc(sem("h_high"), 1)

            def y_row_copies(e):
                for b in range(2):
                    act.activation(y_row[:, 0, b * 512:(b + 1) * 512], bank[4 + b][:, :], ACT.Copy
                                   ).then_inc(sem("y_row_ready"), 1)

            act.wait_ge(sem("moe_start"), 1)
            with act.Fori(0, NEXP) as e:
                mine = act.value_load(two[0:1, bass.ds(e, 1)], min_val=0, max_val=1)
                high_part(e, 0, 0)
                high_part(e, 0, 1)
                act.wait_ge(sem("w_used"), e * (2 * E_SLOTS) + 4)
                y_row_copies(e)
                for nb in (1, 2):
                    with act.If(mine == nb - 1):
                        for b in range(4):
                            act.wait_ge(sem("x_mm"), e * 4 + (b + 1))
                            act.activation(x_hi[:, 2 * b:2 * b + 2, 0:nb * P],
                                           bank[b][:, :].rearrange("p (k r) -> p k r", k=2)[:, :, 0:nb * P], ACT.Copy
                                           ).then_inc(sem("x_high"), 1)
                        for n in range(2, 6):
                            high_part(e, 0, n)
                        silu_rows(e, 0, 0, 0, nb)
                        high_rows(e, 0, 0, 0, nb)
                        for n in range(6, 10):
                            high_part(e, 0, n)
                        silu_rows(e, 0, 1, 1, nb)
                        with act.Fori(0, 2) as i:
                            for g in (2, 3):
                                high_part(e, i, 6 * g - 2)
                                high_rows(e, i, g - 1, (g - 1) % 2, nb)
                                for n in range(6 * g - 1, 6 * g + 4):
                                    high_part(e, i, n)
                                silu_rows(e, i, g, g % 2, nb)
                        g = GROUPS - 1
                        high_part(e, 0, 6 * g - 2)
                        high_rows(e, 0, g - 1, (g - 1) % 2, nb)
                        for n in range(6 * g - 1, 6 * g + 4):
                            high_part(e, 0, n)
                        silu_rows(e, 0, g, g % 2, nb)
                        high_part(e, 0, E_SLOTS - 2)
                        high_rows(e, 0, g, g % 2, nb)
                        high_part(e, 0, E_SLOTS - 1)
            act.wait_ge(sem("w_used"), 2 * NEXP * E_SLOTS + 4)
            y_row_copies(NEXP)
            for j in range(KD):
                act.wait_ge(sem("acc_done"), 4 * NEXP + j // 2 + 1)
                act.activation(yT[:, j, 0:LAT], acc[:, j, :], ACT.Square).then_inc(sem("square_ready"), 1)
            rstd_of(FPOST1)

        @block.vector
        def _(dve):
            chain = [0]

            def link(ins):
                chain[0] += 1
                ins.then_inc(sem("dve_chain"), 1)
                dve.wait_ge(sem("dve_chain"), chain[0])

            dve.memset(ones[:, :], 1.0)
            dve.memset(zeros[:, :], 0.0)
            link(dve.memset(eps[:, :], EPS))
            dve.wait_ge(sem("small_in"), 16 * len(SMALL))
            for i in range(2):
                dve.wait_ge(sem("filt_mm"), i + 1)
                link(dve.tensor_scalar(hk, bank[i][0:64, 0:256], V(f"f_b{i + 1}", p=64), V("f_freq", p=64), ALU.add, ALU.mult))
                link(dve.tensor_scalar(harg, hk, 1.0 / (2 * np.pi), MAGIC, ALU.mult, ALU.add))
                link(dve.tensor_scalar(harg, harg, MAGIC, None, ALU.subtract))
                link(dve.scalar_tensor_tensor(hk, harg, -TWO_PI_HI, hk, ALU.mult, ALU.add))
                link(dve.scalar_tensor_tensor(hk, harg, -TWO_PI_LO, hk, ALU.mult, ALU.add))
                dve.tensor_scalar(hk, hk, PI_DOWN, -PI_DOWN, ALU.min, ALU.max).then_inc(sem("filt_arg"), 1)
                dve.wait_ge(sem("filt_sin"), i + 1)
            for t in range(2):
                dve.wait_ge(sem("filt_mm"), 3 + t)
                dve.tensor_tensor(prod[:, 0, :], bank[2 + 2 * t][:, :], decay[:, t, :], ALU.mult)
                link(dve.scalar_tensor_tensor(prod[:, 1, :], bank[3 + 2 * t][:, :], V("firstrow", t), decay[:, t, :],
                                              ALU.mult, ALU.mult))
                dve.tensor_tensor(pm[:, 0, t, :], prod[:, 0, :], prod[:, 1, :], ALU.add).then_inc(sem("filt_pm"), 1)
                m = dve.tensor_tensor(pm[:, 1, t, :], prod[:, 0, :], prod[:, 1, :], ALU.subtract)
                m.then_inc(sem("filt_pm"), 1)
                dve.wait_ge(sem("filt_pm"), 2 * t + 2)

            def ada_bias(layer, a, b, src):
                n = b - a
                link(dve.tensor_tensor(mod[:, layer, a:b, :], src[:, 2 * (a - src_off[0]):2 * (b - src_off[0])].rearrange("p (n s) -> p n s", s=2),
                                       bc_last(V(f"ada_b{layer}", a, n), 2),
                                       ALU.add))

            def coef_pre(layer, sub):
                s0 = 8 if sub == 0 else 32
                g = V(("mix_pre", "ffn_pre")[sub] + str(layer), 0, 8)
                return dve.scalar_tensor_tensor(coef[:, layer, 2 * sub, :, :], mod[:, layer, s0:s0 + 8, :], 1.0,
                                                bc_last(g, 2), ALU.add, ALU.mult)

            def coef_post(layer, sub):
                s0 = 16 if sub == 0 else 40
                g = V(("mix_post", "ffn_post")[sub] + str(layer), 0, 8)
                return dve.tensor_tensor(coef[:, layer, 2 * sub + 1, :, :], mod[:, layer, s0:s0 + 8, :], bc_last(g, 2), ALU.mult)

            src_off = [0]
            dve.wait_ge(sem("slot_used"), S_EVIN)
            ada_bias(0, 0, 16, bank[6])
            coef_pre(0, 0).then_inc(sem("mod_ready"), 1)

            def scale_rows(n, src, tok=T):
                dve.wait_ge(sem("rstd_ready"), n + 1)
                for k in range(KD):
                    m = dve.tensor_tensor(aT[:, k, 0:tok], src(k), rstd[:, 0:tok], ALU.mult)
                    m.then_inc(sem("scaled"), 1)
                return m

            hn = [0]

            def residual(n, layer, sub, width, last=False):
                dve.wait_ge(sem("rstd_ready"), n + 1)
                for k in range(KD):
                    link(dve.tensor_tensor(mT[:, k, 0:width], mT[:, k, 0:width], rstd[:, 0:width], ALU.mult))
                    for s in ((0, 1) if width == T else (1,)):
                        cols = SEQ[s]
                        mc = SEQ[s] if width == T else slice(0, LAT)
                        m = dve.scalar_tensor_tensor(hT[:, k, cols], mT[:, k, mc], coef[:, layer, 2 * sub + 1, k, s:s + 1],
                                                     hT[:, k, cols], ALU.mult, ALU.add)
                    m.then_inc(sem("h_ready"), 1)
                    hn[0] += 1
                dve.wait_ge(sem("h_ready"), hn[0])

            scale_rows(PRE0, lambda k: hT[:, k, :])

            for j in range(20):
                dve.wait_ge(sem("conv_mid"), j + 1)
                if j < 12:
                    w0, w2_ = V("hy_w", j), V("hy_w", 24 + j)
                    dst = x0[:, j, :] if j < 4 else (u[:, j - 4, :] if j < 8 else vtmp[:, j - 8, :])
                else:
                    w0, w2_ = V("ssm_w", j - 12), V("ssm_w", 16 + j - 12)
                    dst = conv[:, j - 12, :]
                d3 = dst.rearrange("p (s t) -> p s t", s=2)
                b3 = bank[j % 4][:, :].rearrange("p (s t) -> p s t", s=2)
                link(dve.scalar_tensor_tensor(d3[:, :, 1:256], b3[:, :, 0:255], w0, d3[:, :, 1:256], ALU.mult, ALU.add))
                dve.scalar_tensor_tensor(d3[:, :, 0:255], b3[:, :, 1:256], w2_, d3[:, :, 0:255], ALU.mult, ALU.add
                                         ).then_inc(sem("conv_done"), 1)
                if 8 <= j < 12:
                    dve.wait_ge(sem("conv_done"), j + 1)
                    dve.tensor_tensor(u[:, j - 8, :], u[:, j - 8, :], vtmp[:, j - 8, :], ALU.mult).then_inc(sem("u_ready"), 1)
            dve.wait_ge(sem("dt_mm"), 1)
            link(dve.tensor_tensor(dt_x, bank[4][:, 0:64].rearrange("p (c n) -> p c n", c=4),
                                   bc_mid(V("dt_bias", 0, 16), 4), ALU.add))
            link(dve.tensor_scalar(dt_r, dt_x, 0.0, None, ALU.max))
            dve.scalar_tensor_tensor(sp[:, :, :], dt_r, -2.0, dt_x, ALU.mult, ALU.add).then_inc(sem("sp_ready"), 1)

            for s in range(2):
                for t in range(2):
                    g = 2 * s + t
                    b = 2 * (g % 2)
                    dve.wait_ge(sem("U_mm"), g + 1)
                    if g >= 1:
                        dve.wait_ge(sem("Y_ready"), 2 * g)
                    A, B, Dd = spec[:, t, :], spec[:, 2 + t, :], spec[:, 4, :] if t == 0 else spec[:, 1, :]
                    dve.tensor_tensor(prod[:, 0, :], bank[b][:, :], A, ALU.mult).then_inc(sem("prod_mul"), 1)
                    dve.tensor_tensor(prod[:, 1, :], bank[b + 1][:, :], B, ALU.mult).then_inc(sem("prod_mul"), 1)
                    dve.tensor_tensor(prod[:, 2, :], bank[b][:, :], B, ALU.mult).then_inc(sem("prod_mul"), 1)
                    dve.tensor_tensor(prod[:, 3, :], bank[b + 1][:, :], Dd, ALU.mult).then_inc(sem("prod_mul"), 1)
            for i in range(4):
                dve.wait_ge(sem("iy_mm"), i + 1)
                dve.scalar_tensor_tensor(u[:, i, :], u[:, i, :], V("hy_bias", i), bank[i][:, :], ALU.mult, ALU.add
                                         ).then_inc(sem("iy_read"), 1)
                dve.wait_ge(sem("iy_read"), i + 1)
                dve.tensor_tensor(yT[:, i, :], u[:, i, :], x0[:, i, :], ALU.mult).then_inc(sem("ymix_ready"), 1)

            dve.wait_ge(sem("sp_ln"), 2)
            link(dve.tensor_tensor(dtt[:, :, :], sp[:, :, :], dt_r, ALU.add))
            dve.scalar_tensor_tensor(att[:, :, :], dtt[:, :, :], -1.0, bc_mid(nega, 4), ALU.mult, ALU.mult
                                     ).then_inc(sem("a_tok"), 1)
            dve.wait_ge(sem("cs_mm"), 1)
            link(dve.tensor_copy(CS[:, :, :], bank[0][:, 0:128].rearrange("p (c n) -> p c n", c=4)))
            dve.tensor_scalar(ncs[:, :, :], CS[:, :, 0:16], -1.0, None, ALU.mult).then_inc(sem("cs_ready"), 1)
            dve.tensor_tensor(dec[:, :, :], CS[:, :, 16:32], CS[:, :, 0:16], ALU.subtract).then_inc(sem("dec_arg"), 1)
            for c in range(NCH):
                dve.wait_ge(sem("cb_mm"), c + 1)
                for d in range(2):
                    for g in range(2):
                        dve.tensor_tensor(cb[:, c, d, g, :], bank[1 + c % 2][:, g * P:(g + 1) * P], tri[:, d, :], ALU.mult
                                          ).then_inc(sem("cb_ready"), 1)
            def chunk_state(n):
                c, d = STATE_ORDER[n]
                new = st[:, NEXT[c, d], d, :]
                dve.wait_ge(sem("state_mm"), n + 1)
                if (c, d) in ZERO_STATE:
                    m = dve.tensor_copy(new, bank[3][:, :])
                else:
                    link(dve.tensor_tensor(new.rearrange("p (h e) -> p h e", h=8),
                                           st[:, c, d, :].rearrange("p (h e) -> p h e", h=8),
                                           bc_last(etot[:, c, 8 * d:8 * d + 8], 64), ALU.mult))
                    m = dve.tensor_tensor(new, new, bank[3][:, :], ALU.add)
                m.then_inc(sem("state_ready"), 1)
                dve.wait_ge(sem("state_ready"), n + 1)

            dve.wait_ge(sem("tok_copied"), 8)
            dve.wait_ge(sem("dec_ready"), 2)
            for n, (c, d) in enumerate(XD_ORDER):
                x3 = xs_tok[:, c, :].rearrange("p (h e) -> p h e", h=8)
                o3 = xd[:, c, d, :].rearrange("p (h e) -> p h e", h=8)
                m = dve.tensor_tensor(o3, x3, bc_last(dtt[:, c, 8 * d:8 * d + 8], 64), ALU.mult)
                m.then_inc(sem("xd_ready"), 1)
                if n < 6:
                    dve.wait_ge(sem("xd_ready"), n + 1)
                    if n >= 2:
                        dve.wait_ge(sem("state_mm"), n - 1)
                    dve.tensor_tensor(xdd[:, n % 2, :].rearrange("p (h e) -> p h e", h=8), o3,
                                      bc_last(dec[:, c, 8 * d:8 * d + 8], 64), ALU.mult).then_inc(sem("xdd_ready"), 1)
                if 1 <= n < 7:
                    chunk_state(n - 1)
            def ssd_out(c):
                cols = slice(c * P, (c + 1) * P)
                dve.wait_ge(sem("y_mm"), 2 * c + 2)
                for i in range(4):
                    dve.scalar_tensor_tensor(yT[:, 4 + i, cols], xs[:, i, cols], V("ssm_d", i),
                                             bank[4 + c % 2][:, i * P:(i + 1) * P], ALU.mult, ALU.add
                                             ).then_inc(sem("y_read"), 1)

            for r in range(16):
                c, g, d = r // 4, r // 2 % 2, r % 2
                dve.wait_ge(sem("row_mm"), r + 1)
                dve.wait_ge(sem("row_exp"), r + 1)
                if r >= 2:
                    dve.wait_ge(sem("l_ready"), r - 1)
                for i in range(4):
                    h = 8 * d + 4 * g + i
                    dve.tensor_scalar(dif[:, r % 2, i * P:(i + 1) * P], bank[r % 2][:, i * P:(i + 1) * P],
                                      ncs[:, c, h:h + 1], 0.0, ALU.add, ALU.min).then_inc(sem("row_dif"), 1)
                dve.wait_ge(sem("l_ready"), r + 1)
                if r >= 3:
                    dve.wait_ge(sem("y_mm"), (r - 3) // 2 + 1)
                dve.tensor_tensor(sc[:, r % 3, :].rearrange("p (h q) -> p h q", h=4),
                                  lm[:, r % 2, :].rearrange("p (h q) -> p h q", h=4), bc_mid(cb[:, c, d, g, :], 4), ALU.mult
                                  ).then_inc(sem("sc_ready"), 1)
                if r % 4 == 3 and r >= 7:
                    ssd_out(c - 1)
            ssd_out(3)
            for g in range(2):
                dve.wait_ge(sem("rstd_ready"), SSMG0 + g + 1)
                for k in range(2):
                    i = 2 * g + k
                    m = dve.scalar_tensor_tensor(yT[:, 4 + i, :], yT[:, 4 + i, :], V("norm_g", i), rstd[:, :], ALU.mult, ALU.mult)
                    m.then_inc(sem("ymix_ready"), 1)
            src_off[0] = 16
            dve.wait_ge(sem("slot_used"), S_GU)
            ada_bias(0, 16, 48, bank[6])
            link(coef_post(0, 0))
            link(coef_pre(0, 1))
            coef_post(0, 1).then_inc(sem("mod_ready"), 1)
            dve.wait_ge(sem("mod_ready"), 2)
            residual(POST0, 0, 0, T)
            scale_rows(FPRE0, lambda k: hT[:, k, :])
            dve.memset(mark_[:, 3:4], 0.0).then_inc(sem("hff_done"), 2)
            with dve.Fori(0, NFF // 2) as i:
                for h in range(2):
                    dve.wait_ge(sem("sg_ready"), i * 2 + (h + 1))
                    dve.tensor_tensor(hff[:, i * 2 + h, :], sg[:, h, :], bank[2 * h + 1][:, :], ALU.mult
                                      ).then_inc(sem("hff_done"), 1)
            src_off[0] = 0
            dve.wait_ge(sem("slot_used"), S_DOWN)
            ada_bias(1, 0, 48, bank[6])
            for sub in range(2):
                coef_pre(1, sub)
                m = coef_post(1, sub)
            m.then_inc(sem("mod_ready"), 1)
            dve.wait_ge(sem("mod_ready"), 3)
            residual(FPOST0, 0, 1, T)
            scale_rows(PRE1, lambda k: hT[:, k, :])
            dve.wait_ge(sem("od_copied"), 8)
            dve.wait_ge(sem("rope_mm"), 1)
            rn = [0]

            def rope(dst, swapped, cos, sin, work, done="rope_done"):
                m1 = dve.tensor_tensor(work, swapped, sin, ALU.mult)
                link(m1)
                link(dve.tensor_tensor(dst, dst, cos, ALU.mult))
                dve.tensor_tensor(dst, dst, work, ALU.add).then_inc(sem(done), 1)
                rn[0] += 1

            for j in range(4):
                rope(qg[:, j, :], bank[j // 2][:, (j % 2) * LAT:(j % 2 + 1) * LAT], rope_g[:, 0, :], rope_g[:, 1, :], tmp[:, 0, 0:LAT])
                dve.wait_ge(sem("rope_done"), j + 1)
            dve.wait_ge(sem("rope_mm"), 2)
            rope(kg[:, CTX:T], bank[2][:, 0:LAT], rope_g[:, 0, :], rope_g[:, 1, :], tmp[:, 0, 0:LAT])
            dve.wait_ge(sem("rope_done"), 5)
            dve.wait_ge(sem("rope_mm"), 3)
            rope(kcat[64:96, 0, CTX:T], bank[3][64:96, 0:LAT], rope_m[64:96, 0, :], rope_m[64:96, 1, :], tmp[64:96, 0, 0:LAT])
            dve.wait_ge(sem("rope_done"), 6)
            for h in range(1, HEADS):
                m = dve.tensor_copy(kcat[64:96, h, :], kcat[64:96, 0, :])
            m.then_inc(sem("krope_all"), 1)
            dve.wait_ge(sem("rstd_ready"), QLAT + 1)
            for k in range(2):
                m = dve.scalar_tensor_tensor(qlat[:, k, :], qlat[:, k, :], V("q_norm", k), rstd[:, 0:LAT], ALU.mult, ALU.mult)
                m.then_inc(sem("lat_ready"), 1)
            dve.wait_ge(sem("rstd_ready"), KVLAT + 1)
            m = dve.scalar_tensor_tensor(kvlat, kvlat, V("kv_norm"), rstd[:, :], ALU.mult, ALU.mult)
            m.then_inc(sem("lat_ready"), 1)
            for h in range(HEADS):
                dve.wait_ge(sem("qperm_mm"), h + 1)
                dve.wait_ge(sem("qh_copied"), h + 1)
                rope(qh[64:96, h, :], bank[2 + h % 2][64:96, 0:LAT], rope_m[64:96, 0, :], rope_m[64:96, 1, :],
                     tmp[64:96, 0, 0:LAT], "qrope_done")
                dve.wait_ge(sem("qrope_done"), h + 1)

            def attention_max(n):
                h, qt = n // 2, n % 2
                dve.wait_ge(sem("s_mm"), n + 1)
                if n >= 2:
                    dve.wait_ge(sem("exp_ready"), n - 1)
                s = scw[:, n % 2, :]
                if h < HEADS:
                    dve.tensor_scalar(s[:, 0:T], bank[n % 2][:, :], 96.0 ** -0.5, None, ALU.mult).then_inc(sem("s_read"), 1)
                    dve.wait_ge(sem("s_read"), n + 1)
                    w = T
                else:
                    g = h - HEADS
                    dve.tensor_copy(s[:, T:T + 1], V("sink", g))
                    dve.tensor_scalar(s[:, 0:CTX], bank[n % 2][:, 0:CTX], 0.125, None, ALU.mult)
                    dve.scalar_tensor_tensor(s[:, CTX:T], bank[n % 2][:, CTX:T], 0.125, wmask[:, qt, :], ALU.mult, ALU.add
                                             ).then_inc(sem("s_read"), 1)
                    dve.wait_ge(sem("s_read"), n + 1)
                    w = T + 1
                dve.tensor_reduce(stat[:, n % 8, 1:2], s[:, 0:w], AX_X, ALU.max, negate=True).then_inc(sem("max_ready"), 1)

            def attention_norm(n):
                h = n // 2
                dve.wait_ge(sem("exp_ready"), n + 1)
                if h >= HEADS:
                    dve.wait_ge(sem("sink_exp"), n - 2 * HEADS + 1)
                    link(dve.tensor_tensor(stat[:, n % 8, 2:3], stat[:, n % 8, 2:3], sinks[:, n % 8:n % 8 + 1], ALU.add))
                link(dve.reciprocal(stat[:, n % 8, 3:4], stat[:, n % 8, 2:3]))
                dve.tensor_scalar(pr[:, n % 4, :], pr[:, n % 4, :], stat[:, n % 8, 3:4], None, ALU.mult).then_inc(sem("p_ready"), 1)

            def out_copy(h):
                dve.wait_ge(sem("o_mm"), 2 * h + 2)
                if h < HEADS:
                    p0, j = 64 * (h % 2), h // 2
                else:
                    p0, j = 64 * ((h - HEADS) // 4), 4 + (h - HEADS) % 4
                dve.tensor_copy(yT[p0:p0 + 64, j, 0:LAT], bank[4 + h % 2][p0:p0 + 64, 0:LAT]).then_inc(sem("o_copied"), 1)

            for n in range(36):
                if n < 32:
                    attention_max(n)
                if 1 <= n < 33:
                    attention_norm(n - 1)
                if n >= 4 and n % 2 == 0 and (n - 4) // 2 < 16:
                    out_copy((n - 4) // 2)
            residual(POST1, 1, 0, LAT)
            scale_rows(FPRE1, lambda k: hT[:, k, CTX:T], LAT)
            dve.wait_ge(sem("router_in"), 64)
            dve.wait_ge(sem("router_mm"), 1)
            link(dve.tensor_copy(lg[:, :, :], bank[0][:, 0:16].rearrange("p (c n) -> p c n", c=2)))
            for c in range(2):
                r3 = [rt[:, c, x, :].rearrange("p (a b) -> p a b", a=8) for x in range(2)]
                mine = bc_last(lg[:, c, :], 8)
                other = bc_mid(lg[:, c, :], 8)
                dve.tensor_tensor(r3[0], other, mine, ALU.is_gt)
                link(dve.tensor_tensor(r3[1], other, mine, ALU.is_equal))
                link(dve.tensor_tensor(r3[1], r3[1], lower8, ALU.mult))
                link(dve.tensor_tensor(r3[0], r3[0], r3[1], ALU.add))
                link(dve.tensor_reduce(rank[:, c, :], r3[0], AX_X, ALU.add))
                for x in range(2):
                    link(dve.tensor_scalar(sel[:, c, x, :], rank[:, c, :], float(x), None, ALU.is_equal))
                    link(dve.tensor_tensor(mval[:, c, :], sel[:, c, x, :], lg[:, c, :], ALU.mult))
                    link(dve.tensor_reduce(gv[:, c, 2 + x:3 + x], mval[:, c, :], AX_X, ALU.add))
            dve.tensor_tensor(gv[:, :, 0:1], gv[:, :, 3:4], gv[:, :, 2:3], ALU.subtract).then_inc(sem("gv_ready"), 1)
            dve.wait_ge(sem("gv_exp"), 1)
            link(dve.tensor_scalar(gv[:, :, 4:5], gv[:, :, 1:2], 1.0, None, ALU.add))
            link(dve.reciprocal(gv[:, :, 5:6], gv[:, :, 4:5]))
            link(dve.tensor_tensor(gv[:, :, 6:7], gv[:, :, 5:6], gv[:, :, 1:2], ALU.mult))
            for c in range(2):
                link(dve.tensor_scalar(gates[:, c, :], sel[:, c, 1, :], gv[:, c, 6:7], None, ALU.mult))
                m = dve.scalar_tensor_tensor(gates[:, c, :], sel[:, c, 0, :], gv[:, c, 5:6], gates[:, c, :], ALU.mult, ALU.add)
            m.then_inc(sem("gates_ready"), 1)
            link(dve.memset(key[:, :, NEXP:NEXP + 1], -1.0))
            dve.tensor_tensor(seltok[:, :, :], sel[:, :, 0, :], sel[:, :, 1, :], ALU.add).then_inc(sem("sel_ready"), 1)
            dve.wait_ge(sem("pos_mm"), 1)
            link(dve.tensor_tensor(key[:, :, 0:NEXP], bank[1][:, 0:16].rearrange("p (c n) -> p c n", c=2), seltok[:, :, :], ALU.mult))
            link(dve.tensor_scalar(two_f, bank[1][:, 16:24], float(P), None, ALU.is_gt))
            dve.tensor_scalar(key[:, :, 0:NEXP], key[:, :, 0:NEXP], -1.0, None, ALU.add).then_inc(sem("key_ready"), 1)
            link(dve.tensor_copy(two, two_f))
            for x, what in enumerate((gbc, krow)):
                dve.wait_ge(sem("gbc_mm"), x + 1)
                for b in range(4):
                    dve.tensor_copy(what[:, 2 * b:2 * b + 2, :], bank[b][:, :].rearrange("p (e t) -> p e t", e=2)
                                    ).then_inc(sem("gbc_ready"), 1)
            dve.wait_ge(sem("gbc_ready"), 8)

            def make_perm(e):
                for c in range(2):
                    m = dve.tensor_scalar(perm[:, c, :], iota, key[:, c, bass.ds(e, 1)], None, ALU.is_equal)
                m.then_inc(sem("perm_ready"), 1)

            dve.wait_ge(sem("atok_ready"), 4)
            dve.memset(acc, 0.0)
            dve.memset(spread, 0.0).then_inc(sem("spread_ready"), 1)
            dve.memset(mark_[:, 0:1], 0.0).then_inc(sem("h_split"), 1)
            dve.memset(mark_[:, 1:2], 0.0).then_inc(sem("w_used"), 4)
            for c in range(2):
                m = dve.tensor_scalar(perm[:, c, :], iota, key[:, c, 0:1], None, ALU.is_equal)
            m.then_inc(sem("perm_ready"), 1)
            dve.memset(mark_[:, 2:3], 0.0).then_inc(sem("moe_start"), 1)

            def low_part(e, i, n):
                for h in (2 * n, 2 * n + 1):
                    dve.wait_ge(sem("w_high"), e * (2 * E_SLOTS) + i * 24 + (h + 1))
                    dve.tensor_tensor(w_lo[:, h % 4, :], ring[:, (N_PRE + n) % SLOTS, (h % 2) * UNIT:(h % 2 + 1) * UNIT],
                                      w_hi[:, h % 4, :].bitcast(F32), ALU.subtract).then_inc(sem("w_split"), 1)

            def hidden_rows(e, i, g, q, nb):
                dve.wait_ge(sem("silu_done"), e * GROUPS + i * 2 + (g + 1))
                for b in range(nb):
                    m = dve.tensor_tensor(h2[:, b, :], sg2[:, b, :], bank[(2 * q if nb == 1 else 2 * b) + 1][:, :], ALU.mult)
                m.then_inc(sem("h_rows"), 1)

            def low_rows(e, i, g, q, nb):
                dve.wait_ge(sem("h_high"), e * GROUPS + i * 2 + (g + 1))
                for b in range(nb):
                    cols = slice(b * P, (b + 1) * P)
                    m = dve.tensor_tensor(h_lo[:, q, :, cols],
                                          bank[2 * q if nb == 1 else 2 * b][:, :].rearrange("p (f r) -> p f r", f=4),
                                          h_hi[:, q, :, cols].bitcast(F32), ALU.subtract)
                m.then_inc(sem("h_split"), 1)

            def y_row_copies(e):
                for b in range(2):
                    dve.tensor_copy(y_row[:, 1, b * 512:(b + 1) * 512], bank[6 + b][:, :]).then_inc(sem("y_row_ready"), 1)

            def accumulate(e):
                dve.wait_ge(sem("scatter_mm"), e + 1)
                for b in range(4):
                    dve.tensor_tensor(acc[:, 2 * b:2 * b + 2, :], acc[:, 2 * b:2 * b + 2, :],
                                      bank[4 + b][:, :].rearrange("p (k t) -> p k t", k=2), ALU.add).then_inc(sem("acc_done"), 1)

            dve.wait_ge(sem("moe_start"), 1)
            with dve.Fori(0, NEXP) as e:
                mine = dve.value_load(two[0:1, bass.ds(e, 1)], min_val=0, max_val=1)
                low_part(e, 0, 0)
                low_part(e, 0, 1)
                dve.wait_ge(sem("w_used"), e * (2 * E_SLOTS) + 4)
                y_row_copies(e)
                for nb in (1, 2):
                    with dve.If(mine == nb - 1):
                        for b in range(4):
                            dve.wait_ge(sem("x_high"), e * 4 + (b + 1))
                            rows = slice(0, nb * P)
                            dve.tensor_tensor(x_lo[:, 2 * b:2 * b + 2, rows],
                                              bank[b][:, :].rearrange("p (k r) -> p k r", k=2)[:, :, rows],
                                              x_hi[:, 2 * b:2 * b + 2, rows].bitcast(F32), ALU.subtract
                                              ).then_inc(sem("x_split"), 1)
                        for n in range(2, 6):
                            low_part(e, 0, n)
                        hidden_rows(e, 0, 0, 0, nb)
                        accumulate(e)
                        low_rows(e, 0, 0, 0, nb)
                        for n in range(6, 10):
                            low_part(e, 0, n)
                        hidden_rows(e, 0, 1, 1, nb)
                        with dve.Fori(0, 2) as i:
                            for g in (2, 3):
                                low_part(e, i, 6 * g - 2)
                                low_rows(e, i, g - 1, (g - 1) % 2, nb)
                                for n in range(6 * g - 1, 6 * g + 4):
                                    low_part(e, i, n)
                                hidden_rows(e, i, g, g % 2, nb)
                        g = GROUPS - 1
                        low_part(e, 0, 6 * g - 2)
                        low_rows(e, 0, g - 1, (g - 1) % 2, nb)
                        for n in range(6 * g - 1, 6 * g + 4):
                            low_part(e, 0, n)
                        hidden_rows(e, 0, g, g % 2, nb)
                        for b in range(2):
                            m = dve.scalar_tensor_tensor(spread[:, b, :], krow[:, e, :], iota_p[:, b:b + 1], gbc[:, e, :],
                                                         ALU.is_equal, ALU.mult)
                        m.then_inc(sem("spread_ready"), 1)
                        make_perm(e + 1)
                        low_part(e, 0, E_SLOTS - 2)
                        low_rows(e, 0, g, g % 2, nb)
                        low_part(e, 0, E_SLOTS - 1)
            dve.wait_ge(sem("w_used"), 2 * NEXP * E_SLOTS + 4)
            y_row_copies(NEXP)
            accumulate(NEXP)
            dve.wait_ge(sem("acc_done"), 4 * NEXP + 4)
            residual(FPOST1, 1, 1, LAT)

        @block.gpsimd
        def _(pool):
            for s in range(2):
                for t in range(2):
                    g = 2 * s + t
                    pool.wait_ge(sem("prod_mul"), 4 * g + 2)
                    pool.tensor_tensor(Y[:, t, s, :], prod[:, 0, :], prod[:, 1, :], ALU.subtract).then_inc(sem("Y_ready"), 1)
                    pool.wait_ge(sem("prod_mul"), 4 * g + 4)
                    pool.tensor_tensor(Y[:, 2 + t, s, :], prod[:, 2, :], prod[:, 3, :], ALU.add).then_inc(sem("Y_ready"), 1)
            for r in range(16):
                c, g, d = r // 4, r // 2 % 2, r % 2
                pool.wait_ge(sem("row_exp"), r + 1)
                if r >= 3:
                    pool.wait_ge(sem("y_mm"), (r - 3) // 2 + 1)
                pool.tensor_tensor(ce[:, r % 3, :].rearrange("p (h q) -> p h q", h=4),
                                   er[:, r % 2, :].rearrange("p (h q) -> p h q", h=4),
                                   bc_mid(cT[:, g, c * P:(c + 1) * P], 4), ALU.mult).then_inc(sem("ce_ready"), 1)
            for c in range(NCH):
                cols = slice(c * P, (c + 1) * P)
                pool.wait_ge(sem("y_read"), 4 * (c + 1))
                pool.tensor_tensor(yT[:, 4:8, cols], yT[:, 4:8, cols], z[:, :, cols], ALU.mult).then_inc(sem("y_gated"), 1)


def units(w, tiles):
    return w.reshape(KD, P, tiles, P).transpose(2, 1, 0, 3).reshape(tiles, P, UNIT)


def feature_tiles(v):
    return np.ascontiguousarray(v.reshape(-1, P).T)


def shape_constants():
    n, c = LAT, {}
    pos = np.arange(n, dtype=np.float32)
    t = (pos / np.float32(n - 1)).astype(np.float32)
    omega = (np.float32(2.0 * np.pi) * pos / np.float32(n)).astype(np.float32)
    bands = np.linspace(1e-4, 15, 16).astype(np.float32)
    arg = (omega[:, None] * bands).astype(np.float32)
    c["zT"] = np.concatenate([t[:, None], np.cos(arg), -np.sin(arg)], axis=-1).T.astype(np.float32)
    deltas = np.abs(np.linspace(np.log(1e-2) / 1.5, np.log(1e-2) / 0.3, 512).astype(np.float32))
    c["decay"] = np.exp(-t[:, None] * deltas[None, :]).astype(np.float32).reshape(2, P, 512).transpose(1, 0, 2)
    k = np.arange(256)[:, None].astype(np.float64)
    f = np.arange(256)[None, :]
    cos, sin = np.cos(2 * np.pi * k * f / 512), -np.sin(2 * np.pi * k * f / 512)
    nyq = np.cos(np.pi * k[:, 0])
    imag = sin.copy()
    imag[:, 0] = nyq
    two = lambda a: a.reshape(2, P, -1).transpose(1, 0, 2)
    c["dft"] = two(np.concatenate([cos, imag], 1))
    c["dftB"] = two(sin[:, :P])
    d0 = cos[:, :P].copy()
    d0[:, 0] = nyq
    c["dftD"] = two(d0)
    icos, isin = 2 * cos.T / 512, 2 * sin.T / 512
    icos[0] /= 2
    isin[0] = nyq / 512
    c["idft"] = np.concatenate([icos, isin], 0).reshape(4, P, 256).transpose(1, 0, 2)
    c["ident"] = np.eye(P)
    i = np.arange(P)
    c["tri"] = np.stack([i[:, None] <= i[None, :], i[:, None] >= i[None, :]], 1)
    rows = np.repeat(np.arange(n // GRID_W), GRID_W).astype(np.float32)
    cols = np.tile(np.arange(GRID_W), n // GRID_W).astype(np.float32)

    def rope(dim):
        nf = dim // 4
        inv = (10000.0 ** (-np.arange(nf, dtype=np.float32) / nf)).astype(np.float32)
        ang = np.concatenate([rows[:, None] * inv, cols[:, None] * inv], -1).astype(np.float32).T
        ang = np.concatenate([ang, ang], 0)
        return np.stack([np.cos(ang), np.sin(ang)], 1)

    def swap(dim):
        half = dim // 2
        r = np.zeros((dim, dim))
        r[np.arange(half) + half, np.arange(half)] = -1
        r[np.arange(half), np.arange(half) + half] = 1
        return r

    g = rope(64)
    c["rope_g"] = np.concatenate([g, g], 0)
    m = np.zeros((P, 2, n))
    m[64:96] = rope(32)
    c["rope_m"] = m
    pg = np.zeros((P, P))
    pg[:64, :64] = pg[64:, 64:] = swap(64)
    c["perm_g"] = pg
    pm = np.zeros((P, P))
    pm[64:96, 64:96] = swap(32)
    c["perm_m"] = pm
    q = np.arange(n)
    band = np.where(np.abs(q[:, None] - q[None, :]) <= 128, 0.0, -1e30)
    c["wmask"] = band.reshape(2, P, n).transpose(1, 0, 2)
    e = np.arange(8)
    c["lower8"] = np.broadcast_to((e[None, :] < e[:, None])[None], (P, 8, 8))
    c["iota"] = np.broadcast_to(np.arange(n)[None], (P, n))
    c["iota_p"] = np.arange(P)[:, None] + P * np.arange(2)[None]
    return {k: np.ascontiguousarray(v, np.float32) for k, v in c.items()}


def layout(I):
    f = lambda name: np.asarray(I[name])
    a = shape_constants()
    tokens = np.concatenate([f("ctx")[0], f("x")[0]], 0)
    a["xT"] = tokens.T.reshape(KD, P, T).transpose(1, 0, 2)
    a["cond"] = np.stack([f("c_ctx"), f("c")[0]], 1).reshape(KD, P, 2).transpose(1, 0, 2)
    v = np.zeros((P, NVEC), np.float32)

    def put(name, x):
        at, w = VEC[name]
        v[:x.shape[0], at:at + w] = x

    for l in range(2):
        put(f"ada_b{l}", feature_tiles(f("ada_b")[l]))
        for n in ("mix_pre", "mix_post", "ffn_pre", "ffn_post"):
            put(f"{n}{l}", feature_tiles(f(f"{n}_g")[l]))
    put("hy_w", feature_tiles(f("ev_hy_conv_w")[0]))
    put("hy_b", feature_tiles(f("ev_hy_conv_b")[0]))
    put("hy_bias", feature_tiles(f("ev_hy_bias")[0]))
    put("ssm_w", feature_tiles(f("ev_ssm_conv_w")[0]))
    put("ssm_b", feature_tiles(f("ev_ssm_conv_b")[0]))
    put("ssm_d", feature_tiles(np.repeat(f("ev_ssm_d")[0], 64)))
    put("norm_g", feature_tiles(f("ev_ssm_norm_g")[0]))
    put("q_norm", feature_tiles(f("od_mla_q_norm_g")[0]))
    put("kv_norm", feature_tiles(f("od_mla_kv_norm_g")[0]))
    put("dt_bias", np.broadcast_to(f("ev_ssm_dt_bias").reshape(1, 16), (P, 16)))
    put("a_log", np.broadcast_to(f("ev_ssm_a_log").reshape(1, 16), (P, 16)))
    put("sink", np.broadcast_to(f("od_gqa_sink").reshape(1, 8), (P, 8)))
    put("f_b1", f("ev_hy_filt_b1")[0][:, None])
    put("f_b2", f("ev_hy_filt_b2")[0][:, None])
    put("f_freq", f("ev_hy_freq")[0][:, None])
    fr = np.ones((P, 2), np.float32)
    fr[0, 0] = 0
    put("firstrow", fr)
    a["vec"] = v
    a["w1"], a["w2"], a["w3"] = f("ev_hy_filt_w1")[0], f("ev_hy_filt_w2")[0], f("ev_hy_filt_w3")[0]
    ev = f("ev_w_in")[0]
    kt = lambda w: w.reshape(-1, P, w.shape[-1]).transpose(1, 0, 2)
    a["w_dt"] = kt(ev[:, 3072:3088])
    evin = units(np.concatenate([ev[:, 0:1536], ev[:, 2048:3072], ev[:, 1536:2048]], 1), 24)
    ada = [units(f("ada_w")[l], 48) for l in range(2)]
    evout = units(f("ev_w_out")[0], 8)
    gate, up = units(f("ev_ffn_w_gate")[0], NFF), units(f("ev_ffn_w_up")[0], NFF)
    down = f("ev_ffn_w_down")[0].reshape(NFF, P, UNIT)
    od = f("od_w_in")[0]
    q_lat, kv_lat, k_rope, q_g, k_g, v_g = np.split(od, [256, 384, 416, 928, 1056], 1)
    heads = [x for p in range(4) for x in (p, p + 4)]
    q_g = q_g.reshape(D, 8, 64)[:, heads].reshape(D, 512)
    odin = units(np.concatenate([q_lat, kv_lat, q_g, k_g], 1), 8)
    wo = f("od_w_out")[0].copy()
    wo[512:] = wo[512:].reshape(8, 64, D)[heads].reshape(512, D)
    odout = units(wo, 8)
    slots = []
    pair = lambda x, s: [x[2 * s], x[2 * s + 1]]
    for s in range(N_ADA_A):
        slots.append(pair(ada[0], s))
    for s in range(N_EVIN):
        slots += [pair(evin, s), pair(ada[0], N_ADA_A + s)]
    for s in range(N_EVOUT):
        slots += [pair(evout, s), pair(ada[0], N_ADA_A + N_EVIN + s)]
    for j in range(NFF):
        slots += [[gate[j], up[j]], pair(ada[1], j)]
    for s in range(N_ADA_C):
        slots.append(pair(ada[1], NFF + s))
    slots += [pair(down, s) for s in range(N_DOWN)]
    slots += [pair(odin, s) for s in range(N_ODIN)]
    slots += [pair(odout, s) for s in range(N_ODOUT)]
    assert len(slots) == N_PRE
    pre = np.empty((N_PRE, P, 2, UNIT), np.float32)
    for i, (x, y) in enumerate(slots):
        pre[i, :, 0], pre[i, :, 1] = x, y
    a["pre"] = pre.reshape(N_PRE, P, 2 * UNIT)
    a["w_krv"] = kt(np.concatenate([k_rope, v_g], 1))
    a["q_up"] = kt(f("od_mla_w_q_up")[0])
    kvu = f("od_mla_w_kv_up")[0].reshape(P, HEADS, 2, 64)
    a["kv_up"] = kvu.transpose(0, 2, 1, 3).reshape(P, 1024)
    a["router"] = kt(f("od_router")[0])
    moe = np.empty((NEXP, E_SLOTS, P, 4, 512), np.float32)
    for e in range(NEXP):
        for x, name in enumerate(("od_moe_w_gate", "od_moe_w_up")):
            w = f(name)[0, e].reshape(2, 4, P, GROUPS, 512).transpose(3, 0, 2, 1, 4)
            for g in range(GROUPS):
                moe[e, gate_slot(g) + 2 * x:gate_slot(g) + 2 * x + 2] = w[g]
        d = f("od_moe_w_down")[0, e].reshape(GROUPS, 2, 2, P, 2, 512)
        for g in range(GROUPS):
            moe[e, down_slot(g):down_slot(g) + 2] = d[g].transpose(0, 2, 1, 3, 4).reshape(2, P, 4, 512)
    a["moe"] = moe.reshape(N_MOE, P, 2 * UNIT)
    return {k: np.ascontiguousarray(x) for k, x in a.items()}


def kernel(**inputs):
    import concourse.bacc as bacc
    from concourse.bass_utils import run_bass_kernel_spmd

    arrays = layout(inputs)
    nc = bacc.Bacc("TRN2", target_bir_lowering=False, num_devices=1)
    io = {k: nc.dram_tensor(f"in_{k}", v.shape, F32, kind="ExternalInput").ap() for k, v in arrays.items()}
    io["out"] = nc.dram_tensor("out_T", (P, KD, LAT), F32, kind="ExternalOutput").ap()
    build(nc, io)
    r = run_bass_kernel_spmd(nc, [{f"in_{k}": v for k, v in arrays.items()}], core_ids=[0])
    out = np.asarray(r.results[0]["out_T"])
    return out.transpose(2, 1, 0).reshape(1, LAT, D)
```
